# Optimizing a Trainium2 kernel written in Bass

```python
import jax, jax.numpy as jnp
from jax import lax
import numpy as np

D_MODEL = 1024
BATCH = 1
SEQ = 256
DEPTH = 2

D_MIX = D_MODEL
W_GROUP = D_MIX // 4
HEAD_DIM = 64
ROT_DIM = HEAD_DIM // 4
ROPE_THETA = 500000.0
Q_BLOCK = 128
EPS = 1e-6
DSA_HEADS = W_GROUP // HEAD_DIM
IDX_HEADS = 8
IDX_DIM = 32
IDX_ROT = IDX_DIM // 4
DSA_TOPK = 256
NSA_HEADS = W_GROUP // HEAD_DIM
CMP_LEN = 32
CMP_STRIDE = 16
SLC_BLOCK = 64
SLC_TOPN = 16
WINDOW = 512
CONV_WIDTH = 3
POOL_GROUPS = 4
POOL_WINDOWS = (2, 4, 8, 16)
POOL_CH = W_GROUP // POOL_GROUPS

IN_SPLITS = (
    ("a_q", DSA_HEADS * HEAD_DIM), ("a_k", HEAD_DIM), ("a_v", HEAD_DIM),
    ("a_qi", IDX_HEADS * IDX_DIM), ("a_ki", IDX_DIM), ("a_wi", IDX_HEADS), ("a_gate", W_GROUP),
    ("b_q", NSA_HEADS * HEAD_DIM), ("b_kc", HEAD_DIM), ("b_vc", HEAD_DIM), ("b_ks", HEAD_DIM),
    ("b_vs", HEAD_DIM), ("b_kw", HEAD_DIM), ("b_vw", HEAD_DIM), ("b_g", 3 * NSA_HEADS), ("b_gate", W_GROUP),
    ("c_b", W_GROUP), ("c_c", W_GROUP), ("c_x", W_GROUP), ("c_gate", W_GROUP),
    ("d_u", W_GROUP), ("d_gate", W_GROUP),
)
D_IN = sum(w for _, w in IN_SPLITS)


def split_cols(z):
    offs = np.cumsum([w for _, w in IN_SPLITS])[:-1].tolist()
    return dict(zip([n for n, _ in IN_SPLITS], jnp.split(z, offs, axis=-1)))

def rmsnorm(x, g):
    xf = x.astype(jnp.float32)
    y = xf * lax.rsqrt(jnp.mean(xf * xf, axis=-1, keepdims=True) + EPS)
    return (y * g.astype(jnp.float32)).astype(x.dtype)

def rope(x, pos, rot):
    half = rot // 2
    inv = ROPE_THETA ** (-jnp.arange(half, dtype=jnp.float32) / half)
    ang = pos.astype(jnp.float32)[:, None] * inv[None, :]
    cos = jnp.cos(ang)[:, None, :].astype(x.dtype)
    sin = jnp.sin(ang)[:, None, :].astype(x.dtype)
    x1, x2, rest = x[..., :half], x[..., half:rot], x[..., rot:]
    return jnp.concatenate([x1 * cos - x2 * sin, x2 * cos + x1 * sin, rest], axis=-1)

def masked_softmax(s, valid):
    s = jnp.where(valid, s.astype(jnp.float32), -jnp.inf)
    m = jnp.max(s, axis=-1, keepdims=True)
    m = jnp.where(jnp.isfinite(m), m, 0.0)
    e = jnp.where(valid, jnp.exp(s - m), 0.0)
    return e / jnp.maximum(jnp.sum(e, axis=-1, keepdims=True), 1e-30)

take_rows = jax.vmap(lambda a, i: a[i])

def dsa_mixer(q, k, v, qi, ki, wi):
    B, T = q.shape[:2]
    topk = min(DSA_TOPK, T // 4)
    key_pos = jnp.arange(T)

    def block(i):
        q0 = i * Q_BLOCK
        t = q0 + jnp.arange(Q_BLOCK)
        qb = lax.dynamic_slice_in_dim(q, q0, Q_BLOCK, axis=1)
        qib = lax.dynamic_slice_in_dim(qi, q0, Q_BLOCK, axis=1)
        wib = lax.dynamic_slice_in_dim(wi, q0, Q_BLOCK, axis=1) * (IDX_HEADS ** -0.5)
        logits = jnp.einsum('bqhd,bsd->bqhs', qib, ki) * (IDX_DIM ** -0.5)
        score = jnp.einsum('bqhs,bqh->bqs', jax.nn.relu(logits), wib).astype(jnp.float32)
        causal = key_pos[None, :] <= t[:, None]
        score = jnp.where(causal[None], score, -jnp.inf)
        _, idx = lax.top_k(score, topk)
        k_sel = take_rows(k, idx)
        v_sel = take_rows(v, idx)
        s = jnp.einsum('bqhd,bqkd->bhqk', qb, k_sel) * (HEAD_DIM ** -0.5)
        valid = (idx <= t[None, :, None])[:, None]
        p = masked_softmax(s, valid).astype(v.dtype)
        return jnp.einsum('bhqk,bqkd->bqhd', p, v_sel)

    out = lax.map(block, jnp.arange(T // Q_BLOCK))
    return jnp.moveaxis(out, 0, 1).reshape(B, T, -1)

def nsa_mixer(q, kc_tok, vc_tok, ks, vs, kw, vw, gates, pe_cmp, w_cmp_k, w_cmp_v):
    B, T = q.shape[:2]
    dtype = q.dtype
    n_cmp = (T - CMP_LEN) // CMP_STRIDE + 1
    n_slc = T // SLC_BLOCK
    topn = min(SLC_TOPN, n_slc)
    scale = HEAD_DIM ** -0.5
    cmp_start = jnp.arange(n_cmp) * CMP_STRIDE
    cmp_end = cmp_start + CMP_LEN - 1
    cmp_idx = cmp_start[:, None] + jnp.arange(CMP_LEN)[None, :]

    def compress(tok, w):
        blocks = tok[:, cmp_idx] + pe_cmp
        return blocks.reshape(B, n_cmp, CMP_LEN * HEAD_DIM) @ w

    k_cmp = rope(compress(kc_tok, w_cmp_k)[:, :, None], cmp_end, ROT_DIM)[:, :, 0]
    v_cmp = compress(vc_tok, w_cmp_v)
    slc_start = jnp.arange(n_slc) * SLC_BLOCK
    overlap = ((cmp_start[:, None] < slc_start[None, :] + SLC_BLOCK)
               & (cmp_end[:, None] >= slc_start[None, :])).astype(jnp.float32)
    ks_blocks = ks.reshape(B, n_slc, SLC_BLOCK, HEAD_DIM)
    vs_blocks = vs.reshape(B, n_slc, SLC_BLOCK, HEAD_DIM)
    kw_pad = jnp.pad(kw, ((0, 0), (WINDOW, 0), (0, 0)))
    vw_pad = jnp.pad(vw, ((0, 0), (WINDOW, 0), (0, 0)))
    blk_ids = jnp.arange(n_slc)
    in_blk = jnp.arange(SLC_BLOCK)

    def block(i):
        q0 = i * Q_BLOCK
        t = q0 + jnp.arange(Q_BLOCK)
        qb = lax.dynamic_slice_in_dim(q, q0, Q_BLOCK, axis=1)
        gb = lax.dynamic_slice_in_dim(gates, q0, Q_BLOCK, axis=1)
        s_c = jnp.einsum('bqhd,bnd->bhqn', qb, k_cmp) * scale
        valid_c = (cmp_end[None, :] <= t[:, None])[None, None]
        p_c = masked_softmax(s_c, valid_c)
        o_c = jnp.einsum('bhqn,bnd->bqhd', p_c.astype(dtype), v_cmp)
        imp = jnp.einsum('bhqn,nj->bqj', p_c, overlap)
        blk_t = t // SLC_BLOCK
        forced = (blk_ids[None, :] == 0) | (blk_ids[None, :] == blk_t[:, None])
        admissible = blk_ids[None, :] <= blk_t[:, None]
        imp = jnp.where(forced, jnp.inf, jnp.where(admissible, imp, -jnp.inf))
        _, idx = lax.top_k(imp, topn)
        k_sel = take_rows(ks_blocks, idx).reshape(B, Q_BLOCK, topn * SLC_BLOCK, HEAD_DIM)
        v_sel = take_rows(vs_blocks, idx).reshape(B, Q_BLOCK, topn * SLC_BLOCK, HEAD_DIM)
        pos_sel = (idx[..., None] * SLC_BLOCK + in_blk).reshape(B, Q_BLOCK, topn * SLC_BLOCK)
        s_s = jnp.einsum('bqhd,bqkd->bhqk', qb, k_sel) * scale
        p_s = masked_softmax(s_s, (pos_sel <= t[None, :, None])[:, None]).astype(dtype)
        o_s = jnp.einsum('bhqk,bqkd->bqhd', p_s, v_sel)
        kwb = lax.dynamic_slice_in_dim(kw_pad, q0, Q_BLOCK + WINDOW, axis=1)
        vwb = lax.dynamic_slice_in_dim(vw_pad, q0, Q_BLOCK + WINDOW, axis=1)
        pos_w = q0 - WINDOW + jnp.arange(Q_BLOCK + WINDOW)
        valid_w = ((pos_w[None, :] >= 0) & (pos_w[None, :] <= t[:, None])
                   & (t[:, None] - pos_w[None, :] < WINDOW))
        s_w = jnp.einsum('bqhd,bkd->bhqk', qb, kwb) * scale
        p_w = masked_softmax(s_w, valid_w[None, None]).astype(dtype)
        o_w = jnp.einsum('bhqk,bkd->bqhd', p_w, vwb)
        g = jax.nn.sigmoid(gb.astype(jnp.float32)).astype(dtype)
        return g[..., 0:1] * o_c + g[..., 1:2] * o_s + g[..., 2:3] * o_w

    out = lax.map(block, jnp.arange(T // Q_BLOCK))
    return jnp.moveaxis(out, 0, 1).reshape(B, T, -1)

def shortconv_mixer(b_gate, c_gate, xc, conv_w):
    T = xc.shape[1]
    u = c_gate * xc
    up = jnp.pad(u, ((0, 0), (CONV_WIDTH - 1, 0), (0, 0)))
    y = up[:, 0:T] * conv_w[0]
    for j in range(1, CONV_WIDTH):
        y = y + up[:, j:j + T] * conv_w[j]
    return b_gate * y

def pool_mixer(u, pool_w, pool_scale):
    B, T, _ = u.shape
    ug = u.reshape(B, T, POOL_GROUPS, POOL_CH)
    cs = jnp.cumsum(ug.astype(jnp.float32), axis=1)
    cs = jnp.pad(cs, ((0, 0), (1, 0), (0, 0), (0, 0)))
    win = jnp.array(POOL_WINDOWS, dtype=jnp.int32)
    t = jnp.arange(T)
    start = jnp.maximum(t[:, None] + 1 - win[None, :], 0)
    lower = cs[:, start, jnp.arange(POOL_GROUPS)[None, :]]
    count = jnp.minimum(t[:, None] + 1, win[None, :]).astype(jnp.float32)
    mean = (cs[:, 1:] - lower) / count[None, :, :, None]
    pooled = (mean - ug.astype(jnp.float32)).astype(u.dtype)
    y = jnp.einsum('btgc,gcd->btgd', pooled, pool_w).reshape(B, T, W_GROUP)
    return y * pool_scale

def hybrid_layer(x, norm_w, w_in, w_out, conv_w, pe_cmp, w_cmp_k, w_cmp_v, pool_w, pool_scale):
    B, T, _ = x.shape
    pos = jnp.arange(T)
    h = rmsnorm(x, norm_w)
    p = split_cols(h @ w_in)
    heads = lambda a, n: a.reshape(B, T, n, -1)
    one_head_rope = lambda a, rot: rope(a[:, :, None], pos, rot)[:, :, 0]
    o_a = dsa_mixer(rope(heads(p['a_q'], DSA_HEADS), pos, ROT_DIM), one_head_rope(p['a_k'], ROT_DIM),
                    p['a_v'], rope(heads(p['a_qi'], IDX_HEADS), pos, IDX_ROT),
                    one_head_rope(p['a_ki'], IDX_ROT), p['a_wi'])
    o_b = nsa_mixer(rope(heads(p['b_q'], NSA_HEADS), pos, ROT_DIM), p['b_kc'], p['b_vc'],
                    one_head_rope(p['b_ks'], ROT_DIM), p['b_vs'],
                    one_head_rope(p['b_kw'], ROT_DIM), p['b_vw'],
                    heads(p['b_g'], NSA_HEADS), pe_cmp, w_cmp_k, w_cmp_v)
    o_c = shortconv_mixer(p['c_b'], p['c_c'], p['c_x'], conv_w)
    o_d = pool_mixer(p['d_u'], pool_w, pool_scale)
    mixed = jnp.concatenate([jax.nn.silu(p['a_gate']) * o_a, jax.nn.silu(p['b_gate']) * o_b,
                             jax.nn.silu(p['c_gate']) * o_c, jax.nn.silu(p['d_gate']) * o_d], axis=-1)
    return x + mixed @ w_out

def first_inputs(seed: int = 0) -> dict:
    key = jax.random.key(seed)
    ks = jax.random.split(key, 11)
    f32 = jnp.float32
    x = jax.random.normal(ks[0], (BATCH, SEQ, D_MODEL), f32)
    norm_w = 1.0 + 0.1 * jax.random.normal(ks[1], (DEPTH, D_MODEL), f32)
    w_in = jax.random.normal(ks[2], (DEPTH, D_MODEL, D_IN), f32) * D_MODEL ** -0.5
    w_out = jax.random.normal(ks[3], (DEPTH, D_MIX, D_MODEL), f32) * D_MIX ** -0.5
    conv_w = jax.random.normal(ks[4], (DEPTH, CONV_WIDTH, W_GROUP), f32) * CONV_WIDTH ** -0.5
    pe_cmp = 0.02 * jax.random.normal(ks[5], (DEPTH, CMP_LEN, HEAD_DIM), f32)
    w_cmp_k = jax.random.normal(ks[6], (DEPTH, CMP_LEN * HEAD_DIM, HEAD_DIM), f32) * (CMP_LEN * HEAD_DIM) ** -0.5
    w_cmp_v = jax.random.normal(ks[7], (DEPTH, CMP_LEN * HEAD_DIM, HEAD_DIM), f32) * (CMP_LEN * HEAD_DIM) ** -0.5
    pool_w = jax.random.normal(ks[8], (DEPTH, POOL_GROUPS, POOL_CH, POOL_CH), f32) * POOL_CH ** -0.5
    pool_scale = 1.0 + 0.1 * jax.random.normal(ks[9], (DEPTH, W_GROUP), f32)
    final_norm_w = 1.0 + 0.1 * jax.random.normal(ks[10], (D_MODEL,), f32)
    return {"x": x, "norm_w": norm_w, "w_in": w_in, "w_out": w_out, "conv_w": conv_w,
            "pe_cmp": pe_cmp, "w_cmp_k": w_cmp_k, "w_cmp_v": w_cmp_v, "pool_w": pool_w,
            "pool_scale": pool_scale, "final_norm_w": final_norm_w}

def first_block(x, norm_w, w_in, w_out, conv_w, pe_cmp, w_cmp_k, w_cmp_v, pool_w, pool_scale, final_norm_w):
    for l in range(DEPTH):
        x = hybrid_layer(x, norm_w[l], w_in[l], w_out[l], conv_w[l], pe_cmp[l],
                         w_cmp_k[l], w_cmp_v[l], pool_w[l], pool_scale[l])
    return rmsnorm(x, final_norm_w)


DEPTH_2 = 1

CHUNK = 64
D_MIX_2 = D_MODEL
SSD_HEADS = 8
SSD_HEAD_DIM = 64
SSD_INNER = SSD_HEADS * SSD_HEAD_DIM
SSD_GROUPS = 2
SSD_STATE = 128
CONV_WIDTH_2 = 4
SSD_CONV_DIM = SSD_INNER + 2 * SSD_GROUPS * SSD_STATE
ATT_HEADS = 8
ATT_HEAD_DIM = 64
ATT_INNER = ATT_HEADS * ATT_HEAD_DIM
N_EXPERT_GROUPS = 4
EXPERTS_PER_GROUP = 4
N_EXPERTS = N_EXPERT_GROUPS * EXPERTS_PER_GROUP
TOP_K = 2
D_FF_EXPERT = 512
DEEPNORM_ALPHA = (2.0 * DEPTH_2) ** 0.25
DEEPNORM_BETA = (8.0 * DEPTH_2) ** -0.25
LN_EPS = 1e-5
RMS_EPS = 1e-5
IN_SIZES = (SSD_INNER, SSD_CONV_DIM, SSD_HEADS, ATT_INNER, ATT_INNER, ATT_INNER, ATT_HEADS)
D_IN_PROJ = SSD_INNER + SSD_CONV_DIM + SSD_HEADS + 3 * ATT_INNER + ATT_HEADS


def _split_cols(u, sizes):
    idx = np.cumsum(np.array(sizes))[:-1].tolist()
    return jnp.split(u, idx, axis=-1)

def _layer_norm(u, g, b):
    uf = u.astype(jnp.float32)
    mu = jnp.mean(uf, axis=-1, keepdims=True)
    var = jnp.mean(jnp.square(uf - mu), axis=-1, keepdims=True)
    return ((uf - mu) * lax.rsqrt(var + LN_EPS) * g + b).astype(u.dtype)

def _causal_dwconv(u, w, b):
    s = u.shape[1]
    up = jnp.pad(u, ((0, 0), (CONV_WIDTH_2 - 1, 0), (0, 0)))
    out = b
    for k in range(CONV_WIDTH_2):
        out = out + up[:, k:k + s, :] * w[k]
    return out

def _ssd_scan(xs, dt, a, bm, cm, d_skip):
    f32 = jnp.float32
    xs, dt, bm, cm = xs.astype(f32), dt.astype(f32), bm.astype(f32), cm.astype(f32)
    b, s, h, p = xs.shape
    nc = s // CHUNK
    r = h // SSD_GROUPS
    xdt = (xs * dt[..., None]).reshape(b, nc, CHUNK, SSD_GROUPS, r, p)
    da = (dt * a.astype(f32)).reshape(b, nc, CHUNK, SSD_GROUPS, r)
    bc = bm.reshape(b, nc, CHUNK, SSD_GROUPS, SSD_STATE)
    cc = cm.reshape(b, nc, CHUNK, SSD_GROUPS, SSD_STATE)
    a_cum = jnp.cumsum(da, axis=2)
    seg = a_cum[:, :, :, None] - a_cum[:, :, None, :]
    tri = jnp.tril(jnp.ones((CHUNK, CHUNK), dtype=bool))[None, None, :, :, None, None]
    lmat = jnp.exp(jnp.where(tri, seg, -jnp.inf))
    cb = jnp.einsum('bclgn,bcsgn->bclsg', cc, bc)
    y_diag = jnp.einsum('bclsg,bclsgr,bcsgrp->bclgrp', cb, lmat, xdt)
    decay_to_end = jnp.exp(a_cum[:, :, -1:] - a_cum)
    chunk_states = jnp.einsum('bclgn,bclgr,bclgrp->bcgrpn', bc, decay_to_end, xdt)
    chunk_decay = jnp.exp(a_cum[:, :, -1])

    def step(state, inp):
        st, dec = inp
        return state * dec[..., None, None] + st, state

    init = jnp.zeros((b, SSD_GROUPS, r, p, SSD_STATE), f32)
    _, states_in = lax.scan(step, init, (jnp.moveaxis(chunk_states, 1, 0),
                                         jnp.moveaxis(chunk_decay, 1, 0)))
    states_in = jnp.moveaxis(states_in, 0, 1)
    y_off = jnp.einsum('bclgn,bcgrpn,bclgr->bclgrp', cc, states_in, jnp.exp(a_cum))
    y = (y_diag + y_off).reshape(b, s, h, p)
    return y + xs * d_skip.astype(f32)[:, None]

def _forgetting_attention(q, k, v, log_f):
    b, s, h, d = q.shape
    fcum = jnp.transpose(jnp.cumsum(log_f, axis=1), (0, 2, 1))
    scale = d ** -0.5
    outs = []
    for blk in range(s // Q_BLOCK):
        q0, q1 = blk * Q_BLOCK, (blk + 1) * Q_BLOCK
        logits = jnp.einsum('bqhd,bkhd->bhqk', q[:, q0:q1], k[:, :q1]).astype(jnp.float32) * scale
        logits = logits + fcum[:, :, q0:q1, None] - fcum[:, :, None, :q1]
        qpos = jnp.arange(q0, q1)[:, None]
        kpos = jnp.arange(q1)[None, :]
        logits = jnp.where(qpos >= kpos, logits, -jnp.inf)
        probs = jax.nn.softmax(logits, axis=-1)
        outs.append(jnp.einsum('bhqk,bkhd->bqhd', probs.astype(v.dtype), v[:, :q1]))
    return jnp.concatenate(outs, axis=1)

def _hybrid_mixer(h, w_in, b_in, conv_w, conv_b, a_log, d_skip, ssd_norm_g, w_out):
    bsz, s, _ = h.shape
    proj = jnp.einsum('bsd,de->bse', h, w_in) + b_in
    z, xbc, dt_raw, q, k, v, f_raw = _split_cols(proj, IN_SIZES)
    xbc = jax.nn.silu(_causal_dwconv(xbc, conv_w, conv_b))
    xs, bm, cm = _split_cols(xbc, (SSD_INNER, SSD_GROUPS * SSD_STATE, SSD_GROUPS * SSD_STATE))
    xs = xs.reshape(bsz, s, SSD_HEADS, SSD_HEAD_DIM)
    bm = bm.reshape(bsz, s, SSD_GROUPS, SSD_STATE)
    cm = cm.reshape(bsz, s, SSD_GROUPS, SSD_STATE)
    dt = jax.nn.softplus(dt_raw.astype(jnp.float32))
    a = -jnp.exp(a_log.astype(jnp.float32))
    y = _ssd_scan(xs, dt, a, bm, cm, d_skip).reshape(bsz, s, SSD_INNER)
    y = (y * jax.nn.silu(z.astype(jnp.float32))).reshape(bsz, s, SSD_GROUPS, SSD_INNER // SSD_GROUPS)
    y = y * lax.rsqrt(jnp.mean(jnp.square(y), axis=-1, keepdims=True) + RMS_EPS)
    y_ssd = (y.reshape(bsz, s, SSD_INNER) * ssd_norm_g).astype(h.dtype)
    q = q.reshape(bsz, s, ATT_HEADS, ATT_HEAD_DIM)
    k = k.reshape(bsz, s, ATT_HEADS, ATT_HEAD_DIM)
    v = v.reshape(bsz, s, ATT_HEADS, ATT_HEAD_DIM)
    log_f = jax.nn.log_sigmoid(f_raw.astype(jnp.float32))
    y_att = _forgetting_attention(q, k, v, log_f).reshape(bsz, s, ATT_INNER)
    merged = jnp.concatenate([y_ssd, y_att.astype(h.dtype)], axis=-1)
    return jnp.einsum('bse,ed->bsd', merged, w_out)

def _hier_moe(h, rg_w, rg_b, re_w, re_b, w_gate, w_up, w_down):
    bsz, s, d = h.shape
    hf = h.reshape(bsz * s, d)
    g_logits = (hf @ rg_w + rg_b).astype(jnp.float32)
    g_val, g_idx = lax.top_k(jax.nn.softmax(g_logits, axis=-1), 1)
    g_val, g_idx = g_val[:, 0], g_idx[:, 0]
    e_all = (jnp.einsum('td,gde->tge', hf, re_w) + re_b).astype(jnp.float32)
    e_logits = jnp.take_along_axis(e_all, g_idx[:, None, None], axis=1)[:, 0]
    e_val, e_idx = lax.top_k(jax.nn.softmax(e_logits, axis=-1), TOP_K)
    e_val = e_val / jnp.sum(e_val, axis=-1, keepdims=True)
    weights = g_val[:, None] * e_val
    expert_id = g_idx[:, None] * EXPERTS_PER_GROUP + e_idx
    combine = jnp.sum(jax.nn.one_hot(expert_id, N_EXPERTS, dtype=jnp.float32) * weights[..., None], axis=1)
    out = jnp.zeros((bsz * s, d), jnp.float32)
    for e in range(N_EXPERTS):
        act = jax.nn.silu(hf @ w_gate[e]) * (hf @ w_up[e])
        out = out + combine[:, e:e + 1] * (act @ w_down[e]).astype(jnp.float32)
    return out.astype(h.dtype).reshape(bsz, s, d)

def second_inputs(seed: int = 0) -> dict:
    key = jax.random.key(seed)
    ks = jax.random.split(key, 20)
    f32 = jnp.float32
    x = jax.random.normal(ks[0], (BATCH, SEQ, D_MODEL), f32)
    col_scale = np.concatenate([
        np.ones(SSD_INNER + SSD_CONV_DIM), np.full(SSD_HEADS, 0.1),
        np.ones(2 * ATT_INNER), np.full(ATT_INNER, DEEPNORM_BETA), np.full(ATT_HEADS, 0.1)]).astype(np.float32)
    w_in = jax.random.normal(ks[1], (DEPTH_2, D_MODEL, D_IN_PROJ), f32) * (D_MODEL ** -0.5) * jnp.asarray(col_scale)
    b_in = 0.01 * jax.random.normal(ks[2], (DEPTH_2, D_IN_PROJ), f32)
    dt0 = jnp.exp(jax.random.uniform(ks[3], (DEPTH_2, SSD_HEADS), f32, np.log(1e-3), np.log(1e-1)))
    dt_bias = dt0 + jnp.log(-jnp.expm1(-dt0))
    off_dt = SSD_INNER + SSD_CONV_DIM
    b_in = b_in.at[:, off_dt:off_dt + SSD_HEADS].set(dt_bias)
    f_bias = jax.random.uniform(ks[4], (DEPTH_2, ATT_HEADS), f32, 1.0, 5.0)
    b_in = b_in.at[:, D_IN_PROJ - ATT_HEADS:].set(f_bias)
    conv_w = jax.random.normal(ks[5], (DEPTH_2, CONV_WIDTH_2, SSD_CONV_DIM), f32) * (CONV_WIDTH_2 ** -0.5)
    conv_b = 0.01 * jax.random.normal(ks[6], (DEPTH_2, SSD_CONV_DIM), f32)
    a_log = jnp.log(jax.random.uniform(ks[7], (DEPTH_2, SSD_HEADS), f32, 1.0, 16.0))
    d_skip = 1.0 + 0.1 * jax.random.normal(ks[8], (DEPTH_2, SSD_HEADS), f32)
    ssd_norm_g = 1.0 + 0.05 * jax.random.normal(ks[9], (DEPTH_2, SSD_INNER), f32)
    w_out = jax.random.normal(ks[10], (DEPTH_2, D_MIX_2, D_MODEL), f32) * (D_MIX_2 ** -0.5) * DEEPNORM_BETA
    ln1_g = 1.0 + 0.05 * jax.random.normal(ks[11], (DEPTH_2, D_MODEL), f32)
    ln1_b = 0.02 * jax.random.normal(ks[12], (DEPTH_2, D_MODEL), f32)
    router_group_w = jax.random.normal(ks[13], (DEPTH_2, D_MODEL, N_EXPERT_GROUPS), f32) * (D_MODEL ** -0.5)
    router_group_b = 0.01 * jax.random.normal(ks[14], (DEPTH_2, N_EXPERT_GROUPS), f32)
    router_expert_w = jax.random.normal(ks[15], (DEPTH_2, N_EXPERT_GROUPS, D_MODEL, EXPERTS_PER_GROUP), f32) * (D_MODEL ** -0.5)
    router_expert_b = 0.01 * jax.random.normal(ks[16], (DEPTH_2, N_EXPERT_GROUPS, EXPERTS_PER_GROUP), f32)
    kw = jax.random.split(ks[17], 3)
    w_gate = jax.random.normal(kw[0], (DEPTH_2, N_EXPERTS, D_MODEL, D_FF_EXPERT), f32) * (D_MODEL ** -0.5)
    w_up = jax.random.normal(kw[1], (DEPTH_2, N_EXPERTS, D_MODEL, D_FF_EXPERT), f32) * (D_MODEL ** -0.5)
    w_down = jax.random.normal(kw[2], (DEPTH_2, N_EXPERTS, D_FF_EXPERT, D_MODEL), f32) * (D_FF_EXPERT ** -0.5) * DEEPNORM_BETA
    ln2_g = 1.0 + 0.05 * jax.random.normal(ks[18], (DEPTH_2, D_MODEL), f32)
    ln2_b = 0.02 * jax.random.normal(ks[19], (DEPTH_2, D_MODEL), f32)
    return {"x": x, "w_in": w_in, "b_in": b_in, "conv_w": conv_w, "conv_b": conv_b,
            "a_log": a_log, "d_skip": d_skip, "ssd_norm_g": ssd_norm_g, "w_out": w_out,
            "ln1_g": ln1_g, "ln1_b": ln1_b, "router_group_w": router_group_w,
            "router_group_b": router_group_b, "router_expert_w": router_expert_w,
            "router_expert_b": router_expert_b, "w_gate": w_gate, "w_up": w_up,
            "w_down": w_down, "ln2_g": ln2_g, "ln2_b": ln2_b}

def second_block(x, w_in, b_in, conv_w, conv_b, a_log, d_skip, ssd_norm_g, w_out,
              ln1_g, ln1_b, router_group_w, router_group_b, router_expert_w,
              router_expert_b, w_gate, w_up, w_down, ln2_g, ln2_b):
    h = x
    for l in range(DEPTH_2):
        mix = _hybrid_mixer(h, w_in[l], b_in[l], conv_w[l], conv_b[l], a_log[l],
                            d_skip[l], ssd_norm_g[l], w_out[l])
        h = _layer_norm(DEEPNORM_ALPHA * h + mix, ln1_g[l], ln1_b[l])
        ffn = _hier_moe(h, router_group_w[l], router_group_b[l], router_expert_w[l],
                        router_expert_b[l], w_gate[l], w_up[l], w_down[l])
        h = _layer_norm(DEEPNORM_ALPHA * h + ffn, ln2_g[l], ln2_b[l])
    return h


def setup_inputs(seed=0):
    out = dict(first_inputs(seed))
    for name, value in second_inputs(seed + 1).items():
        if name != "x":
            out[name + "_2"] = value
    return out


def reference(
    x, norm_w, w_in, w_out, conv_w, pe_cmp, w_cmp_k, w_cmp_v, pool_w, pool_scale, final_norm_w,
    w_in_2, b_in_2, conv_w_2, conv_b_2, a_log_2, d_skip_2, ssd_norm_g_2, w_out_2, ln1_g_2,
    ln1_b_2, router_group_w_2, router_group_b_2, router_expert_w_2, router_expert_b_2, w_gate_2,
    w_up_2, w_down_2, ln2_g_2, ln2_b_2,
):
    x = first_block(
        x, norm_w, w_in, w_out, conv_w, pe_cmp, w_cmp_k, w_cmp_v, pool_w, pool_scale,
        final_norm_w,
    )
    return second_block(
        x, w_in_2, b_in_2, conv_w_2, conv_b_2, a_log_2, d_skip_2, ssd_norm_g_2, w_out_2,
        ln1_g_2, ln1_b_2, router_group_w_2, router_group_b_2, router_expert_w_2,
        router_expert_b_2, w_gate_2, w_up_2, w_down_2, ln2_g_2, ln2_b_2,
    )


_drawn_inputs = setup_inputs


def setup_inputs(seed=0):
    import zlib

    import numpy as np

    out = dict(_drawn_inputs(seed))
    spreads = {}
    factors = {'pe_cmp': 7.184,
     'conv_b_2': 6.572,
     'a_log_2': 29.544,
     'ssd_norm_g_2': 3.021,
     'router_group_b_2': 43.882,
     'router_expert_b_2': 28.52,
     'ln1_b_2': 2.677}
    for name, (base, spread) in spreads.items():
        noise = np.random.default_rng([zlib.crc32(name.encode()), seed]).standard_normal(out[name].shape)
        drawn = base * np.exp(spread * noise) if base else spread * noise
        out[name] = __import__('jax').numpy.asarray(drawn.astype(out[name].dtype))
    for name, factor in factors.items():
        out[name] = (out[name] * factor).astype(out[name].dtype)
    return out
```

```python
from contextlib import ExitStack

import concourse.bass as bass
import concourse.mybir as mybir
import numpy as np

F32 = mybir.dt.float32
ALU = mybir.AluOpType
ACT = mybir.ActivationFunctionType
AX_X = mybir.AxisListType.X

P = 128
T = 256
TT = T // P
D = 1024
KT = D // P
LAYERS = 2
EPS = 1e-6
HD = 64
NH = 4
TOPK = 64
NCMP = 15
CP = 32
BIG = -1.0e30
TAKEN = -3.0e38
TINY = 1.0e-38
ROPE_THETA = 500000.0

A_Q, A_QI, A_GATE = 0, 384, 680
B_Q, B_KS, B_GATE = 936, 1320, 1588
C_B, C_X, D_U = 1844, 2356, 2868
Z2, XBC2, DT2, Q2, K2, V2, F2 = 0, 512, 1536, 1544, 2056, 2568, 3080
SH = 8
ALPHA = 2.0 ** 0.25
EXPERTS, FF = 16, 512
FT = FF // P
SLOTS = 6
SLOT = KT * 512
ZEROED = 14
SMALL = 16 * 14
SMALL2 = 16 * 21
ARENA = 12584

CONST = {}
CONST_W = 0
for _name, _w in (("ident", 128), ("ncausal", 512), ("cos64", 32), ("sin64", 32), ("cos32", 16), ("sin32", 16),
                  ("cosc", 16), ("sinc", 16), ("cinv", 64), ("cval", 64), ("icnt", 512), ("ltri", 384),
                  ("sgn", 1), ("rank", 4)):
    CONST[_name] = (CONST_W, _w)
    CONST_W += _w


def shape_constants():
    c = np.zeros((P, CONST_W), np.float32)

    def put(name, a, rows=P):
        o, w = CONST[name]
        c[:rows, o:o + w] = np.asarray(a, np.float32).reshape(rows, w)

    p = np.arange(P)
    t = np.arange(TT)[None, :] * P + p[:, None]
    put("ident", np.eye(P))
    put("ncausal", np.arange(T)[None, None, :] > t[:, :, None])

    def angles(pos, half):
        inv = (np.float32(ROPE_THETA) ** (-np.arange(half, dtype=np.float32) / np.float32(half))).astype(np.float32)
        a = pos.astype(np.float32)[..., None] * inv
        return np.concatenate([np.cos(a), np.cos(a)], -1), np.concatenate([np.sin(a), -np.sin(a)], -1)

    for half, name in ((8, "64"), (4, "32")):
        co, si = angles(t, half)
        put("cos" + name, co)
        put("sin" + name, si)
    n = np.arange(CP)
    co, si = angles(16 * n + 31, 8)
    put("cosc", co, CP)
    put("sinc", si, CP)
    inv = (16 * n + 31)[None, None, :] > t[:, :, None]
    inv |= (n >= NCMP)[None, None, :]
    put("cinv", inv)
    put("cval", ~inv)
    win = np.array([[2, 8], [4, 16]])[p // 64]
    put("icnt", 1.0 / np.minimum(np.arange(T)[None, None, :] + 1, win[:, :, None]))
    put("ltri", np.concatenate([p[:, None] <= np.arange(T)[None, :], p[:, None] <= p[None, :]], 1))
    put("sgn", np.where(p < SH, 1.0, -1.0))
    put("rank", np.broadcast_to([4.0, 3.0, 2.0, 1.0], (P, 4)))
    return c


def psum_plan():
    plan, order, used, turn = {}, [], [0] * 8, {}

    def job(key, banks=tuple(range(8))):
        b = banks[turn.get(banks, 0) % len(banks)]
        turn[banks] = turn.get(banks, 0) + 1
        plan[key] = (b, used[b])
        used[b] += 1
        order.append(key)

    def scores(tag, banks=tuple(range(8))):
        for p in range(2):
            job(tag + ("s", p), banks)

    def outputs(tag, banks=tuple(range(8))):
        for kt in range(tag[2] + 1):
            job(tag + ("pT", kt), banks)
        job(tag + ("o",), banks)

    for l in range(LAYERS):
        for tt in range(TT):
            for hf in range(2):
                job((l, "hT", tt, hf))
        job((l, "peT"))
        for name in ("idx", "qkv"):
            for tt in range(TT):
                job((l, name, tt))
        for tt in range(TT):
            job((l, "idxT", tt))
        for tt in range(TT):
            for n in range(4):
                job((l, "logit", tt, n))
        for tt in range(TT):
            job((l, "bq", tt))
        job((l, "kcvc"))
        for tt in range(TT):
            job((l, "bkv", tt))
        for tt in range(TT):
            job((l, "qkT_a", tt))
        for tt in range(TT):
            job((l, "gates", tt))
        for tt in range(TT):
            job((l, "qkT_b", tt))
        for name in ("kcmp", "vcmp"):
            job((l, name))
        for name in ("c_b", "c_c", "c_x", "c_g", "d_u", "d_g"):
            job((l, name))
        job((l, "kcT"))
        for tt in range(TT):
            job((l, "cmp_s", tt))
        for tt in range(TT):
            job((l, "cmp_pT", tt))
            job((l, "cmp_o", tt))
        job((l, "pool"))
        groups = layer_groups(l)
        scores(groups[0])
        for n, tag in enumerate(groups):
            if n + 1 < len(groups):
                scores(groups[n + 1])
            outputs(tag)
        for tt in range(TT):
            job((l, "mixT", tt))
        for tt in range(TT):
            for hf in range(2):
                job((l, "wo", tt, hf))
    for tt in range(TT):
        for hf in range(2):
            job(("hT", tt, hf))
    job(("dtf",))
    for n in range(4):
        job(("xbc", n))
    for name in ("q", "k", "z", "v"):
        for n in range(2):
            job((name, n))
    job(("tA",))
    for tt in range(TT):
        job(("xs", tt))
    for g in range(2):
        job(("cb", g))
    for n in range(TT):
        job(("y", n), (0, 1))
    for h in range(SH):
        job(("Ab", h), (2, 3, 4))
        if h % 2:
            scores(GROUPS2[h // 2], (5, 6, 7))
            if h > 1:
                outputs(GROUPS2[h // 2 - 1], (5, 6, 7))
    outputs(GROUPS2[-1], (5, 6, 7))
    for tt in range(TT):
        for hf in range(2):
            job(("mT", tt, hf))
    for tt in range(TT):
        for hf in range(2):
            job(("wo", tt, hf))
    for tt in range(TT):
        for hf in range(2):
            job(("h1T", tt, hf))
    for tt in range(TT):
        job(("route", tt))
    job(("combT",))
    for n in range(EXPERTS // 2):
        job(("comb", n))
    for n in range(4):
        job(("acc", n), (n,))
    return plan, order, used


def layer_groups(l):
    return [(l, branch, tt) for branch in ("slc", "win", "dsa") for tt in range(TT)]


GROUPS2 = [("att", half, tt) for half in range(2) for tt in range(TT)]


def weight_plan(a):
    w = []

    def cols(m, *ranges):
        out, at = [], 0
        for lo, n in ranges:
            out.append((at, m.rearrange("(p k) n -> p k n", k=KT)[:, :, lo:lo + n]))
            at += n
        return out

    def half(m, n):
        return [(0, m.rearrange("(k p) n -> p k n", p=P)[:, :, n * 512:n * 512 + 512])]

    for l in range(LAYERS):
        m, o = a["w_in"][l], a["w_out"][l]
        w += [((l, "w_idx"), cols(m, (A_QI, 296)), (l, "idx", 1)),
              ((l, "w_qkv"), cols(m, (A_Q, 384)), (l, "qkv", 1)),
              ((l, "w_bq"), cols(m, (B_Q, 384)), (l, "kcvc")),
              ((l, "w_bkv"), cols(m, (B_KS, 268)), (l, "bkv", 1)),
              ((l, "w_gates"), cols(m, (A_GATE, 256), (B_GATE, 256)), (l, "gates", 1)),
              ((l, "w_c1"), cols(m, (C_B, 512)), (l, "c_c")),
              ((l, "w_c2"), cols(m, (C_X, 512)), (l, "c_g")),
              ((l, "w_d"), cols(m, (D_U, 512)), (l, "d_g")),
              ((l, "w_out0"), half(o, 0), (l, "wo", 1, 0)),
              ((l, "w_out1"), half(o, 1), (l, "wo", 1, 1))]
    m, o = a["w_in_2"][0], a["w_out_2"][0]
    w += [(("xbc0",), cols(m, (XBC2, 512)), ("xbc", 1)),
          (("xbc1",), cols(m, (XBC2 + 512, 512)), ("xbc", 3)),
          (("q",), cols(m, (Q2, 512)), ("q", 1)),
          (("k",), cols(m, (K2, 512)), ("k", 1)),
          (("z",), cols(m, (Z2, 512)), ("z", 1)),
          (("v",), cols(m, (V2, 512)), ("v", 1)),
          (("out0",), half(o, 0), ("wo", 1, 0)),
          (("out1",), half(o, 1), ("wo", 1, 1))]
    return w


def build(nc, a, out):
    plan, order, used = psum_plan()
    ctx = ExitStack()
    with ctx:
        def sb(name, *shape):
            return ctx.enter_context(nc.sbuf_tensor(name, [P, *shape], F32))

        def sem(name):
            return ctx.enter_context(nc.semaphore(name))

        def shaped(flat, *shape):
            names = "abcd"[:len(shape)]
            n = int(np.prod(shape))
            if len(shape) == 1:
                return flat[:, 0:n]
            return flat[:, 0:n].rearrange("p (" + " ".join(names) + ") -> p " + " ".join(names),
                                          **dict(zip(names[1:], shape[1:])))

        class Region:

            def __init__(self, flat, width):
                self.flat, self.width, self.at = flat, width, 0

            def take(self, *shape):
                n = int(np.prod(shape))
                assert self.at + n <= self.width, (self.at, n, self.width)
                v = shaped(self.flat[:, self.at:self.at + n], *shape)
                self.at += n
                return v

        psum = [ctx.enter_context(nc.psum_tensor(f"bank{b}", [P, 512], F32)) for b in range(8)]
        ring = sb("weight_ring", SLOTS, SLOT)
        cst = sb("shape_constants_sb", CONST_W)
        zero = sb("zeros", P)
        x = sb("residual_stream", TT, D)
        hn_f, hT_f, mixT_f, ex_f, exT_f = (sb(n, TT * D) for n in ("normed", "normed_T", "mixed_T", "probs", "probs_T"))
        hn = shaped(hn_f, TT, D)
        hT = shaped(hT_f, KT, T)
        mixT = shaped(mixT_f, KT, T)
        sm = shaped(hT_f, 2, NH, T)
        ex = shaped(ex_f, 2, NH, T)
        exT = shaped(exT_f, 2, TT, NH * P)
        arena = sb("arena", ARENA)

        small = Region(sb("small_vectors", 752), 752)
        stat = small.take(4, TT)
        normw = small.take(LAYERS, KT)
        rt = sb("rope_scratch", 2, 192)
        top8 = small.take(8)
        mx, sums, coef = (small.take(2, NH) for _ in range(3))
        cmx, csum = small.take(NH), small.take(NH)
        gate = small.take(TT, 12)
        cw = small.take(LAYERS, 3, 2)
        psc = small.take(LAYERS, 2)
        wdtf = small.take(KT, 16)
        b16 = small.take(4)
        dA = small.take(4, 16)
        bx, bqk = small.take(8), small.take(8)
        cw2 = small.take(4, 8)
        cb2 = small.take(8)
        g8 = small.take(KT)
        dsk = small.take(SH)
        wr = small.take(KT, 20)
        rb = small.take(20)
        rl = small.take(TT, 20)
        rs = small.take(12, TT, 4)
        rv = small.take(12, TT)
        comb = small.take(TT, 16)
        coef2 = small.take(4, TT)
        pw = sb("pool_w_blocks", LAYERS, 2, P)

        A = Region(arena, ARENA)
        ni, na, nb = A.take(TT, 392), A.take(TT, 448), A.take(TT, 652)
        kiT = A.take(4, T)
        kaT, ksT, kwT = (A.take(2, T) for _ in range(3))
        qaT, qbT = A.take(2, T), A.take(2, T)
        amask = A.take(TT, T)
        kvT = A.take(T)
        blk = A.take(32, CP)
        pe2, peT = A.take(2, HD), A.take(32)
        kcN = A.take(2 * HD)
        kcT = A.take(2, CP)
        vcB = A.take(NH, HD)
        gsil = A.take(TT, 512)
        mixN = A.take(TT, 512)
        cgS = A.take(2, T)
        du = A.take(2, T + 16)
        dg = A.take(2, T)
        wcmp = shaped(ex_f, 32, HD)
        over = Region(exT_f, TT * D)
        ccS, cbS, qiT, score = over.take(2, T), over.take(2, T), over.take(2, T), over.take(2, T)
        over = Region(exT_f[:, 1536:2048], 512)
        smc, ec, pcT = over.take(NH, CP), over.take(NH, CP), over.take(P)
        relu = shaped(hn_f, 8, T)
        over = Region(hn_f, TT * D)
        d2, d4, cu = over.take(2, T + 16), over.take(2, T + 16), over.take(2, T)
        ob = shaped(mixT_f, TT, 2, 256)
        cy = mixT[:, 4:6, :]

        B = Region(arena, ARENA)
        xc = B.take(8, T)
        kT2 = B.take(4, 2, T)
        qT2 = B.take(4, T)
        v2, z2 = B.take(TT, 512), B.take(TT, 512)
        cbm, seg, mTh = B.take(2, 384), B.take(2, 384), B.take(2, 384)
        dtf = B.take(8, T)
        brow = B.take(1024)
        xbc = shaped(exT_f, 8, T)
        xsN, xdt = shaped(mixT_f, TT, 512), shaped(mixT_f[:, 1024:2048], TT, 512)
        vec = shaped(ex_f, 2, D)
        merged = hn
        M = Region(arena, ARENA)
        combB = M.take(EXPERTS, T)
        combT = M.take(T)
        silu_g, act_u = M.take(2, 2, T), M.take(2, 2, T)
        actT = shaped(exT_f, 2, FT, T)

        def C(name, rows=P, a_=None):
            o, w = CONST[name]
            v = cst[0:rows, o:o + w]
            return v.rearrange("p (a b) -> p a b", a=a_) if a_ else v

        ident = C("ident")
        ncausal, cos64, sin64, cos32, sin32, cinv, cval, icnt = (
            C(n, a_=2) for n in ("ncausal", "cos64", "sin64", "cos32", "sin32", "cinv", "cval", "icnt"))

        def spread(ap, n):
            return ap.unsqueeze(2).broadcast_to([ap.shape[0], ap.shape[1], n])

        def repeat(ap, n):
            return ap.unsqueeze(1).broadcast_to([ap.shape[0], n, ap.shape[1]])

        filled = [sem(f"bank{b}_filled") for b in range(8)]
        drained = [sem(f"bank{b}_drained") for b in range(8)]
        slot_here = [sem(f"slot{s}_loaded") for s in range(SLOTS)]

        class Signal:

            def __init__(self, name, per=0):
                self.sem, self.n, self.per = sem(name), 0, per

            def fire(self, ins):
                self.n += 1
                return ins.then_inc(self.sem, 1)

            def at(self, l, k):
                return l * self.per + k

        x_loaded, const_loaded, small_loaded, small2_loaded = (sem(n) for n in (
            "x_loaded", "constants_loaded", "layer_vectors_loaded", "second_vectors_loaded"))
        cmp_loaded, vec_loaded, brow_loaded, stored = sem("cmp_weights_loaded"), sem("row_vectors_loaded"), sem("z_v_bias_rows_loaded"), sem("output_stored")
        zeroed = sem("pads_zeroed")
        vstep, astep, gstep = Signal("vector_step"), Signal("scalar_step"), Signal("pool_step")
        sumsq, invms, rstd_s = Signal("squares_summed", TT), Signal("mean_squares_inverted", 1), Signal("rstd_ready", 1)
        normed = Signal("normed_ready", TT)
        scored = Signal("index_scores_ready", TT)
        roped_i, roped_a, roped_b = Signal("idx_roped", TT), Signal("a_roped", TT), Signal("b_roped", TT)
        roped_c, blocks = Signal("kcmp_roped", 1), Signal("cmp_blocks_ready", 1)
        cmax, cexp, cprob = Signal("cmp_max_taken", TT), Signal("cmp_exp_done", TT), Signal("cmp_probs_ready", TT)
        gexp = Signal("branch_gates_exp", TT)
        rmax, expd = Signal("group_max_ready", 6), Signal("group_exp_done", 6 * NH)
        pooled, conv_y, conv_done = Signal("pooled_ready", 1), Signal("conv_taps_summed", 1), Signal("conv_into_mixed", 1)
        b_part, b_done = Signal("b_branches_ready", TT), Signal("b_into_mixed", TT)
        mixr = Signal("mixed_natural_ready", TT)
        vec_free, h0_ready = Signal("row_vectors_used"), Signal("h0_ready")
        coef_in, cum_ready = Signal("dt_f_steps"), Signal("cumsums_ready")
        dt_exp, dt_w, dt_ln = Signal("dt_f_exp"), Signal("dt_f_one_plus"), Signal("dt_f_ln")
        conv2, act2 = Signal("xbc_taps_summed"), Signal("xbc_silu_ready")
        zb, z_ready, xdt_ready = Signal("z_biased"), Signal("z_silu_ready"), Signal("xdt_ready")
        seg_r, dec_e, decay, y_used = Signal("decay_logs"), Signal("decay_exp"), Signal("decay_products"), Signal("y_head_done")
        ysq, yinv, yrstd = Signal("y_squares"), Signal("y_inverted"), Signal("y_rstd")
        merged_ready, ln_mu, ln_sq, ln_inv, ln_rstd = (Signal(n) for n in (
            "merged_ready", "ln_centred", "ln_squares", "ln_inverted", "ln_rstd"))
        h1_ready, final_ready = Signal("h1_ready"), Signal("output_rows_ready")
        r_in, r_exp, comb_ready = Signal("router_shifted"), Signal("router_exp"), Signal("combine_ready")
        act_ready = Signal("expert_act_ready")

        yz, k2_zeroed, g8_ones = Signal("y_gated"), Signal("k2_blocks_zeroed"), Signal("merge_ones")

        def row(name):
            return a[name].rearrange("(o n) -> o n", o=1)

        def load_layer_vectors(eng):
            n = 0
            for l in range(LAYERS):
                pairs = [(normw[:, l, :], a["norm_w"][l].rearrange("(p k) -> p k", k=KT)),
                         (psc[:, l, :], a["pool_scale"][l].rearrange("(c p) -> p c", p=P))]
                pairs += [(cw[:, l, j, :], a["conv_w"][l, j].rearrange("(c p) -> p c", p=P)) for j in range(3)]
                for h in range(2):
                    r = slice(HD * h, HD * h + HD)
                    pairs.append((pw[r, l, :, r], a["pool_w"][l].rearrange("(j h) c d -> h c j d", h=2)[h]))
                for n_, (dst, src) in enumerate(pairs):
                    if l == 0 and n_ == 0:
                        eng.wait_ge(zeroed, ZEROED)
                    eng.dma_start(dst, src, allow_slow_non_contiguous=True).then_inc(small_loaded, 16)
                    n += 1
            assert SMALL == 16 * n, n

        def load_second_vectors(eng):
            wi = a["w_in_2"][0].rearrange("(p k) n -> p k n", k=KT)
            bi = a["b_in_2"][0]
            col = lambda v: v.rearrange("(c p) -> p c", p=P)
            one = lambda v: v.rearrange("(n o) -> n o", o=1)
            pairs = [(wdtf[:, :, 0:8], wi[:, :, DT2:DT2 + 8]), (wdtf[:, :, 8:16], wi[:, :, F2:F2 + 8]),
                     (b16[0:8, 0:1], one(bi[DT2:DT2 + 8])), (b16[8:16, 0:1], one(bi[F2:F2 + 8])),
                     (b16[0:8, 1:2], one(a["a_log_2"][0])),
                     (bx, col(bi[XBC2:XBC2 + 1024])), (bqk, col(bi[Q2:Q2 + 1024])),
                     (cb2, col(a["conv_b_2"][0])), (g8[:, 0:4], col(a["ssd_norm_g_2"][0])),
                     (dsk, a["d_skip_2"].broadcast_to([P, SH])),
                     (rb[:, 0:4], a["router_group_b_2"].broadcast_to([P, 4])),
                     (rb[:, 4:20], a["router_expert_b_2"].rearrange("o g e -> o (g e)").broadcast_to([P, 16])),
                     (wr[:, :, 0:4], a["router_group_w_2"][0].rearrange("(p k) n -> p k n", k=KT))]
            pairs += [(cw2[:, j, :], col(a["conv_w_2"][0, j])) for j in range(4)]
            pairs += [(wr[:, :, 4 + 4 * g:8 + 4 * g], a["router_expert_w_2"][0, g].rearrange("(p k) n -> p k n", k=KT))
                      for g in range(4)]
            for dst, src in pairs:
                eng.dma_start(dst, src, allow_slow_non_contiguous=True).then_inc(small2_loaded, 16)
            assert SMALL2 == 16 * len(pairs), len(pairs)

        small_dmas = (load_layer_vectors, load_second_vectors)
        block = ctx.enter_context(nc.Block())

        def bank(key):
            return psum[plan[key][0]]

        def wait_filled(eng, key):
            b, n = plan[key]
            eng.wait_ge(filled[b], n + 1)
            return psum[b]

        def wait_drained(eng, key):
            b, n = plan[key]
            eng.wait_ge(drained[b], n + 1)

        def drains(ins, key):
            return ins.then_inc(drained[plan[key][0]], 1)

        chunks, loads, value, last = {}, [], [0] * SLOTS, [None] * SLOTS
        for n, (key, pieces, job) in enumerate(weight_plan(a)):
            s = n % SLOTS
            value[s] += 16 * len(pieces)
            width = sum(p[1].shape[2] for p in pieces)
            view = ring[:, s, 0:KT * width].rearrange("p (k n) -> p k n", k=KT)
            loads.append((s, last[s], [(view[:, :, at:at + p.shape[2]], p) for at, p in pieces]))
            chunks[key] = (s, value[s], view)
            last[s] = job
        expert_slot0 = len(loads) % SLOTS

        def eslot(e, k):
            return (expert_slot0 + 3 * (e % 2) + k) % SLOTS

        LAST_BANK = (5, 7, 3)

        @block.sync
        def _(sp):
            for tt in range(TT):
                sp.dma_start(x[:, tt, :], a["x"][0, tt * P:(tt + 1) * P, :]).then_inc(x_loaded, 16)
            for s, job, pieces in loads:
                if job is not None:
                    wait_filled(sp, job)
                for dst, src in pieces:
                    sp.dma_start(dst, src).then_inc(slot_here[s], 16)
            for e in range(EXPERTS):
                for k, name in enumerate(("w_gate_2", "w_up_2", "w_down_2")):
                    s = eslot(e, k)
                    if e < 2:
                        wait_filled(sp, last[s])
                    else:
                        sp.wait_ge(filled[LAST_BANK[k]], used[LAST_BANK[k]] + e - 1)
                    n = KT if k < 2 else FT
                    src = a[name][0, e]
                    src = src.rearrange("(p k) n -> p k n", k=n) if k < 2 else src.rearrange("(k p) n -> p k n", p=P)
                    sp.dma_start(ring[:, s, :].rearrange("p (k n) -> p k n", k=n), src).then_inc(slot_here[s], 16)
            for tt in range(TT):
                sp.wait_ge(final_ready.sem, tt + 1)
                sp.dma_start(out[0, tt * P:(tt + 1) * P, :], x[:, tt, :]).then_inc(stored, 16)
            sp.wait_ge(stored, 16 * TT)

        @block.tensor
        def _(pe):
            todo = list(order)

            def claim(key):
                assert todo.pop(0) == key, key
                b, n = plan[key]
                if n:
                    pe.wait_ge(drained[b], n)
                return psum[b]

            def fill(ins, key):
                ins.then_inc(filled[plan[key][0]], 1)

            def weights(key):
                s, v, view = chunks[key]
                pe.wait_ge(slot_here[s], v)
                return view

            def product(dst, lhs, rhs, n=KT, **kw):
                for k in range(n):
                    ins = pe.matmul(dst, lhs(k), rhs(k), start=(k == 0), stop=(k == n - 1), **kw)
                return ins

            def token_rows(key, w, tt, c0, n):
                ps = claim(key)
                fill(product(ps[:, 0:n], lambda k: hT[:, k, tt * P:(tt + 1) * P], lambda k: w[:, k, c0:c0 + n]), key)

            def channel_rows(key, w, c0, tiles):
                ps = claim(key)
                for j in range(tiles):
                    ins = product(ps[:, j * T:(j + 1) * T], lambda k: w[:, k, c0 + j * P:c0 + (j + 1) * P],
                                  lambda k: hT[:, k, :])
                fill(ins, key)

            def transposes(key, srcs, width=P, rows=P):
                ps = claim(key)
                for n, src in enumerate(srcs):
                    ins = pe.transpose(ps[0:src.shape[1], n * width:n * width + rows], src, ident[0:rows, 0:rows])
                fill(ins, key)

            def natural_to_T(key, src, tt, hf, strided):
                transposes(key, [src[:, tt, (4 * hf + k):D:KT] if strided else
                                 src[:, tt, (4 * hf + k) * P:(4 * hf + k + 1) * P] for k in range(4)])

            group = [0]

            def scores(tag, qT, kT, extra=None):
                tt = tag[2]
                nk = (tt + 1) * P
                for p in range(2):
                    ps = claim(tag + ("s", p))
                    dst = ps[:, 0:2 * nk].rearrange("p (a b) -> p a b", a=2)
                    ins = pe.matmul(dst, qT(p)[:, tt * P:(tt + 1) * P], kT(p)[:, :, 0:nk], start=True, stop=True)
                    if extra is not None:
                        for j in range(2):
                            ins = pe.matmul(dst[:, j, :], extra(2 * p + j), dtf[0:16, 6, 0:nk], start=False, stop=True,
                                            skip_group_check=True)
                    fill(ins, tag + ("s", p))

            def outputs(tag, v):
                tt = tag[2]
                g = group[0]
                group[0] += 1
                for h in range(NH):
                    pe.wait_ge(expd.sem, NH * g + h + 1)
                    if h == 0:
                        for kt in range(tt + 1):
                            claim(tag + ("pT", kt))
                    for kt in range(tt + 1):
                        ins = pe.transpose(bank(tag + ("pT", kt))[:, h * P:(h + 1) * P],
                                           ex[:, g % 2, h, kt * P:(kt + 1) * P], ident)
                        if h == NH - 1:
                            fill(ins, tag + ("pT", kt))
                ps = claim(tag + ("o",))
                for kt in range(tt + 1):
                    wait_drained(pe, tag + ("pT", kt))
                for h in range(NH):
                    ins = product(ps[:, h * HD:(h + 1) * HD], lambda kt: exT[:, g % 2, kt, h * P:(h + 1) * P],
                                  lambda kt: v(kt, h), n=tt + 1)
                fill(ins, tag + ("o",))

            pe.wait_ge(const_loaded, 16)
            pe.wait_ge(zeroed, ZEROED)
            for l in range(LAYERS):
                for tt in range(TT):
                    pe.wait_ge(normed.sem, normed.at(l, tt + 1))
                    for hf in range(2):
                        natural_to_T((l, "hT", tt, hf), hn, tt, hf, True)
                pe.wait_ge(cmp_loaded, 64 * (l + 1))
                transposes((l, "peT"), [pe2[0:32, :, :].rearrange("p a b -> p (a b)")], rows=32)
                for tt in range(TT):
                    for hf in range(2):
                        wait_drained(pe, (l, "hT", tt, hf))
                w = weights((l, "w_idx"))
                for tt in range(TT):
                    token_rows((l, "idx", tt), w, tt, 0, 296)
                w = weights((l, "w_qkv"))
                for tt in range(TT):
                    token_rows((l, "qkv", tt), w, tt, 0, 384)
                for tt in range(TT):
                    pe.wait_ge(roped_i.sem, roped_i.at(l, tt + 1))
                    transposes((l, "idxT", tt), [ni[:, tt, n * P:(n + 1) * P] for n in range(3)])
                for tt in range(TT):
                    wait_drained(pe, (l, "idxT", tt))
                for tt in range(TT):
                    for n in range(4):
                        ps = claim((l, "logit", tt, n))
                        nk = (tt + 1) * P
                        fill(pe.matmul(ps[:, 0:2 * nk].rearrange("p (a b) -> p a b", a=2),
                                       qiT[:, n // 2, tt * P:(tt + 1) * P],
                                       kiT[:, 2 * (n % 2):2 * (n % 2) + 2, 0:nk], start=True, stop=True),
                             (l, "logit", tt, n))
                w = weights((l, "w_bq"))
                for tt in range(TT):
                    token_rows((l, "bq", tt), w, tt, 0, 256)
                channel_rows((l, "kcvc"), w, 256, 1)
                w = weights((l, "w_bkv"))
                for tt in range(TT):
                    token_rows((l, "bkv", tt), w, tt, 0, 268)
                for tt in range(TT):
                    pe.wait_ge(roped_a.sem, roped_a.at(l, tt + 1))
                    transposes((l, "qkT_a", tt), [na[:, tt, n * P:(n + 1) * P] for n in range(3)])
                w = weights((l, "w_gates"))
                for tt in range(TT):
                    token_rows((l, "gates", tt), w, tt, 0, 512)
                for tt in range(TT):
                    pe.wait_ge(roped_b.sem, roped_b.at(l, tt + 1))
                    transposes((l, "qkT_b", tt), [nb[:, tt, n * P:(n + 1) * P] for n in range(4)])
                pe.wait_ge(blocks.sem, blocks.at(l, 1))
                for n, name in enumerate(("kcmp", "vcmp")):
                    r = slice(n * HD, (n + 1) * HD)
                    ps = claim((l, name))
                    fill(product(ps[0:CP, 0:HD], lambda k: blk[r, k, :], lambda k: wcmp[r, k, :], n=32), (l, name))
                w = weights((l, "w_c1"))
                channel_rows((l, "c_b"), w, 0, 2)
                channel_rows((l, "c_c"), w, 256, 2)
                w = weights((l, "w_c2"))
                channel_rows((l, "c_x"), w, 0, 2)
                channel_rows((l, "c_g"), w, 256, 2)
                w = weights((l, "w_d"))
                channel_rows((l, "d_u"), w, 0, 2)
                channel_rows((l, "d_g"), w, 256, 2)
                pe.wait_ge(roped_c.sem, roped_c.at(l, 1))
                transposes((l, "kcT"), [kcN[0:CP, :]], rows=CP)
                wait_drained(pe, (l, "kcT"))
                wait_drained(pe, (l, "vcmp"))
                for tt in range(TT):
                    wait_drained(pe, (l, "qkT_b", tt))
                for tt in range(TT):
                    ps = claim((l, "cmp_s", tt))
                    for p in range(2):
                        ins = pe.matmul(ps[:, p * 64:p * 64 + 64].rearrange("p (a b) -> p a b", a=2),
                                        qbT[:, p, tt * P:(tt + 1) * P], kcT[:, :, :], start=True, stop=True)
                    fill(ins, (l, "cmp_s", tt))
                for tt in range(TT):
                    pe.wait_ge(cprob.sem, cprob.at(l, tt + 1))
                    transposes((l, "cmp_pT", tt), [ec[:].rearrange("p a b -> p (a b)")])
                    wait_drained(pe, (l, "cmp_pT", tt))
                    ps = claim((l, "cmp_o", tt))
                    fill(pe.matmul(ps[:, 0:256], pcT[:, :], vcB[:].rearrange("p a b -> p (a b)"), start=True, stop=True),
                         (l, "cmp_o", tt))
                pe.wait_ge(pooled.sem, pooled.at(l, 1))
                ps = claim((l, "pool"))
                for j in range(2):
                    ins = pe.matmul(ps[:, j * T:(j + 1) * T], pw[:, l, j, :], mixT[:, 6 + j, :], start=True, stop=True)
                fill(ins, (l, "pool"))
                operands = {"slc": (qbT, ksT, nb, 512), "win": (qbT, kwT, nb, 576), "dsa": (qaT, kaT, na, 384)}

                def layer_scores(tag):
                    q, k, _, _ = operands[tag[1]]
                    scores(tag, lambda p: q[:, p, :], lambda p: k[:])

                groups = layer_groups(l)
                layer_scores(groups[0])
                for n, tag in enumerate(groups):
                    if n + 1 < len(groups):
                        layer_scores(groups[n + 1])
                    _, _, vals, at = operands[tag[1]]
                    outputs(tag, lambda kt, h: vals[:, kt, at:at + HD])
                for tt in range(TT):
                    pe.wait_ge(mixr.sem, mixr.at(l, tt + 1))
                    transposes((l, "mixT", tt), [mixN[:, tt, n * P:(n + 1) * P] for n in range(4)])
                pe.wait_ge(conv_done.sem, conv_done.at(l, 1))
                wait_drained(pe, (l, "pool"))
                for tt in range(TT):
                    wait_drained(pe, (l, "mixT", tt))
                    for hf in range(2):
                        w = weights((l, f"w_out{hf}"))
                        ps = claim((l, "wo", tt, hf))
                        fill(product(ps[:, :], lambda k: mixT[:, k, tt * P:(tt + 1) * P], lambda k: w[:, k, :]),
                             (l, "wo", tt, hf))
            for tt in range(TT):
                pe.wait_ge(h0_ready.sem, tt + 1)
                for hf in range(2):
                    natural_to_T(("hT", tt, hf), x, tt, hf, True)
            for tt in range(TT):
                for hf in range(2):
                    wait_drained(pe, ("hT", tt, hf))
            pe.wait_ge(small2_loaded, SMALL2)
            ps = claim(("dtf",))
            fill(product(ps[0:16, 0:T], lambda k: wdtf[:, k, :], lambda k: hT[:, k, :]), ("dtf",))
            for n in range(4):
                channel_rows(("xbc", n), weights((f"xbc{n // 2}",)), 256 * (n % 2), 2)
            for name in ("q", "k"):
                for n in range(2):
                    channel_rows((name, n), weights((name,)), 256 * n, 2)
            for name in ("z", "v"):
                for tt in range(TT):
                    token_rows((name, tt), weights((name,)), tt, 0, 512)
            pe.wait_ge(cum_ready.sem, 1)
            transposes(("tA",), [dtf[0:16, r, tt * P:(tt + 1) * P] for tt in range(TT) for r in (4, 5)], width=16, rows=16)
            pe.wait_ge(act2.sem, 8)
            for tt in range(TT):
                transposes(("xs", tt), [xc[:, n, tt * P:(tt + 1) * P] for n in range(4)])
            for g in range(2):
                ps = claim(("cb", g))
                pe.matmul(ps[:, 0:T], xc[:, 4 + g, 0:P], xc[:, 6 + g, :], start=True, stop=True)
                fill(pe.matmul(ps[:, T:T + P], xc[:, 4 + g, P:T], xc[:, 6 + g, P:T], start=True, stop=True), ("cb", g))
            for n in range(TT):
                claim(("y", n))

            def y_head(h):
                pe.wait_ge(decay.sem, h + 1)
                if h == 0:
                    pe.wait_ge(xdt_ready.sem, 1)
                r = xdt[:, :, h * HD:(h + 1) * HD]
                a0 = pe.matmul(psum[0][:, h * HD:(h + 1) * HD], mTh[:, h % 2, 0:P], r[:, 0, :], start=True, stop=True)
                pe.matmul(psum[1][:, h * HD:(h + 1) * HD], mTh[:, h % 2, P:T], r[:, 0, :], start=True, stop=False)
                a1 = pe.matmul(psum[1][:, h * HD:(h + 1) * HD], mTh[:, h % 2, T:T + P], r[:, 1, :], start=False, stop=True)
                if h < SH - 1:
                    y_used.fire(a1)
                else:
                    fill(a0, ("y", 0))
                    fill(a1, ("y", 1))

            def scores2(tag):
                h0 = NH * tag[1]
                scores(tag, lambda p: qT2[:, h0 // 2 + p, :], lambda p: kT2[:, h0 // 2 + p, :, :],
                       extra=lambda h: ident[0:16, SH + h0 + h:SH + h0 + h + 1].broadcast_to([16, P]))

            def outputs2(tag):
                h0 = NH * tag[1]
                outputs(tag, lambda kt, h: v2[:, kt, (h0 + h) * HD:(h0 + h + 1) * HD])

            for h in range(SH):
                ps = claim(("Ab", h))
                fill(pe.matmul(ps[:, 0:T], ident[0:16, h:h + 1].broadcast_to([16, P]), dtf[0:16, 5, :], start=True, stop=True),
                     ("Ab", h))
                if h:
                    y_head(h - 1)
                if h % 2:
                    if h == 1:
                        wait_drained(pe, ("q", 1))
                        wait_drained(pe, ("k", 1))
                        wait_drained(pe, ("v", 1))
                        pe.wait_ge(cum_ready.sem, 2)
                    scores2(GROUPS2[h // 2])
                    if h > 1:
                        outputs2(GROUPS2[h // 2 - 1])
            y_head(SH - 1)
            outputs2(GROUPS2[-1])
            for tt in range(TT):
                pe.wait_ge(merged_ready.sem, tt + 1)
                for hf in range(2):
                    natural_to_T(("mT", tt, hf), merged, tt, hf, False)
            for tt in range(TT):
                for hf in range(2):
                    wait_drained(pe, ("mT", tt, hf))
                for hf in range(2):
                    w = weights((f"out{hf}",))
                    ps = claim(("wo", tt, hf))
                    fill(product(ps[:, :], lambda k: mixT[:, k, tt * P:(tt + 1) * P], lambda k: w[:, k, :]), ("wo", tt, hf))
            for tt in range(TT):
                pe.wait_ge(h1_ready.sem, tt + 1)
                for hf in range(2):
                    natural_to_T(("h1T", tt, hf), x, tt, hf, True)
            for tt in range(TT):
                for hf in range(2):
                    wait_drained(pe, ("h1T", tt, hf))
                ps = claim(("route", tt))
                fill(product(ps[:, 0:20], lambda k: hT[:, k, tt * P:(tt + 1) * P], lambda k: wr[:, k, :]), ("route", tt))
            pe.wait_ge(comb_ready.sem, 1)
            ps = claim(("combT",))
            for tt in range(TT):
                ins = pe.transpose(ps[0:16, tt * P:(tt + 1) * P], comb[:, tt, :], ident)
            fill(ins, ("combT",))
            wait_drained(pe, ("combT",))
            for n in range(EXPERTS // 2):
                ps = claim(("comb", n))
                for j in range(2):
                    e = 2 * n + j
                    ins = pe.matmul(ps[:, j * T:(j + 1) * T], ident[0:16, e:e + 1].broadcast_to([16, P]), combT[0:16, :],
                                    start=True, stop=True)
                fill(ins, ("comb", n))
            for n in range(4):
                ps = claim(("acc", n))
                fill(pe.matmul(ps[:, :], zero[:, :], x[:, 0, 0:512], start=True, stop=True), ("acc", n))

            def gate_up(e):
                for k in range(2):
                    s = eslot(e, k)
                    pe.wait_ge(slot_here[s], value[s] + 16 * (e // 2 + 1))
                    w = ring[:, s, :].rearrange("p (k n) -> p k n", k=KT)
                    for hf in range(2):
                        b = 4 + 2 * k + hf
                        pe.wait_ge(drained[b], used[b] + e)
                        for j in range(2):
                            c = (2 * hf + j) * P
                            ins = product(psum[b][:, j * T:(j + 1) * T], lambda k: w[:, k, c:c + P], lambda k: hT[:, k, :])
                        ins.then_inc(filled[b], 1)

            def down(e):
                s = eslot(e, 2)
                pe.wait_ge(slot_here[s], value[s] + 16 * (e // 2 + 1))
                pe.wait_ge(act_ready.sem, e + 1)
                w = ring[:, s, :].rearrange("p (k n) -> p k n", k=FT)
                for tt in range(TT):
                    for hf in range(2):
                        for f in range(FT):
                            ins = pe.matmul(psum[2 * tt + hf][:, :], actT[:, e % 2, f, tt * P:(tt + 1) * P],
                                            w[:, f, hf * 512:(hf + 1) * 512], start=False, stop=True, skip_group_check=True)
                ins.then_inc(filled[3], 1)

            for e in range(EXPERTS):
                gate_up(e)
                if e:
                    down(e - 1)
            down(EXPERTS - 1)
            assert not todo

        @block.vector
        def _(dve):
            def step(ins):
                vstep.fire(ins)
                dve.wait_ge(vstep.sem, vstep.n)

            def step_on(signal, ins):
                signal.fire(ins)
                dve.wait_ge(signal.sem, signal.n)

            def drain_step(ins, key):
                drains(ins, key)
                wait_drained(dve, key)

            V = nc.vector

            def inverse(dst, src, guard=None):
                if guard is not None:
                    step(V.tensor_scalar(src, src, guard, None, ALU.max))
                step(V.reciprocal(dst, src))

            def invert_mean_squares(n, eps, src, dst, signal):
                step(V.tensor_scalar(src, src, 1.0 / n, eps, ALU.mult, ALU.add))
                signal.fire(V.reciprocal(dst, src))

            def copy_T(key, tt, hf, scale=None, dst=hT):
                ps = wait_filled(dve, key)[:, :].rearrange("p (a b) -> p a b", a=4)
                d = dst[:, 4 * hf:4 * hf + 4, tt * P:(tt + 1) * P]
                if scale is None:
                    drains(V.tensor_copy(d, ps), key)
                else:
                    drains(V.tensor_tensor(d, ps, spread(scale[:, 4 * hf:4 * hf + 4], P), ALU.mult), key)

            group = [0, 0]

            def mask_and_max(tag, mask):
                g, tt = group[0], tag[2]
                group[0] += 1
                nk = (tt + 1) * P
                if g >= 2:
                    dve.wait_ge(expd.sem, NH * (g - 1))
                s = sm[:, g % 2, :, 0:nk]
                for p in range(2):
                    ps = wait_filled(dve, tag + ("s", p))[:, 0:2 * nk].rearrange("p (a b) -> p a b", a=2)
                    drains(V.scalar_tensor_tensor(s[:, 2 * p:2 * p + 2, :], repeat(mask, 2), BIG, ps, ALU.mult, ALU.add),
                           tag + ("s", p))
                wait_drained(dve, tag + ("s", 1))
                wait_drained(dve, tag + ("s", 0))
                step(V.tensor_reduce(mx[:, g % 2, :], s, AX_X, ALU.max))
                rmax.fire(V.tensor_scalar(mx[:, g % 2, :], mx[:, g % 2, :], -(HD ** -0.5), None, ALU.mult))

            def row_coef():
                g = group[1]
                group[1] += 1
                dve.wait_ge(expd.sem, NH * (g + 1))
                inverse(coef[:, g % 2, :], sums[:, g % 2, :], 1e-30)
                return coef[:, g % 2, :]

            def heads(ap):
                return ap.rearrange("p (a b) -> p a b", a=NH)

            dve.wait_ge(const_loaded, 16)
            dve.wait_ge(small_loaded, SMALL)
            dve.wait_ge(zeroed, ZEROED)
            for l in range(LAYERS):
                dve.wait_ge(sumsq.sem, sumsq.at(l, TT))
                invert_mean_squares(D, EPS, stat[:, 0, :], stat[:, 1, :], invms)
                dve.wait_ge(rstd_s.sem, rstd_s.at(l, 1))
                for tt in range(TT):
                    normed.fire(V.tensor_scalar(hn[:, tt, :], x[:, tt, :], stat[:, 2, tt:tt + 1], None, ALU.mult))
                for tt in range(TT):
                    for hf in range(2):
                        copy_T((l, "hT", tt, hf), tt, hf, normw[:, l, :])
                drains(V.tensor_copy(peT[:, :], wait_filled(dve, (l, "peT"))[:, 0:32]), (l, "peT"))
                for tt in range(TT):
                    nk = (tt + 1) * P
                    for n in range(4):
                        wait_drained(dve, (l, "logit", tt, n))
                    step(V.tensor_scalar(score[:, 0, 0:nk], ncausal[:, tt, 0:nk], BIG, None, ALU.mult))
                    for h in range(8):
                        ins = V.scalar_tensor_tensor(score[:, 0, 0:nk], relu[:, h, 0:nk], ni[:, tt, 384 + h:385 + h],
                                                     score[:, 0, 0:nk], ALU.mult, ALU.add)
                        step(ins) if h < 7 else step_on(scored, ins)
                    for r in range(TOPK // 8):
                        src, dst = score[:, r % 2, 0:nk], score[:, 1 - r % 2, 0:nk]
                        step(V.max(top8[:, :], src))
                        step(V.match_replace(dst, top8[:, :], src, TAKEN))
                    step(V.scalar_tensor_tensor(amask[:, tt, 0:nk], score[:, 0, 0:nk], TAKEN, ncausal[:, tt, 0:nk],
                                                ALU.not_equal, ALU.max))
                wait_drained(dve, (l, "kcvc"))
                wait_drained(dve, (l, "peT"))
                kv = kvT[:, :].rearrange("p (n b) -> p b n", b=16)
                V.tensor_tensor(blk[:, 0:16, 0:NCMP], kv[:, :, 0:NCMP], spread(peT[:, 0:16], NCMP), ALU.add)
                blocks.fire(V.tensor_tensor(blk[:, 16:32, 0:NCMP], kv[:, :, 1:NCMP + 1], spread(peT[:, 16:32], NCMP), ALU.add))
                dve.wait_ge(gexp.sem, gexp.at(l, TT))
                step(V.tensor_scalar(gate[:, :, :], gate[:, :, :], 1.0, None, ALU.add))
                step(V.reciprocal(gate[:, :, :], gate[:, :, :]))
                wait_drained(dve, (l, "c_c"))
                ps = wait_filled(dve, (l, "c_x"))
                drain_step(V.tensor_tensor(cu[:, :, :], ccS[:, :, :], ps[:, :].rearrange("p (a b) -> p a b", a=2), ALU.mult),
                           (l, "c_x"))
                for j in range(2):
                    step(V.tensor_scalar(cy[:, j, :], cu[:, j, :], cw[:, l, 2, j:j + 1], None, ALU.mult))
                    for k in (1, 2):
                        ins = V.scalar_tensor_tensor(cy[:, j, k:T], cu[:, j, 0:T - k], cw[:, l, 2 - k, j:j + 1],
                                                     cy[:, j, k:T], ALU.mult, ALU.add)
                        conv_y.fire(ins) if (j, k) == (1, 2) else step(ins)
                for tt in range(TT):
                    ps = wait_filled(dve, (l, "cmp_s", tt))[:, 0:128].rearrange("p (a b) -> p a b", a=NH)
                    drain_step(V.scalar_tensor_tensor(smc[:, :, :], repeat(cinv[:, tt, :], NH), BIG, ps, ALU.mult, ALU.add),
                               (l, "cmp_s", tt))
                    step(V.tensor_reduce(cmx[:, :], smc[:, :, :], AX_X, ALU.max))
                    cmax.fire(V.tensor_tensor(smc[:, :, :], smc[:, :, :], spread(cmx[:, :], CP), ALU.subtract))
                    dve.wait_ge(cexp.sem, cexp.at(l, tt + 1))
                    step_on(cprob, V.tensor_tensor(ec[:, :, :], ec[:, :, :], repeat(cval[:, tt, :], NH), ALU.mult))
                    step(V.tensor_reduce(csum[:, :], ec[:, :, :], AX_X, ALU.add))
                    inverse(csum[:, :], csum[:, :], 1e-30)
                    step(V.tensor_tensor(csum[:, :], csum[:, :], gate[:, tt, 0:12:3], ALU.mult))
                    ps = wait_filled(dve, (l, "cmp_o", tt))
                    drains(V.tensor_tensor(shaped(ob[:, tt, 0, :], NH, HD), heads(ps[:, 0:256]), spread(csum[:, :], HD), ALU.mult),
                           (l, "cmp_o", tt))
                ps = wait_filled(dve, (l, "pool"))
                wait_drained(dve, (l, "d_g"))
                for j in range(2):
                    ins = V.scalar_tensor_tensor(mixT[:, 6 + j, :], ps[:, j * T:(j + 1) * T], psc[:, l, j:j + 1], dg[:, j, :],
                                                 ALU.mult, ALU.mult)
                drains(ins, (l, "pool"))
                groups = layer_groups(l)

                def mask_of(tag):
                    nk = (tag[2] + 1) * P
                    return (amask if tag[1] == "dsa" else ncausal)[:, tag[2], 0:nk]

                mask_and_max(groups[0], mask_of(groups[0]))
                for n, tag in enumerate(groups):
                    if n + 1 < len(groups):
                        mask_and_max(groups[n + 1], mask_of(groups[n + 1]))
                    _, branch, tt = tag
                    c = row_coef()
                    key = tag + ("o",)
                    if branch != "dsa":
                        step(V.tensor_tensor(c, c, gate[:, tt, (1 if branch == "slc" else 2):12:3], ALU.mult))
                    ps = wait_filled(dve, key)
                    to = {"slc": ob[:, tt, 1, :], "win": mixN[:, tt, 256:512], "dsa": mixN[:, tt, 0:256]}[branch]
                    drains(V.tensor_tensor(heads(to), heads(ps[:, 0:256]), spread(c, HD), ALU.mult), key)
                    if branch == "dsa":
                        wait_drained(dve, key)
                        wait_drained(dve, (l, "gates", tt))
                        dve.wait_ge(b_done.sem, b_done.at(l, tt + 1))
                        mixr.fire(V.tensor_tensor(mixN[:, tt, 0:256], mixN[:, tt, 0:256], gsil[:, tt, 0:256], ALU.mult))
                for tt in range(TT):
                    for hf in range(2):
                        ps = wait_filled(dve, (l, "wo", tt, hf))
                        r = x[:, tt, hf * 512:(hf + 1) * 512]
                        drains(V.tensor_tensor(r, r, ps[:, :], ALU.add), (l, "wo", tt, hf))
            dve.wait_ge(sumsq.sem, sumsq.at(LAYERS, TT))
            invert_mean_squares(D, EPS, stat[:, 0, :], stat[:, 1, :], invms)
            dve.wait_ge(rstd_s.sem, rstd_s.at(LAYERS, 1))
            dve.wait_ge(vec_loaded, 16)
            for tt in range(TT):
                h0_ready.fire(V.scalar_tensor_tensor(x[:, tt, :], x[:, tt, :], stat[:, 2, tt:tt + 1], vec[:, 0, :],
                                                     ALU.mult, ALU.mult))
            for tt in range(TT):
                for hf in range(2):
                    copy_T(("hT", tt, hf), tt, hf)
            dve.wait_ge(small2_loaded, SMALL2)
            coef_in.fire(V.tensor_tensor(b16[0:16, 2:3], b16[0:16, 0:1], C("sgn", rows=16), ALU.mult))
            dve.wait_ge(dt_exp.sem, 2)
            R = [dtf[0:16, r, :] for r in range(8)]
            step_on(dt_w, V.tensor_scalar(R[2], R[1], 1.0, None, ALU.add))
            step(V.tensor_scalar(R[3], R[2], 1.0, None, ALU.subtract))
            step(V.tensor_scalar(R[7], R[3], 0.0, None, ALU.is_equal))
            inverse(R[3], R[3], TINY)
            dve.wait_ge(dt_ln.sem, 1)
            step(V.tensor_tensor(R[4], R[4], R[3], ALU.mult))
            step(V.tensor_tensor(R[4], R[4], R[7], ALU.add))
            step(V.tensor_tensor(R[4], R[4], R[1], ALU.mult))
            step(V.scalar_tensor_tensor(R[4], R[0], 0.0, R[4], ALU.max, ALU.add))
            step(V.memset(R[2], 1.0))
            step(V.tensor_scalar(R[3], R[4], b16[0:16, 3:4], -1.0, ALU.mult, ALU.mult))
            step_on(cum_ready, V.tensor_tensor_scan(R[5], R[2], R[3], 0.0, ALU.mult, ALU.add))
            cum_ready.fire(V.tensor_scalar(R[6], R[5], -8.0, None, ALU.mult))
            for n in range(8):
                if n % 2 == 0:
                    wait_drained(dve, ("xbc", n // 2))
                step(V.tensor_scalar(xc[:, n, :], xbc[:, n, :], cw2[:, 3, n:n + 1], cb2[:, n:n + 1], ALU.mult, ALU.add))
                for k in (1, 2, 3):
                    ins = V.scalar_tensor_tensor(xc[:, n, k:T], xbc[:, n, 0:T - k], cw2[:, 3 - k, n:n + 1],
                                                 xc[:, n, k:T], ALU.mult, ALU.add)
                    conv2.fire(ins) if k == 3 else step(ins)
            dve.wait_ge(brow_loaded, 32)
            for tt in range(TT):
                ps = wait_filled(dve, ("z", tt))
                drains(V.tensor_tensor(z2[:, tt, :], ps[:, :], brow[:, 0:512], ALU.add), ("z", tt))
            for tt in range(TT):
                ps = wait_filled(dve, ("v", tt))
                drains(V.tensor_tensor(v2[:, tt, :], ps[:, :], brow[:, 512:1024], ALU.add), ("v", tt))
            drain_step(V.tensor_copy(dA[:, :, :], wait_filled(dve, ("tA",))[:, 0:64].rearrange("p (a b) -> p a b", a=4)), ("tA",))
            for g in range(2):
                ps = wait_filled(dve, ("cb", g))
                drains(V.tensor_tensor(cbm[:, g, :], ps[:, 0:384], C("ltri"), ALU.mult), ("cb", g))

            def finish2(tag):
                _, half, tt = tag
                c = row_coef()
                ps = wait_filled(dve, tag + ("o",))
                drains(V.tensor_tensor(heads(merged[:, tt, 512 + 256 * half:768 + 256 * half]), heads(ps[:, 0:256]),
                                       spread(c, HD), ALU.mult), tag + ("o",))

            for h in range(SH):
                ps = wait_filled(dve, ("Ab", h))
                if h >= 2:
                    dve.wait_ge(decay.sem, h - 1)
                V.tensor_scalar(seg[:, h % 2, 0:T], ps[:, 0:T], dA[:, 1, h:h + 1], 0.0, ALU.subtract, ALU.min)
                drains(V.tensor_scalar(seg[:, h % 2, T:T + P], ps[:, P:T], dA[:, 3, h:h + 1], 0.0, ALU.subtract, ALU.min),
                       ("Ab", h))
                if h % 2:
                    tag = GROUPS2[h // 2]
                    mask_and_max(tag, ncausal[:, tag[2], 0:(tag[2] + 1) * P])
                    if h > 1:
                        finish2(GROUPS2[h // 2 - 1])
            finish2(GROUPS2[-1])
            dve.wait_ge(xdt_ready.sem, 2)
            for tt in range(TT):
                ps = wait_filled(dve, ("y", tt))
                drain_step(V.tensor_tensor(merged[:, tt, 0:512], ps[:, :], xsN[:, tt, :], ALU.add), ("y", tt))
                dve.wait_ge(z_ready.sem, tt + 1)
                yz.fire(V.tensor_tensor(merged[:, tt, 0:512], merged[:, tt, 0:512], z2[:, tt, :], ALU.mult))
            dve.wait_ge(ysq.sem, 4)
            invert_mean_squares(256, 1e-5, rv[:, 0:4, 0], rv[:, 4:8, 0], yinv)
            dve.wait_ge(yrstd.sem, 1)
            for tt in range(TT):
                for g in range(2):
                    m = merged[:, tt, g * 256:(g + 1) * 256]
                    ins = V.tensor_scalar(m, m, rv[:, 8 + 2 * tt + g, 0:1], None, ALU.mult)
                merged_ready.fire(ins)
            for tt in range(TT):
                for hf in range(2):
                    copy_T(("mT", tt, hf), tt, hf, g8, mixT)

            def layer_norm(tt, residual, loaded, done):
                for hf in range(2):
                    residual(hf)
                s = coef2[:, :, tt:tt + 1]
                step(V.tensor_reduce(s[:, 0, :], x[:, tt, :], AX_X, ALU.add))
                step_on(ln_mu, V.tensor_scalar(s[:, 0, :], s[:, 0, :], -1.0 / D, None, ALU.mult))
                dve.wait_ge(ln_sq.sem, ln_mu.n)
                invert_mean_squares(D, 1e-5, s[:, 1, :], s[:, 2, :], ln_inv)
                dve.wait_ge(ln_rstd.sem, ln_mu.n)
                step(V.tensor_scalar(x[:, tt, :], x[:, tt, :], s[:, 0, :], s[:, 3, :], ALU.add, ALU.mult))
                dve.wait_ge(vec_loaded, loaded)
                step(V.tensor_tensor(x[:, tt, :], x[:, tt, :], vec[:, 0, :], ALU.mult))
                done.fire(V.tensor_tensor(x[:, tt, :], x[:, tt, :], vec[:, 1, :], ALU.add))

            def residual1(tt):
                def one(hf):
                    r = x[:, tt, hf * 512:(hf + 1) * 512]
                    ps = wait_filled(dve, ("wo", tt, hf))
                    drain_step(V.scalar_tensor_tensor(r, r, ALPHA, ps[:, :], ALU.mult, ALU.add), ("wo", tt, hf))
                return one

            for tt in range(TT):
                layer_norm(tt, residual1(tt), 16 * 3, h1_ready)
            for tt in range(TT):
                for hf in range(2):
                    copy_T(("h1T", tt, hf), tt, hf)
            for tt in range(TT):
                ps = wait_filled(dve, ("route", tt))
                drain_step(V.tensor_tensor(rl[:, tt, :], ps[:, 0:20], rb[:, :], ALU.add), ("route", tt))
            S = [rs[:, r, :, :] for r in range(12)]
            U = [rv[:, r, :] for r in range(12)]
            rank = C("rank")

            def first_of(dst, hit, m):
                step(V.tensor_tensor(dst, hit, repeat(rank, TT), ALU.mult))
                step(V.tensor_reduce(m, dst, AX_X, ALU.max))
                step(V.tensor_tensor(dst, dst, spread(m, 4), ALU.is_equal))

            step(V.tensor_reduce(U[0], rl[:, :, 0:4], AX_X, ALU.max))
            step_on(r_in, V.tensor_tensor(S[0], rl[:, :, 0:4], spread(U[0], 4), ALU.subtract))
            step(V.tensor_scalar(S[2], S[0], 0.0, None, ALU.is_equal))
            first_of(S[2], S[2], U[1])
            dve.wait_ge(r_exp.sem, 1)
            step(V.tensor_reduce(U[2], S[1], AX_X, ALU.add))
            step(V.reciprocal(U[2], U[2]))
            for g in range(4):
                dst = S[3] if g == 0 else S[10]
                step(V.tensor_tensor(dst, rl[:, :, 4 + 4 * g:8 + 4 * g], spread(S[2][:, :, g], 4), ALU.mult))
                if g:
                    step(V.tensor_tensor(S[3], S[3], S[10], ALU.add))
            step(V.tensor_reduce(U[3], S[3], AX_X, ALU.max))
            step_on(r_in, V.tensor_tensor(S[4], S[3], spread(U[3], 4), ALU.subtract))
            step(V.tensor_scalar(S[6], S[4], 0.0, None, ALU.is_equal))
            first_of(S[6], S[6], U[4])
            step(V.tensor_scalar(S[7], S[6], BIG, None, ALU.mult))
            step(V.tensor_tensor(S[7], S[7], S[4], ALU.add))
            step(V.tensor_reduce(U[5], S[7], AX_X, ALU.max))
            step(V.tensor_tensor(S[8], S[7], spread(U[5], 4), ALU.is_equal))
            first_of(S[8], S[8], U[6])
            step(V.tensor_tensor(S[8], S[8], S[6], ALU.add))
            dve.wait_ge(r_exp.sem, 2)
            step(V.tensor_tensor(S[9], S[5], S[8], ALU.mult))
            step(V.tensor_reduce(U[7], S[9], AX_X, ALU.add))
            step(V.reciprocal(U[7], U[7]))
            step(V.tensor_tensor(U[7], U[7], U[2], ALU.mult))
            step(V.tensor_tensor(S[9], S[9], spread(U[7], 4), ALU.mult))
            for g in range(4):
                ins = V.tensor_tensor(comb[:, :, 4 * g:4 * g + 4], S[9], spread(S[2][:, :, g], 4), ALU.mult)
            comb_ready.fire(ins)
            drains(V.tensor_copy(combT[0:16, :], wait_filled(dve, ("combT",))[0:16, 0:T]), ("combT",))
            for n in range(EXPERTS // 2):
                ps = wait_filled(dve, ("comb", n))
                drains(V.tensor_copy(combB[:, 2 * n:2 * n + 2, :], ps[:, :].rearrange("p (a b) -> p a b", a=2)), ("comb", n))
            for n in range(EXPERTS // 2):
                wait_drained(dve, ("comb", n))
            for e in range(EXPERTS):
                for hf in range(2):
                    b = 6 + hf
                    dve.wait_ge(drained[b - 2], used[b - 2] + e + 1)
                    dve.wait_ge(filled[b], used[b] + e + 1)
                    V.tensor_tensor(act_u[:, hf, :, :], silu_g[:, hf, :, :], psum[b][:, :].rearrange("p (a b) -> p a b", a=2),
                                    ALU.mult).then_inc(drained[b], 1)
                    dve.wait_ge(drained[b], used[b] + e + 1)
                    if e >= 2 and hf == 0:
                        dve.wait_ge(filled[3], used[3] + e - 1)
                    ins = V.tensor_tensor(actT[:, e % 2, 2 * hf:2 * hf + 2, :], act_u[:, hf, :, :],
                                          repeat(combB[:, e, :], 2), ALU.mult)
                act_ready.fire(ins)

            def residual2(tt):
                def one(hf):
                    r = x[:, tt, hf * 512:(hf + 1) * 512]
                    step(V.scalar_tensor_tensor(r, r, ALPHA, psum[2 * tt + hf][:, :], ALU.mult, ALU.add))
                return one

            dve.wait_ge(filled[3], used[3] + EXPERTS)
            for tt in range(TT):
                layer_norm(tt, residual2(tt), 16 * 5, final_ready)

        @block.scalar
        def _(act):
            def step(ins):
                astep.fire(ins)
                act.wait_ge(astep.sem, astep.n)

            def run(out_, in_, func=ACT.Copy, **kw):
                return nc.scalar.activation(out_, in_, func, **kw)

            act.dma_start(cst[:, :], a["shape_constants"][:, :]).then_inc(const_loaded, 16)
            small_dmas[0](act)

            def load_cmp(l):
                for n, name in enumerate(("w_cmp_k", "w_cmp_v")):
                    act.dma_start(pe2[0:32, n, :], a["pe_cmp"][l]).then_inc(cmp_loaded, 16)
                    act.dma_start(wcmp[n * HD:(n + 1) * HD, :, :], a[name][l].rearrange("(k d) e -> d k e", d=HD))\
                       .then_inc(cmp_loaded, 16)

            load_cmp(0)
            small_dmas[1](act)

            def root_of_mean_squares():
                for tt in range(TT):
                    sumsq.fire(run(hn[:, tt, :], x[:, tt, :], ACT.Square, accum_out=stat[:, 0, tt:tt + 1]))
                act.wait_ge(invms.sem, invms.n)
                rstd_s.fire(run(stat[:, 2, :], stat[:, 1, :], ACT.Sqrt))

            def halves(dst, ps, key, **kw):
                for j in range(2):
                    r = slice(j * HD, (j + 1) * HD)
                    ins = run(dst(j), ps[r], **kw)
                return ins

            group = [0]

            def exps(tag):
                g, tt = group[0], tag[2]
                group[0] += 1
                nk = (tt + 1) * P
                act.wait_ge(rmax.sem, g + 1)
                if g >= 2:
                    wait_filled(act, prev_groups[g - 2] + ("pT", prev_groups[g - 2][2]))
                for h in range(NH):
                    expd.fire(run(ex[:, g % 2, h, 0:nk], sm[:, g % 2, h, 0:nk], ACT.Exp, bias=mx[:, g % 2, h:h + 1],
                                  scale=HD ** -0.5, accum_out=sums[:, g % 2, h:h + 1]))

            prev_groups = [t for l in range(LAYERS) for t in layer_groups(l)] + GROUPS2
            gdone = [0]

            def evacuate_probs(tag):
                g = gdone[0]
                gdone[0] += 1
                if g >= 2:
                    wait_filled(act, prev_groups[g - 2] + ("o",))
                for kt in range(tag[2] + 1):
                    key = tag + ("pT", kt)
                    drains(run(exT[:, g % 2, kt, :], wait_filled(act, key)[:, :]), key)

            act.wait_ge(zeroed, ZEROED)
            for l in range(LAYERS + 1):
                if l == 0:
                    act.wait_ge(x_loaded, 16 * TT)
                else:
                    for tt in range(TT):
                        for hf in range(2):
                            wait_drained(act, (l - 1, "wo", tt, hf))
                for tt in range(TT):
                    sumsq.fire(run(hn[:, tt, :], x[:, tt, :], ACT.Square, accum_out=stat[:, 0, tt:tt + 1]))
                act.wait_ge(invms.sem, l + 1)
                rstd_s.fire(run(stat[:, 2, :], stat[:, 1, :], ACT.Sqrt))
                if l == LAYERS:
                    break
                for tt in range(TT):
                    key = (l, "idx", tt)
                    ps = wait_filled(act, key)
                    run(ni[:, tt, 0:256], ps[:, 0:256])
                    run(shaped(ni[:, tt, 256:384], 4, 32), repeat(ps[:, 256:288], 4))
                    drains(run(ni[:, tt, 384:392], ps[:, 288:296], scale=1.0 / 16.0), key)
                for tt in range(TT):
                    key = (l, "qkv", tt)
                    ps = wait_filled(act, key)
                    run(na[:, tt, 0:256], ps[:, 0:256])
                    run(shaped(na[:, tt, 256:384], 2, HD), repeat(ps[:, 256:320], 2))
                    drains(run(na[:, tt, 384:448], ps[:, 320:384]), key)
                for tt in range(TT):
                    key = (l, "idxT", tt)
                    ps = wait_filled(act, key)
                    tok = slice(tt * P, (tt + 1) * P)
                    run(qiT[:, :, tok], ps[:, 0:256].rearrange("p (a b) -> p a b", a=2))
                    for j in range(4):
                        r = slice(32 * j, 32 * j + 32)
                        ins = run(kiT[r, j, tok], ps[r, 256:384])
                    drains(ins, key)
                for tt in range(TT):
                    nk = (tt + 1) * P
                    if tt:
                        act.wait_ge(scored.sem, scored.at(l, tt))
                    for n in range(4):
                        key = (l, "logit", tt, n)
                        ps = wait_filled(act, key)
                        drains(run(relu[:, 2 * n:2 * n + 2, 0:nk], ps[:, 0:2 * nk].rearrange("p (a b) -> p a b", a=2), ACT.Relu),
                               key)
                for tt in range(TT):
                    key = (l, "bq", tt)
                    drains(run(nb[:, tt, 0:256], wait_filled(act, key)[:, 0:256]), key)
                drains(run(kvT[:, :], wait_filled(act, (l, "kcvc"))[:, 0:T]), (l, "kcvc"))
                for tt in range(TT):
                    key = (l, "bkv", tt)
                    ps = wait_filled(act, key)
                    run(shaped(nb[:, tt, 256:384], 2, HD), repeat(ps[:, 0:64], 2))
                    run(nb[:, tt, 512:576], ps[:, 64:128])
                    run(shaped(nb[:, tt, 384:512], 2, HD), repeat(ps[:, 128:192], 2))
                    drains(run(nb[:, tt, 576:652], ps[:, 192:268]), key)
                for tt in range(TT):
                    key = (l, "qkT_a", tt)
                    ps = wait_filled(act, key)
                    tok = slice(tt * P, (tt + 1) * P)
                    run(qaT[:, :, tok], ps[:, 0:256].rearrange("p (a b) -> p a b", a=2))
                    for j in range(2):
                        r = slice(HD * j, HD * j + HD)
                        ins = run(kaT[r, j, tok], ps[r, 256:384])
                    drains(ins, key)
                for tt in range(TT):
                    key = (l, "gates", tt)
                    drains(run(gsil[:, tt, :], wait_filled(act, key)[:, :], ACT.Silu), key)
                for tt in range(TT):
                    key = (l, "qkT_b", tt)
                    ps = wait_filled(act, key)
                    tok = slice(tt * P, (tt + 1) * P)
                    run(qbT[:, :, tok], ps[:, 0:256].rearrange("p (a b) -> p a b", a=2))
                    for m, dst in enumerate((ksT, kwT)):
                        for j in range(2):
                            r = slice(HD * j, HD * j + HD)
                            ins = run(dst[r, j, tok], ps[r, (2 + m) * P:(3 + m) * P])
                    drains(ins, key)
                ps = wait_filled(act, (l, "kcmp"))
                drains(run(shaped(kcN[0:CP, :], 2, HD), repeat(ps[0:CP, 0:HD], 2)), (l, "kcmp"))
                ps = wait_filled(act, (l, "vcmp"))
                for h in range(NH):
                    ins = run(vcB[CP * h:CP * h + CP, h, :], ps[0:CP, 0:HD])
                drains(ins, (l, "vcmp"))
                for name, dst, func in (("c_b", cbS, ACT.Copy), ("c_c", ccS, ACT.Copy), ("c_g", cgS, ACT.Silu),
                                        ("d_u", du[:, :, 16:], ACT.Copy), ("d_g", dg, ACT.Silu)):
                    ps = wait_filled(act, (l, name))
                    drains(run(dst[:, :, :], ps[:, :].rearrange("p (a b) -> p a b", a=2), func), (l, name))
                for tt in range(TT):
                    wait_drained(act, (l, "bkv", tt))
                    gexp.fire(run(gate[:, tt, :], nb[:, tt, 640:652], ACT.Exp, scale=-1.0))
                ps = wait_filled(act, (l, "kcT"))
                for j in range(2):
                    r = slice(HD * j, HD * j + HD)
                    ins = run(kcT[r, j, :], ps[r, 0:CP])
                drains(ins, (l, "kcT"))
                for tt in range(TT):
                    act.wait_ge(cmax.sem, cmax.at(l, tt + 1))
                    if tt:
                        wait_filled(act, (l, "cmp_pT", tt - 1))
                    cexp.fire(run(ec[:, :, :], smc[:, :, :], ACT.Exp, scale=HD ** -0.5))
                    drains(run(pcT[:, :], wait_filled(act, (l, "cmp_pT", tt))[:, 0:P]), (l, "cmp_pT", tt))
                act.wait_ge(conv_done.sem, conv_done.at(l, 1))
                for tag in layer_groups(l):
                    exps(tag)
                    evacuate_probs(tag)
                if l + 1 < LAYERS:
                    load_cmp(l + 1)
                else:
                    act.dma_start(vec[:, 0, :], row("final_norm_w").broadcast_to([P, D])).then_inc(vec_loaded, 16)
                act.wait_ge(b_done.sem, b_done.at(l, TT))
                for tt in range(TT):
                    key = (l, "mixT", tt)
                    ps = wait_filled(act, key)
                    drains(run(mixT[:, 0:4, tt * P:(tt + 1) * P], ps[:, :].rearrange("p (a b) -> p a b", a=4)), key)
            act.wait_ge(small2_loaded, SMALL2)
            act.wait_ge(coef_in.sem, 1)
            ps = wait_filled(act, ("dtf",))
            drains(run(dtf[0:16, 0, :], ps[0:16, 0:T], ACT.Identity, scale=C("sgn", rows=16), bias=b16[0:16, 2:3]), ("dtf",))
            wait_drained(act, ("dtf",))
            step(run(dtf[0:16, 1, :], dtf[0:16, 0, :], ACT.Abs))
            dt_exp.fire(run(dtf[0:16, 1, :], dtf[0:16, 1, :], ACT.Exp, scale=-1.0))
            dt_exp.fire(run(b16[0:16, 3:4], b16[0:16, 1:2], ACT.Exp))
            for n in range(4):
                ps = wait_filled(act, ("xbc", n))
                for j in range(2):
                    ins = run(xbc[:, 2 * n + j, :], ps[:, j * T:(j + 1) * T], ACT.Identity, bias=bx[:, 2 * n + j:2 * n + j + 1])
                drains(ins, ("xbc", n))
            act.wait_ge(dt_w.sem, 1)
            dt_ln.fire(run(dtf[0:16, 4, :], dtf[0:16, 2, :], ACT.Ln))
            for n in range(2):
                ps = wait_filled(act, ("q", n))
                for j in range(2):
                    ins = run(qT2[:, 2 * n + j, :], ps[:, j * T:(j + 1) * T], ACT.Identity, bias=bqk[:, 2 * n + j:2 * n + j + 1])
                drains(ins, ("q", n))
            act.wait_ge(k2_zeroed.sem, 1)
            for n in range(2):
                ps = wait_filled(act, ("k", n))
                for j in range(2):
                    for i in range(2):
                        r = slice(HD * i, HD * i + HD)
                        c = 4 + 2 * n + j
                        ins = run(kT2[r, 2 * n + j, i, :], ps[r, j * T:(j + 1) * T], ACT.Identity, bias=bqk[r, c:c + 1])
                drains(ins, ("k", n))
            for n in range(8):
                act.wait_ge(conv2.sem, n + 1)
                act2.fire(run(xc[:, n, :], xc[:, n, :], ACT.Silu))
            for tt in range(TT):
                wait_drained(act, ("z", tt))
                z_ready.fire(run(z2[:, tt, :], z2[:, tt, :], ACT.Silu))
            for tt in range(TT):
                drains(run(xsN[:, tt, :], wait_filled(act, ("xs", tt))[:, :]), ("xs", tt))
            for h in range(SH):
                wait_drained(act, ("Ab", h))
                dec_e.fire(run(seg[:, h % 2, :], seg[:, h % 2, :], ACT.Exp))
                if h % 2:
                    if h > 1:
                        evacuate_probs(GROUPS2[h // 2 - 1])
                    exps(GROUPS2[h // 2])
            evacuate_probs(GROUPS2[-1])
            for n, name in enumerate(("ln1_g_2", "ln1_b_2")):
                act.dma_start(vec[:, n, :], a[name].broadcast_to([P, D])).then_inc(vec_loaded, 16)
            for tt in range(TT):
                act.wait_ge(yz.sem, tt + 1)
                for g in range(2):
                    ysq.fire(run(xc[:, 2 * tt + g, :], merged[:, tt, g * 256:(g + 1) * 256],
                                 ACT.Square, accum_out=rv[:, 2 * tt + g, 0:1]))
            act.wait_ge(yinv.sem, 1)
            yrstd.fire(run(rv[:, 8:12, 0], rv[:, 4:8, 0], ACT.Sqrt))

            def layer_norm(tt, n):
                act.wait_ge(ln_mu.sem, n)
                ln_sq.fire(run(hn[:, tt, :], x[:, tt, :], ACT.Square, bias=coef2[:, 0, tt:tt + 1],
                               accum_out=coef2[:, 1, tt:tt + 1]))
                act.wait_ge(ln_inv.sem, n)
                ln_rstd.fire(run(coef2[:, 3, tt:tt + 1], coef2[:, 2, tt:tt + 1], ACT.Sqrt))

            for tt in range(TT):
                layer_norm(tt, tt + 1)
            act.wait_ge(h1_ready.sem, TT)
            for n, name in enumerate(("ln2_g_2", "ln2_b_2")):
                act.dma_start(vec[:, n, :], a[name].broadcast_to([P, D])).then_inc(vec_loaded, 16)
            for n in range(2):
                act.wait_ge(r_in.sem, n + 1)
                r_exp.fire(run(rs[:, 1 + 4 * n, :, :], rs[:, 4 * n, :, :], ACT.Exp))
            for e in range(EXPERTS):
                for hf in range(2):
                    b = 4 + hf
                    act.wait_ge(filled[b], used[b] + e + 1)
                    if e:
                        act.wait_ge(drained[b + 2], used[b + 2] + e)
                    run(silu_g[:, hf, :, :], psum[b][:, :].rearrange("p (a b) -> p a b", a=2), ACT.Silu)\
                        .then_inc(drained[b], 1)
            for tt in range(TT):
                layer_norm(tt, TT + tt + 1)

        @block.gpsimd
        def _(pool):
            G = nc.gpsimd

            def step(ins):
                gstep.fire(ins)
                pool.wait_ge(gstep.sem, gstep.n)

            def rope(buf, n, half, cos, sin, signal):
                rows = buf.shape[0]
                t1, t2 = (shaped(rt[0:rows, k, :], n, 2 * half) for k in range(2))
                w = buf[:, :, 0:2 * half]
                G.tensor_tensor(t1, w, repeat(cos, n), ALU.mult)
                step(G.tensor_tensor(t2, w, repeat(sin, n), ALU.mult))
                G.tensor_tensor(w[:, :, 0:half], t1[:, :, 0:half], t2[:, :, half:2 * half], ALU.add)
                signal.fire(G.tensor_tensor(w[:, :, half:2 * half], t1[:, :, half:2 * half], t2[:, :, 0:half], ALU.add))
                pool.wait_ge(signal.sem, signal.n)

            zero_list = (zero[:, :], kiT, kaT, ksT, kwT, blk, vcB, kcT, du, b16, pw[:, :, :, :], pe2, kcN, dtf[:, 7:8, 0:1])
            assert len(zero_list) == ZEROED
            for v in zero_list:
                pool.memset(v, 0.0).then_inc(zeroed, 1)
            pool.wait_ge(zeroed, ZEROED)
            pool.memset(g8[:, 4:8], 1.0).then_inc(g8_ones.sem, 1)
            pool.wait_ge(const_loaded, 16)
            for l in range(LAYERS):
                for tt in range(TT):
                    wait_drained(pool, (l, "idx", tt))
                    rope(shaped(ni[:, tt, 0:384], 12, 32), 12, 4, cos32[:, tt, :], sin32[:, tt, :], roped_i)
                for tt in range(TT):
                    wait_drained(pool, (l, "qkv", tt))
                    rope(shaped(na[:, tt, 0:384], 6, HD), 6, 8, cos64[:, tt, :], sin64[:, tt, :], roped_a)
                for tt in range(TT):
                    wait_drained(pool, (l, "bq", tt))
                    wait_drained(pool, (l, "bkv", tt))
                    rope(shaped(nb[:, tt, 0:512], 8, HD), 8, 8, cos64[:, tt, :], sin64[:, tt, :], roped_b)
                wait_drained(pool, (l, "kcmp"))
                rope(shaped(kcN[0:CP, :], 2, HD), 2, 8, C("cosc", rows=CP), C("sinc", rows=CP), roped_c)
                wait_drained(pool, (l, "d_u"))
                pool.wait_ge(scored.sem, scored.at(l, TT))
                E = T + 16
                step(G.tensor_tensor(d2[:, :, 1:E], du[:, :, 1:E], du[:, :, 0:E - 1], ALU.add))
                step(G.tensor_tensor(d4[:, :, 4:E], d2[:, :, 4:E], d2[:, :, 2:E - 2], ALU.add))
                step(G.tensor_tensor(d2[:, 1, 8:E], d4[:, 1, 8:E], d4[:, 1, 4:E - 4], ALU.add))
                step(G.tensor_tensor(d4[HD:P, 1, 16:E], d2[HD:P, 1, 16:E], d2[HD:P, 1, 8:E - 8], ALU.add))
                dp = mixT[:, 6:8, :]
                G.tensor_tensor(dp[0:HD], d2[0:HD, :, 16:E], icnt[0:HD], ALU.mult)
                step(G.tensor_tensor(dp[HD:P], d4[HD:P, :, 16:E], icnt[HD:P], ALU.mult))
                pooled.fire(G.tensor_tensor(dp, dp, du[:, :, 16:E], ALU.subtract))
                pool.wait_ge(conv_y.sem, conv_y.at(l, 1))
                wait_drained(pool, (l, "c_b"))
                wait_drained(pool, (l, "c_g"))
                step(G.tensor_tensor(cy, cy, cbS, ALU.mult))
                conv_done.fire(G.tensor_tensor(cy, cy, cgS, ALU.mult))
                for tt in range(TT):
                    wait_drained(pool, (l, "win", tt, "o"))
                    m = mixN[:, tt, 256:512]
                    step(G.tensor_tensor(m, m, ob[:, tt, 0, :], ALU.add))
                    step(G.tensor_tensor(m, m, ob[:, tt, 1, :], ALU.add))
                    b_done.fire(G.tensor_tensor(m, m, gsil[:, tt, 256:512], ALU.mult))
            pool.wait_ge(h0_ready.sem, TT)
            for n, c in enumerate((Z2, V2)):
                pool.dma_start(brow[:, n * 512:(n + 1) * 512], a["b_in_2"][:, c:c + 512].broadcast_to([P, 512]))\
                    .then_inc(brow_loaded, 16)
            k2_zeroed.fire(G.memset(kT2, 0.0))
            wait_drained(pool, ("tA",))
            for tt in range(TT):
                wait_drained(pool, ("xs", tt))
                ins = G.tensor_tensor(shaped(xdt[:, tt, :], SH, HD), shaped(xsN[:, tt, :], SH, HD),
                                      spread(dA[:, 2 * tt, 0:SH], HD), ALU.mult)
            xdt_ready.fire(ins)
            pool.wait_ge(xdt_ready.sem, 1)
            for tt in range(TT):
                v = shaped(xsN[:, tt, :], SH, HD)
                ins = G.tensor_tensor(v, v, spread(dsk, HD), ALU.mult)
            xdt_ready.fire(ins)
            for g in range(2):
                wait_drained(pool, ("cb", g))
            for h in range(SH):
                pool.wait_ge(dec_e.sem, h + 1)
                if h >= 2:
                    pool.wait_ge(y_used.sem, h - 1)
                decay.fire(G.tensor_tensor(mTh[:, h % 2, :], seg[:, h % 2, :], cbm[:, h // 4, :], ALU.mult))


_INPUTS = ["x", "norm_w", "w_in", "w_out", "conv_w", "pe_cmp", "w_cmp_k", "w_cmp_v", "pool_w", "pool_scale", "final_norm_w",
           "w_in_2", "b_in_2", "conv_w_2", "conv_b_2", "a_log_2", "d_skip_2", "ssd_norm_g_2", "w_out_2", "ln1_g_2",
           "ln1_b_2", "router_group_w_2", "router_group_b_2", "router_expert_w_2", "router_expert_b_2", "w_gate_2",
           "w_up_2", "w_down_2", "ln2_g_2", "ln2_b_2"]


def kernel(**inputs):
    import concourse.bacc as bacc
    from concourse.bass_utils import run_bass_kernel_spmd

    nc = bacc.Bacc("TRN2", target_bir_lowering=False, num_devices=1)
    arrays = {n: np.ascontiguousarray(inputs[n]) for n in _INPUTS}
    arrays["shape_constants"] = shape_constants()
    feeds, aps = {}, {}
    for n, v in arrays.items():
        feeds[f"in_{n}"] = v
        aps[n] = nc.dram_tensor(f"in_{n}", v.shape, mybir.dt.from_np(v.dtype), kind="ExternalInput").ap()
    out = nc.dram_tensor("out", (1, T, D), F32, kind="ExternalOutput").ap()
    build(nc, aps, out)
    r = run_bass_kernel_spmd(nc, [feeds], core_ids=[0])
    return r.results[0]["out"]
```

```python
from contextlib import ExitStack

import concourse.bass as bass
import concourse.mybir as mybir
import numpy as np

F32 = mybir.dt.float32
ALU = mybir.AluOpType
ACT = mybir.ActivationFunctionType
AX_X = mybir.AxisListType.X

P = 128
T = 256
TT = T // P
D = 1024
KT = D // P
LAYERS = 2
EPS = 1e-6
HD = 64
NH = 4
TOPK = 64
NCMP = 15
CP = 32
BIG = -1.0e30
TAKEN = -3.0e38
TINY = 1.0e-38
ROPE_THETA = 500000.0

A_Q, A_QI, A_GATE = 0, 384, 680
B_Q, B_KS, B_GATE = 936, 1320, 1588
C_B, C_X, D_U = 1844, 2356, 2868
Z2, XBC2, DT2, Q2, K2, V2, F2 = 0, 512, 1536, 1544, 2056, 2568, 3080
SH = 8
ALPHA = 2.0 ** 0.25
EXPERTS, GROUPS, FF = 16, 4, 512
GE = EXPERTS // GROUPS
FT = FF // P
SLOTS = 6
SLOT = KT * 512
ZEROED = 14
SMALL = 16 * 14
SMALL2 = 16 * 21
ARENA = 12584

CONST = {}
CONST_W = 0
for _name, _w in (("ident", 128), ("ncausal", 512), ("cos64", 32), ("sin64", 32), ("cos32", 16), ("sin32", 16),
                  ("cosc", 16), ("sinc", 16), ("cinv", 64), ("cval", 64), ("icnt", 512), ("ltri", 384),
                  ("sgn", 1), ("rank", 4), ("iota", 128)):
    CONST[_name] = (CONST_W, _w)
    CONST_W += _w


def shape_constants():
    c = np.zeros((P, CONST_W), np.float32)

    def put(name, a, rows=P):
        o, w = CONST[name]
        c[:rows, o:o + w] = np.asarray(a, np.float32).reshape(rows, w)

    p = np.arange(P)
    t = np.arange(TT)[None, :] * P + p[:, None]
    put("ident", np.eye(P))
    put("ncausal", np.arange(T)[None, None, :] > t[:, :, None])

    def angles(pos, half):
        inv = (np.float32(ROPE_THETA) ** (-np.arange(half, dtype=np.float32) / np.float32(half))).astype(np.float32)
        a = pos.astype(np.float32)[..., None] * inv
        return np.concatenate([np.cos(a), np.cos(a)], -1), np.concatenate([np.sin(a), -np.sin(a)], -1)

    for half, name in ((8, "64"), (4, "32")):
        co, si = angles(t, half)
        put("cos" + name, co)
        put("sin" + name, si)
    n = np.arange(CP)
    co, si = angles(16 * n + 31, 8)
    put("cosc", co, CP)
    put("sinc", si, CP)
    inv = (16 * n + 31)[None, None, :] > t[:, :, None]
    inv |= (n >= NCMP)[None, None, :]
    put("cinv", inv)
    put("cval", ~inv)
    win = np.array([[2, 8], [4, 16]])[p // 64]
    put("icnt", 1.0 / np.minimum(np.arange(T)[None, None, :] + 1, win[:, :, None]))
    put("ltri", np.concatenate([p[:, None] <= np.arange(T)[None, :], p[:, None] <= p[None, :]], 1))
    put("sgn", np.where(p < SH, 1.0, -1.0))
    put("rank", np.broadcast_to([4.0, 3.0, 2.0, 1.0], (P, 4)))
    put("iota", np.broadcast_to(np.arange(P), (P, P)))
    return c


def psum_plan():
    plan, order, used, turn = {}, [], [0] * 8, {}

    def job(key, banks=tuple(range(8))):
        b = banks[turn.get(banks, 0) % len(banks)]
        turn[banks] = turn.get(banks, 0) + 1
        plan[key] = (b, used[b])
        used[b] += 1
        order.append(key)

    def scores(tag, banks=tuple(range(8))):
        for p in range(2):
            job(tag + ("s", p), banks)

    def outputs(tag, banks=tuple(range(8))):
        for kt in range(tag[2] + 1):
            job(tag + ("pT", kt), banks)
        job(tag + ("o",), banks)

    for l in range(LAYERS):
        for tt in range(TT):
            for hf in range(2):
                job((l, "hT", tt, hf))
        job((l, "peT"))
        for name in ("idx", "qkv"):
            for tt in range(TT):
                job((l, name, tt))
        for tt in range(TT):
            job((l, "idxT", tt))
        for tt in range(TT):
            for n in range(4):
                job((l, "logit", tt, n))
        for tt in range(TT):
            job((l, "bq", tt))
        job((l, "kcvc"))
        for tt in range(TT):
            job((l, "bkv", tt))
        for tt in range(TT):
            job((l, "qkT_a", tt))
        for tt in range(TT):
            job((l, "gates", tt))
        for tt in range(TT):
            job((l, "qkT_b", tt))
        for name in ("kcmp", "vcmp"):
            job((l, name))
        for name in ("c_b", "c_c", "c_x", "c_g", "d_u", "d_g"):
            job((l, name))
        job((l, "kcT"))
        for tt in range(TT):
            job((l, "cmp_s", tt))
        for tt in range(TT):
            job((l, "cmp_pT", tt))
            job((l, "cmp_o", tt))
        job((l, "pool"))
        groups = layer_groups(l)
        scores(groups[0])
        for n, tag in enumerate(groups):
            if n + 1 < len(groups):
                scores(groups[n + 1])
            outputs(tag)
        for tt in range(TT):
            job((l, "mixT", tt))
        for tt in range(TT):
            for hf in range(2):
                job((l, "wo", tt, hf))
    for tt in range(TT):
        for hf in range(2):
            job(("hT", tt, hf))
    job(("dtf",))
    for n in range(4):
        job(("xbc", n))
    for name in ("q", "k", "z", "v"):
        for n in range(2):
            job((name, n))
    job(("tA",))
    for tt in range(TT):
        job(("xs", tt))
    for g in range(2):
        job(("cb", g))
    for n in range(TT):
        job(("y", n), (0, 1))
    for h in range(SH):
        job(("Ab", h), (2, 3, 4))
        if h % 2:
            scores(GROUPS2[h // 2], (5, 6, 7))
            if h > 1:
                outputs(GROUPS2[h // 2 - 1], (5, 6, 7))
    outputs(GROUPS2[-1], (5, 6, 7))
    for tt in range(TT):
        for hf in range(2):
            job(("mT", tt, hf))
    for tt in range(TT):
        for hf in range(2):
            job(("wo", tt, hf))
    for tt in range(TT):
        for hf in range(2):
            job(("h1T", tt, hf))
    for tt in range(TT):
        job(("route", tt))
    job(("rank",))
    return plan, order, used


def layer_groups(l):
    return [(l, branch, tt) for branch in ("slc", "win", "dsa") for tt in range(TT)]


GROUPS2 = [("att", half, tt) for half in range(2) for tt in range(TT)]


def weight_plan(a):
    w = []

    def cols(m, *ranges):
        out, at = [], 0
        for lo, n in ranges:
            out.append((at, m.rearrange("(p k) n -> p k n", k=KT)[:, :, lo:lo + n]))
            at += n
        return out

    def half(m, n):
        return [(0, m.rearrange("(k p) n -> p k n", p=P)[:, :, n * 512:n * 512 + 512])]

    for l in range(LAYERS):
        m, o = a["w_in"][l], a["w_out"][l]
        w += [((l, "w_idx"), cols(m, (A_QI, 296)), (l, "idx", 1)),
              ((l, "w_qkv"), cols(m, (A_Q, 384)), (l, "qkv", 1)),
              ((l, "w_bq"), cols(m, (B_Q, 384)), (l, "kcvc")),
              ((l, "w_bkv"), cols(m, (B_KS, 268)), (l, "bkv", 1)),
              ((l, "w_gates"), cols(m, (A_GATE, 256), (B_GATE, 256)), (l, "gates", 1)),
              ((l, "w_c1"), cols(m, (C_B, 512)), (l, "c_c")),
              ((l, "w_c2"), cols(m, (C_X, 512)), (l, "c_g")),
              ((l, "w_d"), cols(m, (D_U, 512)), (l, "d_g")),
              ((l, "w_out0"), half(o, 0), (l, "wo", 1, 0)),
              ((l, "w_out1"), half(o, 1), (l, "wo", 1, 1))]
    m, o = a["w_in_2"][0], a["w_out_2"][0]
    w += [(("xbc0",), cols(m, (XBC2, 512)), ("xbc", 1)),
          (("xbc1",), cols(m, (XBC2 + 512, 512)), ("xbc", 3)),
          (("q",), cols(m, (Q2, 512)), ("q", 1)),
          (("k",), cols(m, (K2, 512)), ("k", 1)),
          (("z",), cols(m, (Z2, 512)), ("z", 1)),
          (("v",), cols(m, (V2, 512)), ("v", 1)),
          (("out0",), half(o, 0), ("wo", 1, 0)),
          (("out1",), half(o, 1), ("wo", 1, 1))]
    return w


def build(nc, a, out):
    plan, order, used = psum_plan()
    ctx = ExitStack()
    with ctx:
        def sb(name, *shape):
            return ctx.enter_context(nc.sbuf_tensor(name, [P, *shape], F32))

        def sem(name):
            return ctx.enter_context(nc.semaphore(name))

        def shaped(flat, *shape):
            names = "abcd"[:len(shape)]
            n = int(np.prod(shape))
            if len(shape) == 1:
                return flat[:, 0:n]
            return flat[:, 0:n].rearrange("p (" + " ".join(names) + ") -> p " + " ".join(names),
                                          **dict(zip(names[1:], shape[1:])))

        class Region:

            def __init__(self, flat, width):
                self.flat, self.width, self.at = flat, width, 0

            def take(self, *shape):
                n = int(np.prod(shape))
                assert self.at + n <= self.width, (self.at, n, self.width)
                v = shaped(self.flat[:, self.at:self.at + n], *shape)
                self.at += n
                return v

        psum = [ctx.enter_context(nc.psum_tensor(f"bank{b}", [P, 512], F32)) for b in range(8)]
        ring = sb("weight_ring", SLOTS, SLOT)
        cst = sb("shape_constants_sb", CONST_W)
        zero = sb("zeros", P)
        x = sb("residual_stream", TT, D)
        hn_f, hT_f, mixT_f, ex_f, exT_f = (sb(n, TT * D) for n in ("normed", "normed_T", "mixed_T", "probs", "probs_T"))
        hn = shaped(hn_f, TT, D)
        hT = shaped(hT_f, KT, T)
        mixT = shaped(mixT_f, KT, T)
        sm = shaped(hT_f, 2, NH, T)
        ex = shaped(ex_f, 2, NH, T)
        exT = shaped(exT_f, 2, TT, NH * P)
        arena = sb("arena", ARENA)

        small = Region(sb("small_vectors", 754), 754)
        stat = small.take(4, TT)
        normw = small.take(LAYERS, KT)
        rt = sb("rope_scratch", 2, 192)
        top8 = small.take(8)
        mx, sums, coef = (small.take(2, NH) for _ in range(3))
        cmx, csum = small.take(NH), small.take(NH)
        gate = small.take(TT, 12)
        cw = small.take(LAYERS, 3, 2)
        psc = small.take(LAYERS, 2)
        wdtf = small.take(KT, 16)
        b16 = small.take(4)
        dA = small.take(4, 16)
        bx, bqk = small.take(8), small.take(8)
        cw2 = small.take(4, 8)
        cb2 = small.take(8)
        g8 = small.take(KT)
        dsk = small.take(SH)
        wr = small.take(KT, 20)
        rb = small.take(20)
        rl = small.take(TT, 20)
        rs = small.take(12, TT, 4)
        rv = small.take(12, TT)
        grp = small.take(8, 4)
        slot_of = small.take(TT)
        coef2 = small.take(4, TT)
        pw = sb("pool_w_blocks", LAYERS, 2, P)

        A = Region(arena, ARENA)
        ni, na, nb = A.take(TT, 392), A.take(TT, 448), A.take(TT, 652)
        kiT = A.take(4, T)
        kaT, ksT, kwT = (A.take(2, T) for _ in range(3))
        qaT, qbT = A.take(2, T), A.take(2, T)
        amask = A.take(TT, T)
        kvT = A.take(T)
        blk = A.take(32, CP)
        pe2, peT = A.take(2, HD), A.take(32)
        kcN = A.take(2 * HD)
        kcT = A.take(2, CP)
        vcB = A.take(NH, HD)
        gsil = A.take(TT, 512)
        mixN = A.take(TT, 512)
        cgS = A.take(2, T)
        du = A.take(2, T + 16)
        dg = A.take(2, T)
        wcmp = shaped(ex_f, 32, HD)
        over = Region(exT_f, TT * D)
        ccS, cbS, qiT, score = over.take(2, T), over.take(2, T), over.take(2, T), over.take(2, T)
        over = Region(exT_f[:, 1536:2048], 512)
        smc, ec, pcT = over.take(NH, CP), over.take(NH, CP), over.take(P)
        relu = shaped(hn_f, 8, T)
        over = Region(hn_f, TT * D)
        d2, d4, cu = over.take(2, T + 16), over.take(2, T + 16), over.take(2, T)
        ob = shaped(mixT_f, TT, 2, 256)
        cy = mixT[:, 4:6, :]

        B = Region(arena, ARENA)
        xc = B.take(8, T)
        kT2 = B.take(4, 2, T)
        qT2 = B.take(4, T)
        v2, z2 = B.take(TT, 512), B.take(TT, 512)
        cbm, seg, mTh = B.take(2, 384), B.take(2, 384), B.take(2, 384)
        dtf = B.take(8, T)
        brow = B.take(1024)
        xbc = shaped(exT_f, 8, T)
        xsN, xdt = shaped(mixT_f, TT, 512), shaped(mixT_f[:, 1024:2048], TT, 512)
        vec = shaped(ex_f, 2, D)
        merged = hn
        M = Region(arena, ARENA)
        xg = [M.take(KT, P) for _ in range(2)]
        sel = [M.take(TT, P) for _ in range(2)]
        selT = [M.take(T) for _ in range(2)]
        combine = [M.take(GE) for _ in range(2)]
        yS = [M.take(D) for _ in range(2)]
        silu_g, act_n, actT = M.take(FF), M.take(FF), M.take(FT, P)
        acc = shaped(exT_f, TT, D)
        order_i = ctx.enter_context(nc.sbuf_tensor("group_order", [P, GROUPS], mybir.dt.int32))

        def C(name, rows=P, a_=None):
            o, w = CONST[name]
            v = cst[0:rows, o:o + w]
            return v.rearrange("p (a b) -> p a b", a=a_) if a_ else v

        ident = C("ident")
        ncausal, cos64, sin64, cos32, sin32, cinv, cval, icnt = (
            C(n, a_=2) for n in ("ncausal", "cos64", "sin64", "cos32", "sin32", "cinv", "cval", "icnt"))

        def spread(ap, n):
            return ap.unsqueeze(2).broadcast_to([ap.shape[0], ap.shape[1], n])

        def repeat(ap, n):
            return ap.unsqueeze(1).broadcast_to([ap.shape[0], n, ap.shape[1]])

        filled = [sem(f"bank{b}_filled") for b in range(8)]
        drained = [sem(f"bank{b}_drained") for b in range(8)]
        slot_here = [sem(f"slot{s}_loaded") for s in range(SLOTS)]

        class Signal:

            def __init__(self, name, per=0):
                self.sem, self.n, self.per = sem(name), 0, per

            def fire(self, ins):
                self.n += 1
                return ins.then_inc(self.sem, 1)

            def at(self, l, k):
                return l * self.per + k

        x_loaded, const_loaded, small_loaded, small2_loaded = (sem(n) for n in (
            "x_loaded", "constants_loaded", "layer_vectors_loaded", "second_vectors_loaded"))
        cmp_loaded, vec_loaded, brow_loaded, stored = sem("cmp_weights_loaded"), sem("row_vectors_loaded"), sem("z_v_bias_rows_loaded"), sem("output_stored")
        zeroed = sem("pads_zeroed")
        vstep, astep, gstep = Signal("vector_step"), Signal("scalar_step"), Signal("pool_step")
        sumsq, invms, rstd_s = Signal("squares_summed", TT), Signal("mean_squares_inverted", 1), Signal("rstd_ready", 1)
        normed = Signal("normed_ready", TT)
        scored = Signal("index_scores_ready", TT)
        roped_i, roped_a, roped_b = Signal("idx_roped", TT), Signal("a_roped", TT), Signal("b_roped", TT)
        roped_c, blocks = Signal("kcmp_roped", 1), Signal("cmp_blocks_ready", 1)
        cmax, cexp, cprob = Signal("cmp_max_taken", TT), Signal("cmp_exp_done", TT), Signal("cmp_probs_ready", TT)
        gexp = Signal("branch_gates_exp", TT)
        rmax, expd = Signal("group_max_ready", 6), Signal("group_exp_done", 6 * NH)
        pooled, conv_y, conv_done = Signal("pooled_ready", 1), Signal("conv_taps_summed", 1), Signal("conv_into_mixed", 1)
        b_part, b_done = Signal("b_branches_ready", TT), Signal("b_into_mixed", TT)
        mixr = Signal("mixed_natural_ready", TT)
        vec_free, h0_ready = Signal("row_vectors_used"), Signal("h0_ready")
        coef_in, cum_ready = Signal("dt_f_steps"), Signal("cumsums_ready")
        dt_exp, dt_w, dt_ln = Signal("dt_f_exp"), Signal("dt_f_one_plus"), Signal("dt_f_ln")
        conv2, act2 = Signal("xbc_taps_summed"), Signal("xbc_silu_ready")
        zb, z_ready, xdt_ready = Signal("z_biased"), Signal("z_silu_ready"), Signal("xdt_ready")
        seg_r, dec_e, decay, y_used = Signal("decay_logs"), Signal("decay_exp"), Signal("decay_products"), Signal("y_head_done")
        ysq, yinv, yrstd = Signal("y_squares"), Signal("y_inverted"), Signal("y_rstd")
        merged_ready, ln_mu, ln_sq, ln_inv, ln_rstd = (Signal(n) for n in (
            "merged_ready", "ln_centred", "ln_squares", "ln_inverted", "ln_rstd"))
        h1_ready, final_ready = Signal("h1_ready"), Signal("output_rows_ready")
        r_in, r_exp, one_hot = Signal("router_shifted"), Signal("router_exp"), Signal("group_one_hot_ready")
        next_tile, combine_here = Signal("slots_moved_on"), Signal("slot_weights_here")
        order_ready, sel_ready = Signal("group_order_ready"), Signal("slot_selection_ready")

        yz, k2_zeroed, g8_ones = Signal("y_gated"), Signal("k2_blocks_zeroed"), Signal("merge_ones")

        def row(name):
            return a[name].rearrange("(o n) -> o n", o=1)

        def load_layer_vectors(eng):
            n = 0
            for l in range(LAYERS):
                pairs = [(normw[:, l, :], a["norm_w"][l].rearrange("(p k) -> p k", k=KT)),
                         (psc[:, l, :], a["pool_scale"][l].rearrange("(c p) -> p c", p=P))]
                pairs += [(cw[:, l, j, :], a["conv_w"][l, j].rearrange("(c p) -> p c", p=P)) for j in range(3)]
                for h in range(2):
                    r = slice(HD * h, HD * h + HD)
                    pairs.append((pw[r, l, :, r], a["pool_w"][l].rearrange("(j h) c d -> h c j d", h=2)[h]))
                for n_, (dst, src) in enumerate(pairs):
                    if l == 0 and n_ == 0:
                        eng.wait_ge(zeroed, ZEROED)
                    eng.dma_start(dst, src, allow_slow_non_contiguous=True).then_inc(small_loaded, 16)
                    n += 1
            assert SMALL == 16 * n, n

        def load_second_vectors(eng):
            wi = a["w_in_2"][0].rearrange("(p k) n -> p k n", k=KT)
            bi = a["b_in_2"][0]
            col = lambda v: v.rearrange("(c p) -> p c", p=P)
            one = lambda v: v.rearrange("(n o) -> n o", o=1)
            pairs = [(wdtf[:, :, 0:8], wi[:, :, DT2:DT2 + 8]), (wdtf[:, :, 8:16], wi[:, :, F2:F2 + 8]),
                     (b16[0:8, 0:1], one(bi[DT2:DT2 + 8])), (b16[8:16, 0:1], one(bi[F2:F2 + 8])),
                     (b16[0:8, 1:2], one(a["a_log_2"][0])),
                     (bx, col(bi[XBC2:XBC2 + 1024])), (bqk, col(bi[Q2:Q2 + 1024])),
                     (cb2, col(a["conv_b_2"][0])), (g8[:, 0:4], col(a["ssd_norm_g_2"][0])),
                     (dsk, a["d_skip_2"].broadcast_to([P, SH])),
                     (rb[:, 0:4], a["router_group_b_2"].broadcast_to([P, 4])),
                     (rb[:, 4:20], a["router_expert_b_2"].rearrange("o g e -> o (g e)").broadcast_to([P, 16])),
                     (wr[:, :, 0:4], a["router_group_w_2"][0].rearrange("(p k) n -> p k n", k=KT))]
            pairs += [(cw2[:, j, :], col(a["conv_w_2"][0, j])) for j in range(4)]
            pairs += [(wr[:, :, 4 + 4 * g:8 + 4 * g], a["router_expert_w_2"][0, g].rearrange("(p k) n -> p k n", k=KT))
                      for g in range(4)]
            for dst, src in pairs:
                eng.dma_start(dst, src, allow_slow_non_contiguous=True).then_inc(small2_loaded, 16)
            assert SMALL2 == 16 * len(pairs), len(pairs)

        small_dmas = (load_layer_vectors, load_second_vectors)
        block = ctx.enter_context(nc.Block())

        def bank(key):
            return psum[plan[key][0]]

        def wait_filled(eng, key):
            b, n = plan[key]
            eng.wait_ge(filled[b], n + 1)
            return psum[b]

        def wait_drained(eng, key):
            b, n = plan[key]
            eng.wait_ge(drained[b], n + 1)

        def drains(ins, key):
            return ins.then_inc(drained[plan[key][0]], 1)

        chunks, loads, value, last = {}, [], [0] * SLOTS, [None] * SLOTS
        for n, (key, pieces, job) in enumerate(weight_plan(a)):
            s = n % SLOTS
            value[s] += 16 * len(pieces)
            width = sum(p[1].shape[2] for p in pieces)
            view = ring[:, s, 0:KT * width].rearrange("p (k n) -> p k n", k=KT)
            loads.append((s, last[s], [(view[:, :, at:at + p.shape[2]], p) for at, p in pieces]))
            chunks[key] = (s, value[s], view)
            last[s] = job
        expert_slot0 = len(loads) % SLOTS

        def eslot(e, k):
            return (expert_slot0 + 3 * (e % 2) + k) % SLOTS

        FILLS = {0: 1, 1: 1, 2: GE, 3: 1, 4: GE + 1, 5: GE + 1, 6: GE + 1, 7: 2}
        LAST = GROUPS - 1

        def at(b, n, k):
            return used[b] + n * FILLS[b] + k

        def outputs_read(n):
            return [used[b] + n + 1 for b in (2, 3)]

        def released(k, n, e):
            b = (4, 5, 2)[k]
            return b, at(b, n, e + 1)

        @block.sync
        def _(sp):
            for tt in range(TT):
                sp.dma_start(x[:, tt, :], a["x"][0, tt * P:(tt + 1) * P, :]).then_inc(x_loaded, 16)
            for s, job, pieces in loads:
                if job is not None:
                    wait_filled(sp, job)
                for dst, src in pieces:
                    sp.dma_start(dst, src).then_inc(slot_here[s], 16)

            def expert_weights(k, group, e):
                s = eslot(e, k)
                n = KT if k < 2 else FT
                src = a[("w_gate_2", "w_up_2", "w_down_2")[k]][0][bass.ds(group * GE + e, 1)].rearrange("o a b -> (o a) b")
                src = src.rearrange("(p k) n -> p k n", k=n) if k < 2 else src.rearrange("(k p) n -> p k n", p=P)
                sp.dma_start(ring[:, s, :].rearrange("p (k n) -> p k n", k=n), src).then_inc(slot_here[s], 16)

            sp.wait_ge(order_ready.sem, 1)
            with sp.Fori(0, LAST) as n:
                group = sp.value_load(order_i[0:1, bass.ds(n, 1)], min_val=0, max_val=GROUPS - 1)
                for e in range(GE):
                    for k in range(3):
                        b, count = released(k, n, e - 2) if e >= 2 else released(k, n - 1, e + 2)
                        sp.wait_ge(filled[b], count)
                        expert_weights(k, group, e)
            group = sp.value_load(order_i[0:1, LAST:GROUPS], min_val=0, max_val=GROUPS - 1)
            for e in range(GE):
                for k in range(3):
                    if e < 2:
                        b, count = released(k, LAST - 1, e + 2)
                    else:
                        b = (4, 5, 2)[k]
                        count = at(b, LAST, 2 * (e - 2) + 2)
                    sp.wait_ge(filled[b], count)
                    expert_weights(k, group, e)
            for tt in range(TT):
                sp.wait_ge(final_ready.sem, tt + 1)
                sp.dma_start(out[0, tt * P:(tt + 1) * P, :], acc[:, tt, :]).then_inc(stored, 16)
            sp.wait_ge(stored, 16 * TT)

        @block.tensor
        def _(pe):
            todo = list(order)

            def claim(key):
                assert todo.pop(0) == key, key
                b, n = plan[key]
                if n:
                    pe.wait_ge(drained[b], n)
                return psum[b]

            def fill(ins, key):
                ins.then_inc(filled[plan[key][0]], 1)

            def weights(key):
                s, v, view = chunks[key]
                pe.wait_ge(slot_here[s], v)
                return view

            def product(dst, lhs, rhs, n=KT, **kw):
                for k in range(n):
                    ins = pe.matmul(dst, lhs(k), rhs(k), start=(k == 0), stop=(k == n - 1), **kw)
                return ins

            def token_rows(key, w, tt, c0, n):
                ps = claim(key)
                fill(product(ps[:, 0:n], lambda k: hT[:, k, tt * P:(tt + 1) * P], lambda k: w[:, k, c0:c0 + n]), key)

            def channel_rows(key, w, c0, tiles):
                ps = claim(key)
                for j in range(tiles):
                    ins = product(ps[:, j * T:(j + 1) * T], lambda k: w[:, k, c0 + j * P:c0 + (j + 1) * P],
                                  lambda k: hT[:, k, :])
                fill(ins, key)

            def transposes(key, srcs, width=P, rows=P):
                ps = claim(key)
                for n, src in enumerate(srcs):
                    ins = pe.transpose(ps[0:src.shape[1], n * width:n * width + rows], src, ident[0:rows, 0:rows])
                fill(ins, key)

            def natural_to_T(key, src, tt, hf, strided):
                transposes(key, [src[:, tt, (4 * hf + k):D:KT] if strided else
                                 src[:, tt, (4 * hf + k) * P:(4 * hf + k + 1) * P] for k in range(4)])

            group = [0]

            def scores(tag, qT, kT, extra=None):
                tt = tag[2]
                nk = (tt + 1) * P
                for p in range(2):
                    ps = claim(tag + ("s", p))
                    dst = ps[:, 0:2 * nk].rearrange("p (a b) -> p a b", a=2)
                    ins = pe.matmul(dst, qT(p)[:, tt * P:(tt + 1) * P], kT(p)[:, :, 0:nk], start=True, stop=True)
                    if extra is not None:
                        for j in range(2):
                            ins = pe.matmul(dst[:, j, :], extra(2 * p + j), dtf[0:16, 6, 0:nk], start=False, stop=True,
                                            skip_group_check=True)
                    fill(ins, tag + ("s", p))

            def outputs(tag, v):
                tt = tag[2]
                g = group[0]
                group[0] += 1
                for h in range(NH):
                    pe.wait_ge(expd.sem, NH * g + h + 1)
                    if h == 0:
                        for kt in range(tt + 1):
                            claim(tag + ("pT", kt))
                    for kt in range(tt + 1):
                        ins = pe.transpose(bank(tag + ("pT", kt))[:, h * P:(h + 1) * P],
                                           ex[:, g % 2, h, kt * P:(kt + 1) * P], ident)
                        if h == NH - 1:
                            fill(ins, tag + ("pT", kt))
                ps = claim(tag + ("o",))
                for kt in range(tt + 1):
                    wait_drained(pe, tag + ("pT", kt))
                for h in range(NH):
                    ins = product(ps[:, h * HD:(h + 1) * HD], lambda kt: exT[:, g % 2, kt, h * P:(h + 1) * P],
                                  lambda kt: v(kt, h), n=tt + 1)
                fill(ins, tag + ("o",))

            pe.wait_ge(const_loaded, 16)
            pe.wait_ge(zeroed, ZEROED)
            for l in range(LAYERS):
                for tt in range(TT):
                    pe.wait_ge(normed.sem, normed.at(l, tt + 1))
                    for hf in range(2):
                        natural_to_T((l, "hT", tt, hf), hn, tt, hf, True)
                pe.wait_ge(cmp_loaded, 64 * (l + 1))
                transposes((l, "peT"), [pe2[0:32, :, :].rearrange("p a b -> p (a b)")], rows=32)
                for tt in range(TT):
                    for hf in range(2):
                        wait_drained(pe, (l, "hT", tt, hf))
                w = weights((l, "w_idx"))
                for tt in range(TT):
                    token_rows((l, "idx", tt), w, tt, 0, 296)
                w = weights((l, "w_qkv"))
                for tt in range(TT):
                    token_rows((l, "qkv", tt), w, tt, 0, 384)
                for tt in range(TT):
                    pe.wait_ge(roped_i.sem, roped_i.at(l, tt + 1))
                    transposes((l, "idxT", tt), [ni[:, tt, n * P:(n + 1) * P] for n in range(3)])
                for tt in range(TT):
                    wait_drained(pe, (l, "idxT", tt))
                for tt in range(TT):
                    for n in range(4):
                        ps = claim((l, "logit", tt, n))
                        nk = (tt + 1) * P
                        fill(pe.matmul(ps[:, 0:2 * nk].rearrange("p (a b) -> p a b", a=2),
                                       qiT[:, n // 2, tt * P:(tt + 1) * P],
                                       kiT[:, 2 * (n % 2):2 * (n % 2) + 2, 0:nk], start=True, stop=True),
                             (l, "logit", tt, n))
                w = weights((l, "w_bq"))
                for tt in range(TT):
                    token_rows((l, "bq", tt), w, tt, 0, 256)
                channel_rows((l, "kcvc"), w, 256, 1)
                w = weights((l, "w_bkv"))
                for tt in range(TT):
                    token_rows((l, "bkv", tt), w, tt, 0, 268)
                for tt in range(TT):
                    pe.wait_ge(roped_a.sem, roped_a.at(l, tt + 1))
                    transposes((l, "qkT_a", tt), [na[:, tt, n * P:(n + 1) * P] for n in range(3)])
                w = weights((l, "w_gates"))
                for tt in range(TT):
                    token_rows((l, "gates", tt), w, tt, 0, 512)
                for tt in range(TT):
                    pe.wait_ge(roped_b.sem, roped_b.at(l, tt + 1))
                    transposes((l, "qkT_b", tt), [nb[:, tt, n * P:(n + 1) * P] for n in range(4)])
                pe.wait_ge(blocks.sem, blocks.at(l, 1))
                for n, name in enumerate(("kcmp", "vcmp")):
                    r = slice(n * HD, (n + 1) * HD)
                    ps = claim((l, name))
                    fill(product(ps[0:CP, 0:HD], lambda k: blk[r, k, :], lambda k: wcmp[r, k, :], n=32), (l, name))
                w = weights((l, "w_c1"))
                channel_rows((l, "c_b"), w, 0, 2)
                channel_rows((l, "c_c"), w, 256, 2)
                w = weights((l, "w_c2"))
                channel_rows((l, "c_x"), w, 0, 2)
                channel_rows((l, "c_g"), w, 256, 2)
                w = weights((l, "w_d"))
                channel_rows((l, "d_u"), w, 0, 2)
                channel_rows((l, "d_g"), w, 256, 2)
                pe.wait_ge(roped_c.sem, roped_c.at(l, 1))
                transposes((l, "kcT"), [kcN[0:CP, :]], rows=CP)
                wait_drained(pe, (l, "kcT"))
                wait_drained(pe, (l, "vcmp"))
                for tt in range(TT):
                    wait_drained(pe, (l, "qkT_b", tt))
                for tt in range(TT):
                    ps = claim((l, "cmp_s", tt))
                    for p in range(2):
                        ins = pe.matmul(ps[:, p * 64:p * 64 + 64].rearrange("p (a b) -> p a b", a=2),
                                        qbT[:, p, tt * P:(tt + 1) * P], kcT[:, :, :], start=True, stop=True)
                    fill(ins, (l, "cmp_s", tt))
                for tt in range(TT):
                    pe.wait_ge(cprob.sem, cprob.at(l, tt + 1))
                    transposes((l, "cmp_pT", tt), [ec[:].rearrange("p a b -> p (a b)")])
                    wait_drained(pe, (l, "cmp_pT", tt))
                    ps = claim((l, "cmp_o", tt))
                    fill(pe.matmul(ps[:, 0:256], pcT[:, :], vcB[:].rearrange("p a b -> p (a b)"), start=True, stop=True),
                         (l, "cmp_o", tt))
                pe.wait_ge(pooled.sem, pooled.at(l, 1))
                ps = claim((l, "pool"))
                for j in range(2):
                    ins = pe.matmul(ps[:, j * T:(j + 1) * T], pw[:, l, j, :], mixT[:, 6 + j, :], start=True, stop=True)
                fill(ins, (l, "pool"))
                operands = {"slc": (qbT, ksT, nb, 512), "win": (qbT, kwT, nb, 576), "dsa": (qaT, kaT, na, 384)}

                def layer_scores(tag):
                    q, k, _, _ = operands[tag[1]]
                    scores(tag, lambda p: q[:, p, :], lambda p: k[:])

                groups = layer_groups(l)
                layer_scores(groups[0])
                for n, tag in enumerate(groups):
                    if n + 1 < len(groups):
                        layer_scores(groups[n + 1])
                    _, _, vals, column = operands[tag[1]]
                    outputs(tag, lambda kt, h: vals[:, kt, column:column + HD])
                for tt in range(TT):
                    pe.wait_ge(mixr.sem, mixr.at(l, tt + 1))
                    transposes((l, "mixT", tt), [mixN[:, tt, n * P:(n + 1) * P] for n in range(4)])
                pe.wait_ge(conv_done.sem, conv_done.at(l, 1))
                wait_drained(pe, (l, "pool"))
                for tt in range(TT):
                    wait_drained(pe, (l, "mixT", tt))
                    for hf in range(2):
                        w = weights((l, f"w_out{hf}"))
                        ps = claim((l, "wo", tt, hf))
                        fill(product(ps[:, :], lambda k: mixT[:, k, tt * P:(tt + 1) * P], lambda k: w[:, k, :]),
                             (l, "wo", tt, hf))
            for tt in range(TT):
                pe.wait_ge(h0_ready.sem, tt + 1)
                for hf in range(2):
                    natural_to_T(("hT", tt, hf), x, tt, hf, True)
            for tt in range(TT):
                for hf in range(2):
                    wait_drained(pe, ("hT", tt, hf))
            pe.wait_ge(small2_loaded, SMALL2)
            ps = claim(("dtf",))
            fill(product(ps[0:16, 0:T], lambda k: wdtf[:, k, :], lambda k: hT[:, k, :]), ("dtf",))
            for n in range(4):
                channel_rows(("xbc", n), weights((f"xbc{n // 2}",)), 256 * (n % 2), 2)
            for name in ("q", "k"):
                for n in range(2):
                    channel_rows((name, n), weights((name,)), 256 * n, 2)
            for name in ("z", "v"):
                for tt in range(TT):
                    token_rows((name, tt), weights((name,)), tt, 0, 512)
            pe.wait_ge(cum_ready.sem, 1)
            transposes(("tA",), [dtf[0:16, r, tt * P:(tt + 1) * P] for tt in range(TT) for r in (4, 5)], width=16, rows=16)
            pe.wait_ge(act2.sem, 8)
            for tt in range(TT):
                transposes(("xs", tt), [xc[:, n, tt * P:(tt + 1) * P] for n in range(4)])
            for g in range(2):
                ps = claim(("cb", g))
                pe.matmul(ps[:, 0:T], xc[:, 4 + g, 0:P], xc[:, 6 + g, :], start=True, stop=True)
                fill(pe.matmul(ps[:, T:T + P], xc[:, 4 + g, P:T], xc[:, 6 + g, P:T], start=True, stop=True), ("cb", g))
            for n in range(TT):
                claim(("y", n))

            def y_head(h):
                pe.wait_ge(decay.sem, h + 1)
                if h == 0:
                    pe.wait_ge(xdt_ready.sem, 1)
                r = xdt[:, :, h * HD:(h + 1) * HD]
                a0 = pe.matmul(psum[0][:, h * HD:(h + 1) * HD], mTh[:, h % 2, 0:P], r[:, 0, :], start=True, stop=True)
                pe.matmul(psum[1][:, h * HD:(h + 1) * HD], mTh[:, h % 2, P:T], r[:, 0, :], start=True, stop=False)
                a1 = pe.matmul(psum[1][:, h * HD:(h + 1) * HD], mTh[:, h % 2, T:T + P], r[:, 1, :], start=False, stop=True)
                if h < SH - 1:
                    y_used.fire(a1)
                else:
                    fill(a0, ("y", 0))
                    fill(a1, ("y", 1))

            def scores2(tag):
                h0 = NH * tag[1]
                scores(tag, lambda p: qT2[:, h0 // 2 + p, :], lambda p: kT2[:, h0 // 2 + p, :, :],
                       extra=lambda h: ident[0:16, SH + h0 + h:SH + h0 + h + 1].broadcast_to([16, P]))

            def outputs2(tag):
                h0 = NH * tag[1]
                outputs(tag, lambda kt, h: v2[:, kt, (h0 + h) * HD:(h0 + h + 1) * HD])

            for h in range(SH):
                ps = claim(("Ab", h))
                fill(pe.matmul(ps[:, 0:T], ident[0:16, h:h + 1].broadcast_to([16, P]), dtf[0:16, 5, :], start=True, stop=True),
                     ("Ab", h))
                if h:
                    y_head(h - 1)
                if h % 2:
                    if h == 1:
                        wait_drained(pe, ("q", 1))
                        wait_drained(pe, ("k", 1))
                        wait_drained(pe, ("v", 1))
                        pe.wait_ge(cum_ready.sem, 2)
                    scores2(GROUPS2[h // 2])
                    if h > 1:
                        outputs2(GROUPS2[h // 2 - 1])
            y_head(SH - 1)
            outputs2(GROUPS2[-1])
            for tt in range(TT):
                pe.wait_ge(merged_ready.sem, tt + 1)
                for hf in range(2):
                    natural_to_T(("mT", tt, hf), merged, tt, hf, False)
            for tt in range(TT):
                for hf in range(2):
                    wait_drained(pe, ("mT", tt, hf))
                for hf in range(2):
                    w = weights((f"out{hf}",))
                    ps = claim(("wo", tt, hf))
                    fill(product(ps[:, :], lambda k: mixT[:, k, tt * P:(tt + 1) * P], lambda k: w[:, k, :]), ("wo", tt, hf))
            for tt in range(TT):
                pe.wait_ge(h1_ready.sem, tt + 1)
                for hf in range(2):
                    natural_to_T(("h1T", tt, hf), x, tt, hf, True)
            for tt in range(TT):
                for hf in range(2):
                    wait_drained(pe, ("h1T", tt, hf))
                ps = claim(("route", tt))
                fill(product(ps[:, 0:20], lambda k: hT[:, k, tt * P:(tt + 1) * P], lambda k: wr[:, k, :]), ("route", tt))
            pe.wait_ge(one_hot.sem, 1)
            oh = rs[:, 2, :, :]
            tri = C("ltri")
            ps = claim(("rank",))
            pe.matmul(ps[:, 0:4], tri[:, 0:P], oh[:, 0, :], start=True, stop=True)
            pe.matmul(ps[:, 4:8], tri[:, P:T], oh[:, 0, :], start=True, stop=False)
            pe.matmul(ps[:, 4:8], tri[:, T:T + P], oh[:, 1, :], start=False, stop=True)
            pe.matmul(ps[:, 8:12], tri[:, P:T], oh[:, 0, :], start=True, stop=False)
            fill(pe.matmul(ps[:, 8:12], tri[:, P:T], oh[:, 1, :], start=False, stop=True), ("rank",))

            def gather(n, tile, selected):
                pe.wait_ge(sel_ready.sem, selected)
                for b in range(2):
                    pe.wait_ge(drained[b], at(b, n, 0))
                    for k in range(4):
                        ins = product(psum[b][:, k * P:(k + 1) * P], lambda tt: x[:, tt, 4 * b + k:D:KT],
                                      lambda tt: sel[tile][:, tt, :], n=TT)
                    ins.then_inc(filled[b], 1)

            def turn_selection(n, tile, k):
                pe.wait_ge(drained[7], at(7, n, k))
                for tt in range(TT):
                    pe.transpose(psum[7][:, tt * P:(tt + 1) * P], sel[tile][:, tt, :], ident)
                product(psum[7][:, T:T + GE], lambda tt: sel[tile][:, tt, :], lambda tt: rs[:, 9, tt, :], n=TT)\
                    .then_inc(filled[7], 1)

            def expert_matrix(e, k, turn):
                s = eslot(e, k)
                pe.wait_ge(slot_here[s], value[s] + 16 * turn)
                return ring[:, s, :].rearrange("p (k n) -> p k n", k=KT if k < 2 else FT)

            def gate_or_up(n, e, k, step, tile, turn):
                b = 4 + k
                w = expert_matrix(e, k, turn)
                pe.wait_ge(drained[b], at(b, n, step))
                product(psum[b][:, :], lambda i: xg[tile][:, i, :], lambda i: w[:, i, :]).then_inc(filled[b], 1)

            def turn_act(n, step):
                pe.wait_ge(drained[5], at(5, n, step + 1))
                pe.wait_ge(drained[6], at(6, n, step))
                for f in range(FT):
                    ins = pe.transpose(psum[6][:, f * P:(f + 1) * P], act_n[:, f * P:(f + 1) * P], ident)
                ins.then_inc(filled[6], 1)

            def down(n, e, step, tile, turn):
                w = expert_matrix(e, 2, turn)
                pe.wait_ge(drained[6], at(6, n, step + 1))
                for hf in range(2):
                    for f in range(FT):
                        ins = pe.matmul(psum[(2 + hf) if tile == 0 else hf][:, :], actT[:, f, :],
                                        w[:, f, hf * 512:(hf + 1) * 512], start=(e == 0 and f == 0),
                                        stop=(e == GE - 1 and f == FT - 1))
                ins.then_inc(filled[2], 1)

            def group_experts(n, tiles, turn0, before_last):
                for b in (2, 3):
                    pe.wait_ge(drained[b], used[b] + n)
                steps = [(e, tile) for e in range(GE) for tile in range(tiles)]
                for s, (e, tile) in enumerate(steps):
                    gate_or_up(n, e, 0, s, tile, turn0 + e // 2)
                    if s:
                        turn_act(n, s - 1)
                    gate_or_up(n, e, 1, s, tile, turn0 + e // 2)
                    if s:
                        down(n, steps[s - 1][0], s - 1, steps[s - 1][1], turn0 + steps[s - 1][0] // 2)
                before_last()
                turn_act(n, len(steps) - 1)
                down(n, GE - 1, len(steps) - 1, tiles - 1, turn0 + 1)

            def put_back(n, tiles, k7):
                for b, count in zip((2, 3), outputs_read(n)):
                    pe.wait_ge(drained[b], count)
                if tiles == 2:
                    for b in (0, 1):
                        pe.wait_ge(drained[b], at(b, LAST, 3))
                for q in range(4):
                    b, tt, hf = 4 + q, q // 2, q % 2
                    pe.wait_ge(drained[b], at(b, n, k7 if b == 7 else GE * tiles))
                    product(psum[b][:, :], lambda i: selT[i][:, tt * P:(tt + 1) * P],
                            lambda i: yS[i][:, hf * 512:(hf + 1) * 512], n=tiles).then_inc(filled[b], 1)

            gather(0, 0, 1)
            turn_selection(0, 0, 0)
            with pe.Fori(0, LAST) as n:
                for b in range(2):
                    pe.wait_ge(drained[b], at(b, n, 1))
                group_experts(n, 1, 2 * n + 1, lambda: gather(n + 1, 0, n + 2))
                pe.wait_ge(drained[7], at(7, n, 1))
                put_back(n, 1, 1)
                turn_selection(n + 1, 0, 0)
            gather(LAST + 1, 1, LAST + 2)
            turn_selection(LAST, 1, 1)
            for b in range(2):
                pe.wait_ge(drained[b], at(b, LAST, 2))
            group_experts(LAST, 2, 2 * LAST + 1, lambda: None)
            pe.wait_ge(drained[7], at(7, LAST, 2))
            put_back(LAST, 2, 2)
            assert not todo

        @block.vector
        def _(dve):
            def step(ins):
                vstep.fire(ins)
                dve.wait_ge(vstep.sem, vstep.n)

            def step_on(signal, ins):
                signal.fire(ins)
                dve.wait_ge(signal.sem, signal.n)

            def drain_step(ins, key):
                drains(ins, key)
                wait_drained(dve, key)

            V = nc.vector

            def inverse(dst, src, guard=None):
                if guard is not None:
                    step(V.tensor_scalar(src, src, guard, None, ALU.max))
                step(V.reciprocal(dst, src))

            def invert_mean_squares(n, eps, src, dst, signal):
                step(V.tensor_scalar(src, src, 1.0 / n, eps, ALU.mult, ALU.add))
                signal.fire(V.reciprocal(dst, src))

            def copy_T(key, tt, hf, scale=None, dst=hT):
                ps = wait_filled(dve, key)[:, :].rearrange("p (a b) -> p a b", a=4)
                d = dst[:, 4 * hf:4 * hf + 4, tt * P:(tt + 1) * P]
                if scale is None:
                    drains(V.tensor_copy(d, ps), key)
                else:
                    drains(V.tensor_tensor(d, ps, spread(scale[:, 4 * hf:4 * hf + 4], P), ALU.mult), key)

            group = [0, 0]

            def mask_and_max(tag, mask):
                g, tt = group[0], tag[2]
                group[0] += 1
                nk = (tt + 1) * P
                if g >= 2:
                    dve.wait_ge(expd.sem, NH * (g - 1))
                s = sm[:, g % 2, :, 0:nk]
                for p in range(2):
                    ps = wait_filled(dve, tag + ("s", p))[:, 0:2 * nk].rearrange("p (a b) -> p a b", a=2)
                    drains(V.scalar_tensor_tensor(s[:, 2 * p:2 * p + 2, :], repeat(mask, 2), BIG, ps, ALU.mult, ALU.add),
                           tag + ("s", p))
                wait_drained(dve, tag + ("s", 1))
                wait_drained(dve, tag + ("s", 0))
                step(V.tensor_reduce(mx[:, g % 2, :], s, AX_X, ALU.max))
                rmax.fire(V.tensor_scalar(mx[:, g % 2, :], mx[:, g % 2, :], -(HD ** -0.5), None, ALU.mult))

            def row_coef():
                g = group[1]
                group[1] += 1
                dve.wait_ge(expd.sem, NH * (g + 1))
                inverse(coef[:, g % 2, :], sums[:, g % 2, :], 1e-30)
                return coef[:, g % 2, :]

            def heads(ap):
                return ap.rearrange("p (a b) -> p a b", a=NH)

            dve.wait_ge(const_loaded, 16)
            dve.wait_ge(small_loaded, SMALL)
            dve.wait_ge(zeroed, ZEROED)
            for l in range(LAYERS):
                dve.wait_ge(sumsq.sem, sumsq.at(l, TT))
                invert_mean_squares(D, EPS, stat[:, 0, :], stat[:, 1, :], invms)
                dve.wait_ge(rstd_s.sem, rstd_s.at(l, 1))
                for tt in range(TT):
                    normed.fire(V.tensor_scalar(hn[:, tt, :], x[:, tt, :], stat[:, 2, tt:tt + 1], None, ALU.mult))
                for tt in range(TT):
                    for hf in range(2):
                        copy_T((l, "hT", tt, hf), tt, hf, normw[:, l, :])
                drains(V.tensor_copy(peT[:, :], wait_filled(dve, (l, "peT"))[:, 0:32]), (l, "peT"))
                for tt in range(TT):
                    nk = (tt + 1) * P
                    for n in range(4):
                        wait_drained(dve, (l, "logit", tt, n))
                    step(V.tensor_scalar(score[:, 0, 0:nk], ncausal[:, tt, 0:nk], BIG, None, ALU.mult))
                    for h in range(8):
                        ins = V.scalar_tensor_tensor(score[:, 0, 0:nk], relu[:, h, 0:nk], ni[:, tt, 384 + h:385 + h],
                                                     score[:, 0, 0:nk], ALU.mult, ALU.add)
                        step(ins) if h < 7 else step_on(scored, ins)
                    for r in range(TOPK // 8):
                        src, dst = score[:, r % 2, 0:nk], score[:, 1 - r % 2, 0:nk]
                        step(V.max(top8[:, :], src))
                        step(V.match_replace(dst, top8[:, :], src, TAKEN))
                    step(V.scalar_tensor_tensor(amask[:, tt, 0:nk], score[:, 0, 0:nk], TAKEN, ncausal[:, tt, 0:nk],
                                                ALU.not_equal, ALU.max))
                wait_drained(dve, (l, "kcvc"))
                wait_drained(dve, (l, "peT"))
                kv = kvT[:, :].rearrange("p (n b) -> p b n", b=16)
                V.tensor_tensor(blk[:, 0:16, 0:NCMP], kv[:, :, 0:NCMP], spread(peT[:, 0:16], NCMP), ALU.add)
                blocks.fire(V.tensor_tensor(blk[:, 16:32, 0:NCMP], kv[:, :, 1:NCMP + 1], spread(peT[:, 16:32], NCMP), ALU.add))
                dve.wait_ge(gexp.sem, gexp.at(l, TT))
                step(V.tensor_scalar(gate[:, :, :], gate[:, :, :], 1.0, None, ALU.add))
                step(V.reciprocal(gate[:, :, :], gate[:, :, :]))
                wait_drained(dve, (l, "c_c"))
                ps = wait_filled(dve, (l, "c_x"))
                drain_step(V.tensor_tensor(cu[:, :, :], ccS[:, :, :], ps[:, :].rearrange("p (a b) -> p a b", a=2), ALU.mult),
                           (l, "c_x"))
                for j in range(2):
                    step(V.tensor_scalar(cy[:, j, :], cu[:, j, :], cw[:, l, 2, j:j + 1], None, ALU.mult))
                    for k in (1, 2):
                        ins = V.scalar_tensor_tensor(cy[:, j, k:T], cu[:, j, 0:T - k], cw[:, l, 2 - k, j:j + 1],
                                                     cy[:, j, k:T], ALU.mult, ALU.add)
                        conv_y.fire(ins) if (j, k) == (1, 2) else step(ins)
                for tt in range(TT):
                    ps = wait_filled(dve, (l, "cmp_s", tt))[:, 0:128].rearrange("p (a b) -> p a b", a=NH)
                    drain_step(V.scalar_tensor_tensor(smc[:, :, :], repeat(cinv[:, tt, :], NH), BIG, ps, ALU.mult, ALU.add),
                               (l, "cmp_s", tt))
                    step(V.tensor_reduce(cmx[:, :], smc[:, :, :], AX_X, ALU.max))
                    cmax.fire(V.tensor_tensor(smc[:, :, :], smc[:, :, :], spread(cmx[:, :], CP), ALU.subtract))
                    dve.wait_ge(cexp.sem, cexp.at(l, tt + 1))
                    step_on(cprob, V.tensor_tensor(ec[:, :, :], ec[:, :, :], repeat(cval[:, tt, :], NH), ALU.mult))
                    step(V.tensor_reduce(csum[:, :], ec[:, :, :], AX_X, ALU.add))
                    inverse(csum[:, :], csum[:, :], 1e-30)
                    step(V.tensor_tensor(csum[:, :], csum[:, :], gate[:, tt, 0:12:3], ALU.mult))
                    ps = wait_filled(dve, (l, "cmp_o", tt))
                    drains(V.tensor_tensor(shaped(ob[:, tt, 0, :], NH, HD), heads(ps[:, 0:256]), spread(csum[:, :], HD), ALU.mult),
                           (l, "cmp_o", tt))
                ps = wait_filled(dve, (l, "pool"))
                wait_drained(dve, (l, "d_g"))
                for j in range(2):
                    ins = V.scalar_tensor_tensor(mixT[:, 6 + j, :], ps[:, j * T:(j + 1) * T], psc[:, l, j:j + 1], dg[:, j, :],
                                                 ALU.mult, ALU.mult)
                drains(ins, (l, "pool"))
                groups = layer_groups(l)

                def mask_of(tag):
                    nk = (tag[2] + 1) * P
                    return (amask if tag[1] == "dsa" else ncausal)[:, tag[2], 0:nk]

                mask_and_max(groups[0], mask_of(groups[0]))
                for n, tag in enumerate(groups):
                    if n + 1 < len(groups):
                        mask_and_max(groups[n + 1], mask_of(groups[n + 1]))
                    _, branch, tt = tag
                    c = row_coef()
                    key = tag + ("o",)
                    if branch != "dsa":
                        step(V.tensor_tensor(c, c, gate[:, tt, (1 if branch == "slc" else 2):12:3], ALU.mult))
                    ps = wait_filled(dve, key)
                    to = {"slc": ob[:, tt, 1, :], "win": mixN[:, tt, 256:512], "dsa": mixN[:, tt, 0:256]}[branch]
                    drains(V.tensor_tensor(heads(to), heads(ps[:, 0:256]), spread(c, HD), ALU.mult), key)
                    if branch == "dsa":
                        wait_drained(dve, key)
                        wait_drained(dve, (l, "gates", tt))
                        dve.wait_ge(b_done.sem, b_done.at(l, tt + 1))
                        mixr.fire(V.tensor_tensor(mixN[:, tt, 0:256], mixN[:, tt, 0:256], gsil[:, tt, 0:256], ALU.mult))
                for tt in range(TT):
                    for hf in range(2):
                        ps = wait_filled(dve, (l, "wo", tt, hf))
                        r = x[:, tt, hf * 512:(hf + 1) * 512]
                        drains(V.tensor_tensor(r, r, ps[:, :], ALU.add), (l, "wo", tt, hf))
            dve.wait_ge(sumsq.sem, sumsq.at(LAYERS, TT))
            invert_mean_squares(D, EPS, stat[:, 0, :], stat[:, 1, :], invms)
            dve.wait_ge(rstd_s.sem, rstd_s.at(LAYERS, 1))
            dve.wait_ge(vec_loaded, 16)
            for tt in range(TT):
                h0_ready.fire(V.scalar_tensor_tensor(x[:, tt, :], x[:, tt, :], stat[:, 2, tt:tt + 1], vec[:, 0, :],
                                                     ALU.mult, ALU.mult))
            for tt in range(TT):
                for hf in range(2):
                    copy_T(("hT", tt, hf), tt, hf)
            dve.wait_ge(small2_loaded, SMALL2)
            coef_in.fire(V.tensor_tensor(b16[0:16, 2:3], b16[0:16, 0:1], C("sgn", rows=16), ALU.mult))
            dve.wait_ge(dt_exp.sem, 2)
            R = [dtf[0:16, r, :] for r in range(8)]
            step_on(dt_w, V.tensor_scalar(R[2], R[1], 1.0, None, ALU.add))
            step(V.tensor_scalar(R[3], R[2], 1.0, None, ALU.subtract))
            step(V.tensor_scalar(R[7], R[3], 0.0, None, ALU.is_equal))
            inverse(R[3], R[3], TINY)
            dve.wait_ge(dt_ln.sem, 1)
            step(V.tensor_tensor(R[4], R[4], R[3], ALU.mult))
            step(V.tensor_tensor(R[4], R[4], R[7], ALU.add))
            step(V.tensor_tensor(R[4], R[4], R[1], ALU.mult))
            step(V.scalar_tensor_tensor(R[4], R[0], 0.0, R[4], ALU.max, ALU.add))
            step(V.memset(R[2], 1.0))
            step(V.tensor_scalar(R[3], R[4], b16[0:16, 3:4], -1.0, ALU.mult, ALU.mult))
            step_on(cum_ready, V.tensor_tensor_scan(R[5], R[2], R[3], 0.0, ALU.mult, ALU.add))
            cum_ready.fire(V.tensor_scalar(R[6], R[5], -8.0, None, ALU.mult))
            for n in range(8):
                if n % 2 == 0:
                    wait_drained(dve, ("xbc", n // 2))
                step(V.tensor_scalar(xc[:, n, :], xbc[:, n, :], cw2[:, 3, n:n + 1], cb2[:, n:n + 1], ALU.mult, ALU.add))
                for k in (1, 2, 3):
                    ins = V.scalar_tensor_tensor(xc[:, n, k:T], xbc[:, n, 0:T - k], cw2[:, 3 - k, n:n + 1],
                                                 xc[:, n, k:T], ALU.mult, ALU.add)
                    conv2.fire(ins) if k == 3 else step(ins)
            dve.wait_ge(brow_loaded, 32)
            for tt in range(TT):
                ps = wait_filled(dve, ("z", tt))
                drains(V.tensor_tensor(z2[:, tt, :], ps[:, :], brow[:, 0:512], ALU.add), ("z", tt))
            for tt in range(TT):
                ps = wait_filled(dve, ("v", tt))
                drains(V.tensor_tensor(v2[:, tt, :], ps[:, :], brow[:, 512:1024], ALU.add), ("v", tt))
            drain_step(V.tensor_copy(dA[:, :, :], wait_filled(dve, ("tA",))[:, 0:64].rearrange("p (a b) -> p a b", a=4)), ("tA",))
            for g in range(2):
                ps = wait_filled(dve, ("cb", g))
                drains(V.tensor_tensor(cbm[:, g, :], ps[:, 0:384], C("ltri"), ALU.mult), ("cb", g))

            def finish2(tag):
                _, half, tt = tag
                c = row_coef()
                ps = wait_filled(dve, tag + ("o",))
                drains(V.tensor_tensor(heads(merged[:, tt, 512 + 256 * half:768 + 256 * half]), heads(ps[:, 0:256]),
                                       spread(c, HD), ALU.mult), tag + ("o",))

            for h in range(SH):
                ps = wait_filled(dve, ("Ab", h))
                if h >= 2:
                    dve.wait_ge(decay.sem, h - 1)
                V.tensor_scalar(seg[:, h % 2, 0:T], ps[:, 0:T], dA[:, 1, h:h + 1], 0.0, ALU.subtract, ALU.min)
                drains(V.tensor_scalar(seg[:, h % 2, T:T + P], ps[:, P:T], dA[:, 3, h:h + 1], 0.0, ALU.subtract, ALU.min),
                       ("Ab", h))
                if h % 2:
                    tag = GROUPS2[h // 2]
                    mask_and_max(tag, ncausal[:, tag[2], 0:(tag[2] + 1) * P])
                    if h > 1:
                        finish2(GROUPS2[h // 2 - 1])
            finish2(GROUPS2[-1])
            dve.wait_ge(xdt_ready.sem, 2)
            for tt in range(TT):
                ps = wait_filled(dve, ("y", tt))
                drain_step(V.tensor_tensor(merged[:, tt, 0:512], ps[:, :], xsN[:, tt, :], ALU.add), ("y", tt))
                dve.wait_ge(z_ready.sem, tt + 1)
                yz.fire(V.tensor_tensor(merged[:, tt, 0:512], merged[:, tt, 0:512], z2[:, tt, :], ALU.mult))
            dve.wait_ge(ysq.sem, 4)
            invert_mean_squares(256, 1e-5, rv[:, 0:4, 0], rv[:, 4:8, 0], yinv)
            dve.wait_ge(yrstd.sem, 1)
            for tt in range(TT):
                for g in range(2):
                    m = merged[:, tt, g * 256:(g + 1) * 256]
                    ins = V.tensor_scalar(m, m, rv[:, 8 + 2 * tt + g, 0:1], None, ALU.mult)
                merged_ready.fire(ins)
            for tt in range(TT):
                for hf in range(2):
                    copy_T(("mT", tt, hf), tt, hf, g8, mixT)

            def layer_norm(tt, residual, loaded, done, x):
                for hf in range(2):
                    residual(hf)
                s = coef2[:, :, tt:tt + 1]
                step(V.tensor_reduce(s[:, 0, :], x[:, tt, :], AX_X, ALU.add))
                step_on(ln_mu, V.tensor_scalar(s[:, 0, :], s[:, 0, :], -1.0 / D, None, ALU.mult))
                dve.wait_ge(ln_sq.sem, ln_mu.n)
                invert_mean_squares(D, 1e-5, s[:, 1, :], s[:, 2, :], ln_inv)
                dve.wait_ge(ln_rstd.sem, ln_mu.n)
                step(V.tensor_scalar(x[:, tt, :], x[:, tt, :], s[:, 0, :], s[:, 3, :], ALU.add, ALU.mult))
                dve.wait_ge(vec_loaded, loaded)
                step(V.tensor_tensor(x[:, tt, :], x[:, tt, :], vec[:, 0, :], ALU.mult))
                done.fire(V.tensor_tensor(x[:, tt, :], x[:, tt, :], vec[:, 1, :], ALU.add))

            def residual1(tt):
                def one(hf):
                    r = x[:, tt, hf * 512:(hf + 1) * 512]
                    ps = wait_filled(dve, ("wo", tt, hf))
                    drain_step(V.scalar_tensor_tensor(r, r, ALPHA, ps[:, :], ALU.mult, ALU.add), ("wo", tt, hf))
                return one

            for tt in range(TT):
                layer_norm(tt, residual1(tt), 16 * 3, h1_ready, x)
            for tt in range(TT):
                for hf in range(2):
                    copy_T(("h1T", tt, hf), tt, hf)
            for tt in range(TT):
                ps = wait_filled(dve, ("route", tt))
                drain_step(V.tensor_tensor(rl[:, tt, :], ps[:, 0:20], rb[:, :], ALU.add), ("route", tt))
            S = [rs[:, r, :, :] for r in range(12)]
            U = [rv[:, r, :] for r in range(12)]
            rank = C("rank")

            def first_of(dst, hit, m):
                step(V.tensor_tensor(dst, hit, repeat(rank, TT), ALU.mult))
                step(V.tensor_reduce(m, dst, AX_X, ALU.max))
                ins = V.tensor_tensor(dst, dst, spread(m, 4), ALU.is_equal)
                if dst is S[2]:
                    step_on(one_hot, ins)
                else:
                    step(ins)

            step(V.tensor_reduce(U[0], rl[:, :, 0:4], AX_X, ALU.max))
            step_on(r_in, V.tensor_tensor(S[0], rl[:, :, 0:4], spread(U[0], 4), ALU.subtract))
            step(V.tensor_scalar(S[2], S[0], 0.0, None, ALU.is_equal))
            first_of(S[2], S[2], U[1])
            dve.wait_ge(r_exp.sem, 1)
            step(V.tensor_reduce(U[2], S[1], AX_X, ALU.add))
            step(V.reciprocal(U[2], U[2]))
            for g in range(4):
                dst = S[3] if g == 0 else S[10]
                step(V.tensor_tensor(dst, rl[:, :, 4 + 4 * g:8 + 4 * g], spread(S[2][:, :, g], 4), ALU.mult))
                if g:
                    step(V.tensor_tensor(S[3], S[3], S[10], ALU.add))
            step(V.tensor_reduce(U[3], S[3], AX_X, ALU.max))
            step_on(r_in, V.tensor_tensor(S[4], S[3], spread(U[3], 4), ALU.subtract))
            step(V.tensor_scalar(S[6], S[4], 0.0, None, ALU.is_equal))
            first_of(S[6], S[6], U[4])
            step(V.tensor_scalar(S[7], S[6], BIG, None, ALU.mult))
            step(V.tensor_tensor(S[7], S[7], S[4], ALU.add))
            step(V.tensor_reduce(U[5], S[7], AX_X, ALU.max))
            step(V.tensor_tensor(S[8], S[7], spread(U[5], 4), ALU.is_equal))
            first_of(S[8], S[8], U[6])
            step(V.tensor_tensor(S[8], S[8], S[6], ALU.add))
            dve.wait_ge(r_exp.sem, 2)
            step(V.tensor_tensor(S[9], S[5], S[8], ALU.mult))
            step(V.tensor_reduce(U[7], S[9], AX_X, ALU.add))
            step(V.reciprocal(U[7], U[7]))
            step(V.tensor_tensor(U[7], U[7], U[2], ALU.mult))
            step(V.tensor_tensor(S[9], S[9], spread(U[7], 4), ALU.mult))
            ps = wait_filled(dve, ("rank",))
            ranks, counts = ps[:, 0:8].rearrange("p (a b) -> p a b", a=TT), ps[:, 8:12]
            Q = [grp[:, r_, :] for r_ in range(8)]
            step(V.tensor_copy(Q[0], counts))
            step(V.tensor_reduce(U[8][:, 0:1], Q[0], AX_X, ALU.max))
            step(V.tensor_scalar(Q[1], Q[0], U[8][:, 0:1], None, ALU.is_equal))
            step(V.tensor_tensor(Q[1], Q[1], rank, ALU.mult))
            step(V.tensor_reduce(U[8][:, 0:1], Q[1], AX_X, ALU.max))
            step(V.tensor_scalar(Q[1], Q[1], U[8][:, 0:1], None, ALU.is_equal))
            step(V.memset(Q[2], 1.0))
            step(V.tensor_tensor_scan(Q[3], Q[2], Q[1], 0.0, ALU.mult, ALU.add))
            step(V.tensor_scalar(Q[4], rank, -1.0, 4.0, ALU.mult, ALU.add))
            step(V.tensor_tensor(Q[5], Q[4], Q[3], ALU.add))
            step(V.tensor_tensor(Q[6], Q[4], Q[1], ALU.mult))
            step(V.tensor_reduce(U[8][:, 0:1], Q[6], AX_X, ALU.add))
            V.tensor_copy(order_i[:, 0:LAST], Q[5][:, 0:LAST])
            order_ready.fire(V.tensor_copy(order_i[:, LAST:GROUPS], U[8][:, 0:1]))
            step(V.tensor_tensor(Q[4], Q[4], Q[3], ALU.subtract))
            step(V.tensor_tensor(Q[4], Q[4], Q[1], ALU.add))
            step(V.scalar_tensor_tensor(Q[6], rank, -1.0, Q[1], ALU.add, ALU.mult))
            step(V.tensor_tensor(Q[4], Q[4], Q[6], ALU.add))
            step(V.tensor_scalar(Q[4], Q[4], float(P), None, ALU.mult))
            drain_step(V.tensor_tensor(S[10], ranks, repeat(Q[4], TT), ALU.add), ("rank",))
            step(V.tensor_tensor(S[10], S[10], S[2], ALU.mult))
            step(V.tensor_reduce(slot_of, S[10], AX_X, ALU.add))
            step(V.tensor_scalar(slot_of, slot_of, -1.0, None, ALU.add))

            def select(tile, before):
                for tt in range(TT):
                    ins = V.tensor_scalar(sel[tile][:, tt, :], C("iota"), slot_of[:, tt:tt + 1], None, ALU.is_equal)
                sel_ready.fire(ins)
                dve.wait_ge(sel_ready.sem, before + 1)
                V.tensor_scalar(slot_of, slot_of, -float(P), None, ALU.add).then_inc(next_tile.sem, 1)

            def take_gathered(n, k, tile):
                dve.wait_ge(filled[0], at(0, n, k + 1))
                V.tensor_copy(xg[tile][:, 0:4, :], psum[0][:, :].rearrange("p (a b) -> p a b", a=4)).then_inc(drained[0], 1)

            def take_selection(n, k, tile):
                dve.wait_ge(filled[7], at(7, n, k + 1))
                V.tensor_copy(combine[tile], psum[7][:, T:T + GE]).then_inc(combine_here.sem, 1)
                V.tensor_copy(selT[tile], psum[7][:, 0:T]).then_inc(drained[7], 1)

            def activate(n, s, e, tile):
                dve.wait_ge(drained[4], at(4, n, s + 1))
                dve.wait_ge(filled[5], at(5, n, s + 1))
                V.scalar_tensor_tensor(act_n, silu_g, combine[tile][:, e:e + 1], psum[5][:, :], ALU.mult, ALU.mult)\
                    .then_inc(drained[5], 1)

            def add_outputs(n, tiles, k7):
                for q in range(4):
                    b, tt, hf = 4 + q, q // 2, q % 2
                    dve.wait_ge(filled[b], at(b, n, (k7 if b == 7 else GE * tiles) + 1))
                    r = acc[:, tt, hf * 512:(hf + 1) * 512]
                    V.tensor_tensor(r, r, psum[b][:, :], ALU.add).then_inc(drained[b], 1)

            select(0, 0)
            step(V.tensor_scalar(acc[:, :, :], x[:, :, :], ALPHA, None, ALU.mult))
            take_gathered(0, 0, 0)
            with dve.Fori(0, LAST) as n:
                take_selection(n, 0, 0)
                dve.wait_ge(combine_here.sem, n + 1)
                dve.wait_ge(next_tile.sem, n + 1)
                select(0, n + 1)
                for e in range(GE):
                    activate(n, e, e, 0)
                take_gathered(n + 1, 0, 0)
                add_outputs(n, 1, 1)
            take_selection(LAST, 0, 0)
            dve.wait_ge(next_tile.sem, LAST + 1)
            select(1, LAST + 1)
            take_gathered(LAST + 1, 0, 1)
            take_selection(LAST, 1, 1)
            dve.wait_ge(combine_here.sem, GROUPS + 1)
            for s in range(2 * GE):
                activate(LAST, s, s // 2, s % 2)
            add_outputs(LAST, 2, 2)
            for b, k in zip(range(4, 8), (2 * GE, 2 * GE, 2 * GE, 2)):
                dve.wait_ge(drained[b], at(b, LAST, k + 1))
            for tt in range(TT):
                layer_norm(tt, lambda hf: None, 16 * 5, final_ready, acc)

        @block.scalar
        def _(act):
            def step(ins):
                astep.fire(ins)
                act.wait_ge(astep.sem, astep.n)

            def run(out_, in_, func=ACT.Copy, **kw):
                return nc.scalar.activation(out_, in_, func, **kw)

            act.dma_start(cst[:, :], a["shape_constants"][:, :]).then_inc(const_loaded, 16)
            small_dmas[0](act)

            def load_cmp(l):
                for n, name in enumerate(("w_cmp_k", "w_cmp_v")):
                    act.dma_start(pe2[0:32, n, :], a["pe_cmp"][l]).then_inc(cmp_loaded, 16)
                    act.dma_start(wcmp[n * HD:(n + 1) * HD, :, :], a[name][l].rearrange("(k d) e -> d k e", d=HD))\
                       .then_inc(cmp_loaded, 16)

            load_cmp(0)
            small_dmas[1](act)

            def root_of_mean_squares():
                for tt in range(TT):
                    sumsq.fire(run(hn[:, tt, :], x[:, tt, :], ACT.Square, accum_out=stat[:, 0, tt:tt + 1]))
                act.wait_ge(invms.sem, invms.n)
                rstd_s.fire(run(stat[:, 2, :], stat[:, 1, :], ACT.Sqrt))

            def halves(dst, ps, key, **kw):
                for j in range(2):
                    r = slice(j * HD, (j + 1) * HD)
                    ins = run(dst(j), ps[r], **kw)
                return ins

            group = [0]

            def exps(tag):
                g, tt = group[0], tag[2]
                group[0] += 1
                nk = (tt + 1) * P
                act.wait_ge(rmax.sem, g + 1)
                if g >= 2:
                    wait_filled(act, prev_groups[g - 2] + ("pT", prev_groups[g - 2][2]))
                for h in range(NH):
                    expd.fire(run(ex[:, g % 2, h, 0:nk], sm[:, g % 2, h, 0:nk], ACT.Exp, bias=mx[:, g % 2, h:h + 1],
                                  scale=HD ** -0.5, accum_out=sums[:, g % 2, h:h + 1]))

            prev_groups = [t for l in range(LAYERS) for t in layer_groups(l)] + GROUPS2
            gdone = [0]

            def evacuate_probs(tag):
                g = gdone[0]
                gdone[0] += 1
                if g >= 2:
                    wait_filled(act, prev_groups[g - 2] + ("o",))
                for kt in range(tag[2] + 1):
                    key = tag + ("pT", kt)
                    drains(run(exT[:, g % 2, kt, :], wait_filled(act, key)[:, :]), key)

            act.wait_ge(zeroed, ZEROED)
            for l in range(LAYERS + 1):
                if l == 0:
                    act.wait_ge(x_loaded, 16 * TT)
                else:
                    for tt in range(TT):
                        for hf in range(2):
                            wait_drained(act, (l - 1, "wo", tt, hf))
                for tt in range(TT):
                    sumsq.fire(run(hn[:, tt, :], x[:, tt, :], ACT.Square, accum_out=stat[:, 0, tt:tt + 1]))
                act.wait_ge(invms.sem, l + 1)
                rstd_s.fire(run(stat[:, 2, :], stat[:, 1, :], ACT.Sqrt))
                if l == LAYERS:
                    break
                for tt in range(TT):
                    key = (l, "idx", tt)
                    ps = wait_filled(act, key)
                    run(ni[:, tt, 0:256], ps[:, 0:256])
                    run(shaped(ni[:, tt, 256:384], 4, 32), repeat(ps[:, 256:288], 4))
                    drains(run(ni[:, tt, 384:392], ps[:, 288:296], scale=1.0 / 16.0), key)
                for tt in range(TT):
                    key = (l, "qkv", tt)
                    ps = wait_filled(act, key)
                    run(na[:, tt, 0:256], ps[:, 0:256])
                    run(shaped(na[:, tt, 256:384], 2, HD), repeat(ps[:, 256:320], 2))
                    drains(run(na[:, tt, 384:448], ps[:, 320:384]), key)
                for tt in range(TT):
                    key = (l, "idxT", tt)
                    ps = wait_filled(act, key)
                    tok = slice(tt * P, (tt + 1) * P)
                    run(qiT[:, :, tok], ps[:, 0:256].rearrange("p (a b) -> p a b", a=2))
                    for j in range(4):
                        r = slice(32 * j, 32 * j + 32)
                        ins = run(kiT[r, j, tok], ps[r, 256:384])
                    drains(ins, key)
                for tt in range(TT):
                    nk = (tt + 1) * P
                    if tt:
                        act.wait_ge(scored.sem, scored.at(l, tt))
                    for n in range(4):
                        key = (l, "logit", tt, n)
                        ps = wait_filled(act, key)
                        drains(run(relu[:, 2 * n:2 * n + 2, 0:nk], ps[:, 0:2 * nk].rearrange("p (a b) -> p a b", a=2), ACT.Relu),
                               key)
                for tt in range(TT):
                    key = (l, "bq", tt)
                    drains(run(nb[:, tt, 0:256], wait_filled(act, key)[:, 0:256]), key)
                drains(run(kvT[:, :], wait_filled(act, (l, "kcvc"))[:, 0:T]), (l, "kcvc"))
                for tt in range(TT):
                    key = (l, "bkv", tt)
                    ps = wait_filled(act, key)
                    run(shaped(nb[:, tt, 256:384], 2, HD), repeat(ps[:, 0:64], 2))
                    run(nb[:, tt, 512:576], ps[:, 64:128])
                    run(shaped(nb[:, tt, 384:512], 2, HD), repeat(ps[:, 128:192], 2))
                    drains(run(nb[:, tt, 576:652], ps[:, 192:268]), key)
                for tt in range(TT):
                    key = (l, "qkT_a", tt)
                    ps = wait_filled(act, key)
                    tok = slice(tt * P, (tt + 1) * P)
                    run(qaT[:, :, tok], ps[:, 0:256].rearrange("p (a b) -> p a b", a=2))
                    for j in range(2):
                        r = slice(HD * j, HD * j + HD)
                        ins = run(kaT[r, j, tok], ps[r, 256:384])
                    drains(ins, key)
                for tt in range(TT):
                    key = (l, "gates", tt)
                    drains(run(gsil[:, tt, :], wait_filled(act, key)[:, :], ACT.Silu), key)
                for tt in range(TT):
                    key = (l, "qkT_b", tt)
                    ps = wait_filled(act, key)
                    tok = slice(tt * P, (tt + 1) * P)
                    run(qbT[:, :, tok], ps[:, 0:256].rearrange("p (a b) -> p a b", a=2))
                    for m, dst in enumerate((ksT, kwT)):
                        for j in range(2):
                            r = slice(HD * j, HD * j + HD)
                            ins = run(dst[r, j, tok], ps[r, (2 + m) * P:(3 + m) * P])
                    drains(ins, key)
                ps = wait_filled(act, (l, "kcmp"))
                drains(run(shaped(kcN[0:CP, :], 2, HD), repeat(ps[0:CP, 0:HD], 2)), (l, "kcmp"))
                ps = wait_filled(act, (l, "vcmp"))
                for h in range(NH):
                    ins = run(vcB[CP * h:CP * h + CP, h, :], ps[0:CP, 0:HD])
                drains(ins, (l, "vcmp"))
                for name, dst, func in (("c_b", cbS, ACT.Copy), ("c_c", ccS, ACT.Copy), ("c_g", cgS, ACT.Silu),
                                        ("d_u", du[:, :, 16:], ACT.Copy), ("d_g", dg, ACT.Silu)):
                    ps = wait_filled(act, (l, name))
                    drains(run(dst[:, :, :], ps[:, :].rearrange("p (a b) -> p a b", a=2), func), (l, name))
                for tt in range(TT):
                    wait_drained(act, (l, "bkv", tt))
                    gexp.fire(run(gate[:, tt, :], nb[:, tt, 640:652], ACT.Exp, scale=-1.0))
                ps = wait_filled(act, (l, "kcT"))
                for j in range(2):
                    r = slice(HD * j, HD * j + HD)
                    ins = run(kcT[r, j, :], ps[r, 0:CP])
                drains(ins, (l, "kcT"))
                for tt in range(TT):
                    act.wait_ge(cmax.sem, cmax.at(l, tt + 1))
                    if tt:
                        wait_filled(act, (l, "cmp_pT", tt - 1))
                    cexp.fire(run(ec[:, :, :], smc[:, :, :], ACT.Exp, scale=HD ** -0.5))
                    drains(run(pcT[:, :], wait_filled(act, (l, "cmp_pT", tt))[:, 0:P]), (l, "cmp_pT", tt))
                act.wait_ge(conv_done.sem, conv_done.at(l, 1))
                for tag in layer_groups(l):
                    exps(tag)
                    evacuate_probs(tag)
                if l + 1 < LAYERS:
                    load_cmp(l + 1)
                else:
                    act.dma_start(vec[:, 0, :], row("final_norm_w").broadcast_to([P, D])).then_inc(vec_loaded, 16)
                act.wait_ge(b_done.sem, b_done.at(l, TT))
                for tt in range(TT):
                    key = (l, "mixT", tt)
                    ps = wait_filled(act, key)
                    drains(run(mixT[:, 0:4, tt * P:(tt + 1) * P], ps[:, :].rearrange("p (a b) -> p a b", a=4)), key)
            act.wait_ge(small2_loaded, SMALL2)
            act.wait_ge(coef_in.sem, 1)
            ps = wait_filled(act, ("dtf",))
            drains(run(dtf[0:16, 0, :], ps[0:16, 0:T], ACT.Identity, scale=C("sgn", rows=16), bias=b16[0:16, 2:3]), ("dtf",))
            wait_drained(act, ("dtf",))
            step(run(dtf[0:16, 1, :], dtf[0:16, 0, :], ACT.Abs))
            dt_exp.fire(run(dtf[0:16, 1, :], dtf[0:16, 1, :], ACT.Exp, scale=-1.0))
            dt_exp.fire(run(b16[0:16, 3:4], b16[0:16, 1:2], ACT.Exp))
            for n in range(4):
                ps = wait_filled(act, ("xbc", n))
                for j in range(2):
                    ins = run(xbc[:, 2 * n + j, :], ps[:, j * T:(j + 1) * T], ACT.Identity, bias=bx[:, 2 * n + j:2 * n + j + 1])
                drains(ins, ("xbc", n))
            act.wait_ge(dt_w.sem, 1)
            dt_ln.fire(run(dtf[0:16, 4, :], dtf[0:16, 2, :], ACT.Ln))
            for n in range(2):
                ps = wait_filled(act, ("q", n))
                for j in range(2):
                    ins = run(qT2[:, 2 * n + j, :], ps[:, j * T:(j + 1) * T], ACT.Identity, bias=bqk[:, 2 * n + j:2 * n + j + 1])
                drains(ins, ("q", n))
            act.wait_ge(k2_zeroed.sem, 1)
            for n in range(2):
                ps = wait_filled(act, ("k", n))
                for j in range(2):
                    for i in range(2):
                        r = slice(HD * i, HD * i + HD)
                        c = 4 + 2 * n + j
                        ins = run(kT2[r, 2 * n + j, i, :], ps[r, j * T:(j + 1) * T], ACT.Identity, bias=bqk[r, c:c + 1])
                drains(ins, ("k", n))
            for n in range(8):
                act.wait_ge(conv2.sem, n + 1)
                act2.fire(run(xc[:, n, :], xc[:, n, :], ACT.Silu))
            for tt in range(TT):
                wait_drained(act, ("z", tt))
                z_ready.fire(run(z2[:, tt, :], z2[:, tt, :], ACT.Silu))
            for tt in range(TT):
                drains(run(xsN[:, tt, :], wait_filled(act, ("xs", tt))[:, :]), ("xs", tt))
            for h in range(SH):
                wait_drained(act, ("Ab", h))
                dec_e.fire(run(seg[:, h % 2, :], seg[:, h % 2, :], ACT.Exp))
                if h % 2:
                    if h > 1:
                        evacuate_probs(GROUPS2[h // 2 - 1])
                    exps(GROUPS2[h // 2])
            evacuate_probs(GROUPS2[-1])
            for n, name in enumerate(("ln1_g_2", "ln1_b_2")):
                act.dma_start(vec[:, n, :], a[name].broadcast_to([P, D])).then_inc(vec_loaded, 16)
            for tt in range(TT):
                act.wait_ge(yz.sem, tt + 1)
                for g in range(2):
                    ysq.fire(run(xc[:, 2 * tt + g, :], merged[:, tt, g * 256:(g + 1) * 256],
                                 ACT.Square, accum_out=rv[:, 2 * tt + g, 0:1]))
            act.wait_ge(yinv.sem, 1)
            yrstd.fire(run(rv[:, 8:12, 0], rv[:, 4:8, 0], ACT.Sqrt))

            def layer_norm(tt, n, x):
                act.wait_ge(ln_mu.sem, n)
                ln_sq.fire(run(hn[:, tt, :], x[:, tt, :], ACT.Square, bias=coef2[:, 0, tt:tt + 1],
                               accum_out=coef2[:, 1, tt:tt + 1]))
                act.wait_ge(ln_inv.sem, n)
                ln_rstd.fire(run(coef2[:, 3, tt:tt + 1], coef2[:, 2, tt:tt + 1], ACT.Sqrt))

            for tt in range(TT):
                layer_norm(tt, tt + 1, x)
            act.wait_ge(h1_ready.sem, TT)
            for n, name in enumerate(("ln2_g_2", "ln2_b_2")):
                act.dma_start(vec[:, n, :], a[name].broadcast_to([P, D])).then_inc(vec_loaded, 16)
            for n in range(2):
                act.wait_ge(r_in.sem, n + 1)
                r_exp.fire(run(rs[:, 1 + 4 * n, :, :], rs[:, 4 * n, :, :], ACT.Exp))

            def take_gathered(n, k, tile):
                act.wait_ge(filled[1], at(1, n, k + 1))
                run(xg[tile][:, 4:8, :], psum[1][:, :].rearrange("p (a b) -> p a b", a=4)).then_inc(drained[1], 1)

            def silu_gate(n, s):
                act.wait_ge(filled[4], at(4, n, s + 1))
                act.wait_ge(drained[5], at(5, n, s))
                run(silu_g, psum[4][:, :], ACT.Silu).then_inc(drained[4], 1)

            def take_act(n, s):
                act.wait_ge(filled[6], at(6, n, s + 1))
                run(actT, psum[6][:, :].rearrange("p (a b) -> p a b", a=FT)).then_inc(drained[6], 1)

            def take_outputs(down_count, banks, counts, tile):
                act.wait_ge(filled[2], down_count)
                for hf, b in enumerate(banks):
                    run(yS[tile][:, hf * 512:(hf + 1) * 512], psum[b][:, :]).then_inc(drained[b], 1)

            take_gathered(0, 0, 0)
            with act.Fori(0, LAST) as n:
                silu_gate(n, 0)
                for e in range(1, GE):
                    silu_gate(n, e)
                    take_act(n, e - 1)
                take_gathered(n + 1, 0, 0)
                take_act(n, GE - 1)
                take_outputs(at(2, n, GE), (2, 3), None, 0)
            take_gathered(LAST + 1, 0, 1)
            silu_gate(LAST, 0)
            for s in range(1, 2 * GE):
                silu_gate(LAST, s)
                take_act(LAST, s - 1)
            take_outputs(at(2, LAST, 2 * GE - 1), (2, 3), None, 0)
            take_act(LAST, 2 * GE - 1)
            take_outputs(at(2, LAST, 2 * GE), (0, 1), None, 1)
            for tt in range(TT):
                layer_norm(tt, TT + tt + 1, acc)

        @block.gpsimd
        def _(pool):
            G = nc.gpsimd

            def step(ins):
                gstep.fire(ins)
                pool.wait_ge(gstep.sem, gstep.n)

            def rope(buf, n, half, cos, sin, signal):
                rows = buf.shape[0]
                t1, t2 = (shaped(rt[0:rows, k, :], n, 2 * half) for k in range(2))
                w = buf[:, :, 0:2 * half]
                G.tensor_tensor(t1, w, repeat(cos, n), ALU.mult)
                step(G.tensor_tensor(t2, w, repeat(sin, n), ALU.mult))
                G.tensor_tensor(w[:, :, 0:half], t1[:, :, 0:half], t2[:, :, half:2 * half], ALU.add)
                signal.fire(G.tensor_tensor(w[:, :, half:2 * half], t1[:, :, half:2 * half], t2[:, :, 0:half], ALU.add))
                pool.wait_ge(signal.sem, signal.n)

            zero_list = (zero[:, :], kiT, kaT, ksT, kwT, blk, vcB, kcT, du, b16, pw[:, :, :, :], pe2, kcN, dtf[:, 7:8, 0:1])
            assert len(zero_list) == ZEROED
            for v in zero_list:
                pool.memset(v, 0.0).then_inc(zeroed, 1)
            pool.wait_ge(zeroed, ZEROED)
            pool.memset(g8[:, 4:8], 1.0).then_inc(g8_ones.sem, 1)
            pool.wait_ge(const_loaded, 16)
            for l in range(LAYERS):
                for tt in range(TT):
                    wait_drained(pool, (l, "idx", tt))
                    rope(shaped(ni[:, tt, 0:384], 12, 32), 12, 4, cos32[:, tt, :], sin32[:, tt, :], roped_i)
                for tt in range(TT):
                    wait_drained(pool, (l, "qkv", tt))
                    rope(shaped(na[:, tt, 0:384], 6, HD), 6, 8, cos64[:, tt, :], sin64[:, tt, :], roped_a)
                for tt in range(TT):
                    wait_drained(pool, (l, "bq", tt))
                    wait_drained(pool, (l, "bkv", tt))
                    rope(shaped(nb[:, tt, 0:512], 8, HD), 8, 8, cos64[:, tt, :], sin64[:, tt, :], roped_b)
                wait_drained(pool, (l, "kcmp"))
                rope(shaped(kcN[0:CP, :], 2, HD), 2, 8, C("cosc", rows=CP), C("sinc", rows=CP), roped_c)
                wait_drained(pool, (l, "d_u"))
                pool.wait_ge(scored.sem, scored.at(l, TT))
                E = T + 16
                step(G.tensor_tensor(d2[:, :, 1:E], du[:, :, 1:E], du[:, :, 0:E - 1], ALU.add))
                step(G.tensor_tensor(d4[:, :, 4:E], d2[:, :, 4:E], d2[:, :, 2:E - 2], ALU.add))
                step(G.tensor_tensor(d2[:, 1, 8:E], d4[:, 1, 8:E], d4[:, 1, 4:E - 4], ALU.add))
                step(G.tensor_tensor(d4[HD:P, 1, 16:E], d2[HD:P, 1, 16:E], d2[HD:P, 1, 8:E - 8], ALU.add))
                dp = mixT[:, 6:8, :]
                G.tensor_tensor(dp[0:HD], d2[0:HD, :, 16:E], icnt[0:HD], ALU.mult)
                step(G.tensor_tensor(dp[HD:P], d4[HD:P, :, 16:E], icnt[HD:P], ALU.mult))
                pooled.fire(G.tensor_tensor(dp, dp, du[:, :, 16:E], ALU.subtract))
                pool.wait_ge(conv_y.sem, conv_y.at(l, 1))
                wait_drained(pool, (l, "c_b"))
                wait_drained(pool, (l, "c_g"))
                step(G.tensor_tensor(cy, cy, cbS, ALU.mult))
                conv_done.fire(G.tensor_tensor(cy, cy, cgS, ALU.mult))
                for tt in range(TT):
                    wait_drained(pool, (l, "win", tt, "o"))
                    m = mixN[:, tt, 256:512]
                    step(G.tensor_tensor(m, m, ob[:, tt, 0, :], ALU.add))
                    step(G.tensor_tensor(m, m, ob[:, tt, 1, :], ALU.add))
                    b_done.fire(G.tensor_tensor(m, m, gsil[:, tt, 256:512], ALU.mult))
            pool.wait_ge(h0_ready.sem, TT)
            for n, c in enumerate((Z2, V2)):
                pool.dma_start(brow[:, n * 512:(n + 1) * 512], a["b_in_2"][:, c:c + 512].broadcast_to([P, 512]))\
                    .then_inc(brow_loaded, 16)
            k2_zeroed.fire(G.memset(kT2, 0.0))
            wait_drained(pool, ("tA",))
            for tt in range(TT):
                wait_drained(pool, ("xs", tt))
                ins = G.tensor_tensor(shaped(xdt[:, tt, :], SH, HD), shaped(xsN[:, tt, :], SH, HD),
                                      spread(dA[:, 2 * tt, 0:SH], HD), ALU.mult)
            xdt_ready.fire(ins)
            pool.wait_ge(xdt_ready.sem, 1)
            for tt in range(TT):
                v = shaped(xsN[:, tt, :], SH, HD)
                ins = G.tensor_tensor(v, v, spread(dsk, HD), ALU.mult)
            xdt_ready.fire(ins)
            for g in range(2):
                wait_drained(pool, ("cb", g))
            for h in range(SH):
                pool.wait_ge(dec_e.sem, h + 1)
                if h >= 2:
                    pool.wait_ge(y_used.sem, h - 1)
                decay.fire(G.tensor_tensor(mTh[:, h % 2, :], seg[:, h % 2, :], cbm[:, h // 4, :], ALU.mult))


_INPUTS = ["x", "norm_w", "w_in", "w_out", "conv_w", "pe_cmp", "w_cmp_k", "w_cmp_v", "pool_w", "pool_scale", "final_norm_w",
           "w_in_2", "b_in_2", "conv_w_2", "conv_b_2", "a_log_2", "d_skip_2", "ssd_norm_g_2", "w_out_2", "ln1_g_2",
           "ln1_b_2", "router_group_w_2", "router_group_b_2", "router_expert_w_2", "router_expert_b_2", "w_gate_2",
           "w_up_2", "w_down_2", "ln2_g_2", "ln2_b_2"]


def kernel(**inputs):
    import concourse.bacc as bacc
    from concourse.bass_utils import run_bass_kernel_spmd

    nc = bacc.Bacc("TRN2", target_bir_lowering=False, num_devices=1)
    arrays = {n: np.ascontiguousarray(inputs[n]) for n in _INPUTS}
    arrays["shape_constants"] = shape_constants()
    feeds, aps = {}, {}
    for n, v in arrays.items():
        feeds[f"in_{n}"] = v
        aps[n] = nc.dram_tensor(f"in_{n}", v.shape, mybir.dt.from_np(v.dtype), kind="ExternalInput").ap()
    out = nc.dram_tensor("out", (1, T, D), F32, kind="ExternalOutput").ap()
    build(nc, aps, out)
    r = run_bass_kernel_spmd(nc, [feeds], core_ids=[0])
    return r.results[0]["out"]
```

```python
from contextlib import ExitStack

import concourse.bass as bass
import concourse.mybir as mybir
import numpy as np

F32 = mybir.dt.float32
ALU = mybir.AluOpType
ACT = mybir.ActivationFunctionType
AX_X = mybir.AxisListType.X

P = 128
T = 256
TT = T // P
D = 1024
KT = D // P
LAYERS = 2
EPS = 1e-6
HD = 64
NH = 4
TOPK = 64
NCMP = 15
CP = 32
BIG = -1.0e30
TAKEN = -3.0e38
TINY = 1.0e-38
ROPE_THETA = 500000.0

A_Q, A_QI, A_GATE = 0, 384, 680
B_Q, B_KS, B_GATE = 936, 1320, 1588
C_B, C_X, D_U = 1844, 2356, 2868
Z2, XBC2, DT2, Q2, K2, V2, F2 = 0, 512, 1536, 1544, 2056, 2568, 3080
SH = 8
ALPHA = 2.0 ** 0.25
EXPERTS, GROUPS, FF = 16, 4, 512
GE = EXPERTS // GROUPS
FT = FF // P
SLOTS = 3
UNIT = 1024
UNITS = 3
PER_SLOT = KT * 512 // UNIT
SLOT = KT * 512
ZEROED = 13
SMALL = 16 * 14
SMALL2 = 16 * 21
ARENA = 12584

CONST = {}
CONST_W = 0
for _name, _w in (("ident", 128), ("ncausal", 512), ("cos64", 32), ("sin64", 32), ("cos32", 16), ("sin32", 16),
                  ("cosc", 16), ("sinc", 16), ("cinv", 64), ("cval", 64), ("icnt", 512), ("ltri", 384),
                  ("sgn", 1), ("rank", 4), ("iota", 128)):
    CONST[_name] = (CONST_W, _w)
    CONST_W += _w


def shape_constants():
    c = np.zeros((P, CONST_W), np.float32)

    def put(name, a, rows=P):
        o, w = CONST[name]
        c[:rows, o:o + w] = np.asarray(a, np.float32).reshape(rows, w)

    p = np.arange(P)
    t = np.arange(TT)[None, :] * P + p[:, None]
    put("ident", np.eye(P))
    put("ncausal", np.arange(T)[None, None, :] > t[:, :, None])

    def angles(pos, half):
        inv = (np.float32(ROPE_THETA) ** (-np.arange(half, dtype=np.float32) / np.float32(half))).astype(np.float32)
        a = pos.astype(np.float32)[..., None] * inv
        return np.concatenate([np.cos(a), np.cos(a)], -1), np.concatenate([np.sin(a), -np.sin(a)], -1)

    for half, name in ((8, "64"), (4, "32")):
        co, si = angles(t, half)
        put("cos" + name, co)
        put("sin" + name, si)
    n = np.arange(CP)
    co, si = angles(16 * n + 31, 8)
    put("cosc", co, CP)
    put("sinc", si, CP)
    inv = (16 * n + 31)[None, None, :] > t[:, :, None]
    inv |= (n >= NCMP)[None, None, :]
    put("cinv", inv)
    put("cval", ~inv)
    win = np.array([[2, 8], [4, 16]])[p // 64]
    put("icnt", 1.0 / np.minimum(np.arange(T)[None, None, :] + 1, win[:, :, None]))
    put("ltri", np.concatenate([p[:, None] <= np.arange(T)[None, :], p[:, None] <= p[None, :]], 1))
    put("sgn", np.where(p < SH, 1.0, -1.0))
    put("rank", np.broadcast_to([4.0, 3.0, 2.0, 1.0], (P, 4)))
    put("iota", np.broadcast_to(np.arange(P), (P, P)))
    return c


SPLIT_COLUMNS = {"d_u": ("w_d", 0), "d_g": ("w_d", 256), "c_c": ("w_c1", 256), "c_x": ("w_c2", 0),
                 "c_b": ("w_c1", 0), "c_g": ("w_c2", 256),
                 ("xbc", 0): ("xbc0", 0), ("xbc", 1): ("xbc0", 256), ("xbc", 2): ("xbc1", 0), ("xbc", 3): ("xbc1", 256),
                 ("q", 0): ("q", 0), ("q", 1): ("q", 256), ("k", 0): ("k", 0), ("k", 1): ("k", 256)}
JOB_UNITS = 2
SPLIT_ROWS = ("z", "v", "wo0", "wo1")
ROW_UNITS = 4
BETWEEN_GROUPS = ("c_c", "c_x", "c_b", "c_g", "pool")
SPLIT_BETWEEN = sum(name in SPLIT_COLUMNS for name in BETWEEN_GROUPS)


def psum_plan():
    plan, order, fills, reads, turn, by_units, units = {}, [], [0] * 8, [0] * 8, {}, {}, [0]

    def job(key, banks=tuple(range(8))):
        b = banks[turn.get(banks, 0) % len(banks)]
        turn[banks] = turn.get(banks, 0) + 1
        plan[key] = (b, fills[b], reads[b])
        reads[b] += 1
        if key in SPLIT_COLUMNS or key[-1] in SPLIT_COLUMNS:
            units[0] += JOB_UNITS
            by_units[key] = units[0]
        elif len(key) > 1 and key[-2] in SPLIT_ROWS:
            units[0] += ROW_UNITS * (key[-1] == 0)
            by_units[key] = units[0]
        else:
            fills[b] += 1
        order.append(key)

    def scores(tag, banks=tuple(range(8))):
        for p in range(2):
            job(tag + ("s", p), banks)

    def outputs(tag, banks=tuple(range(8))):
        for kt in range(tag[2] + 1):
            job(tag + ("pT", kt), banks)
        job(tag + ("o",), banks)

    for l in range(LAYERS):
        for tt in range(TT):
            for hf in range(2):
                job((l, "hT", tt, hf))
        job((l, "peT"))
        for name in ("idx", "qkv"):
            for tt in range(TT):
                job((l, name, tt))
        for tt in range(TT):
            job((l, "idxT", tt))
        for tt in range(TT):
            for n in range(4):
                job((l, "logit", tt, n))
        for tt in range(TT):
            job((l, "bq", tt))
        job((l, "kcvc"))
        for tt in range(TT):
            job((l, "bkv", tt))
        for tt in range(TT):
            job((l, "qkT_a", tt))
        job((l, "gates", 0))
        for tt in range(TT):
            job((l, "qkT_b", tt))
        for name in ("kcmp", "vcmp"):
            job((l, name))
        job((l, "d_u"))
        job((l, "gates", 1))
        job((l, "kcT"))
        for tt in range(TT):
            job((l, "cmp_s", tt))
        job((l, "d_g"))
        for tt in range(TT):
            job((l, "cmp_pT", tt))
            job((l, "cmp_o", tt))
        groups = layer_groups(l)
        scores(groups[0])
        for n, tag in enumerate(groups):
            if n + 1 < len(groups):
                scores(groups[n + 1])
            if n < len(BETWEEN_GROUPS):
                job((l, BETWEEN_GROUPS[n]))
            outputs(tag)
        for tt in range(TT):
            job((l, "mixT", tt))
        for hf in range(2):
            for tt in range(TT):
                job((l, f"wo{hf}", tt))
    for tt in range(TT):
        for hf in range(2):
            job(("hT", tt, hf))
    job(("dtf",))
    for n in range(4):
        job(("xbc", n))
    for name in ("q", "k", "z", "v"):
        for n in range(2):
            job((name, n))
    job(("tA",))
    for tt in range(TT):
        job(("xs", tt))
    for g in range(2):
        job(("cb", g))
    for n in range(TT):
        job(("y", n), (0, 1))
    scores(GROUPS2[0], (5, 6, 7))
    for h in range(SH):
        job(("Ab", h), (2, 3, 4))
        if h % 2:
            n = h // 2
            if n + 1 < len(GROUPS2):
                scores(GROUPS2[n + 1], (5, 6, 7))
            outputs(GROUPS2[n], (5, 6, 7))
    for tt in range(TT):
        job(("mT", tt, 1), (2, 3))
    for tt in range(TT):
        for hf in range(2):
            job(("wo", tt, hf), (4, 5, 6, 7))
    for tt in range(TT):
        job(("mT", tt, 0), (2, 3))
    for tt in range(TT):
        for hf in range(2):
            job(("h1T", tt, hf))
    for tt in range(TT):
        job(("route", tt))
    job(("rank",))
    return plan, order, fills, reads, by_units


def layer_groups(l):
    return [(l, branch, tt) for branch in ("slc", "win", "dsa") for tt in range(TT)]


GROUPS2 = [("att", half, tt) for half in range(2) for tt in range(TT)]


def weight_plan(a):
    w = []

    def cols(m, *ranges):
        out, at = [], 0
        for lo, n in ranges:
            out.append((at, m.rearrange("(p k) n -> p k n", k=KT)[:, :, lo:lo + n]))
            at += n
        return out

    def half(m, n):
        return [(0, m.rearrange("(k p) n -> p k n", p=P)[:, :, n * 512:n * 512 + 512])]

    for l in range(LAYERS):
        m, o = a["w_in"][l], a["w_out"][l]
        w += [((l, "w_idx"), cols(m, (A_QI, 296)), (l, "idx", 1)),
              ((l, "w_qkv"), cols(m, (A_Q, 384)), (l, "qkv", 1)),
              ((l, "w_bq"), cols(m, (B_Q, 384)), (l, "kcvc")),
              ((l, "w_bkv"), cols(m, (B_KS, 268)), (l, "bkv", 1)),
              ((l, "w_gates"), cols(m, (A_GATE, 256), (B_GATE, 256)), (l, "gates", 1)),
              ((l, "w_d"), cols(m, (D_U, 512)), (l, "d_g")),
              ((l, "w_c1"), cols(m, (C_B, 512)), (l, "c_b")),
              ((l, "w_c2"), cols(m, (C_X, 512)), (l, "c_g")),
              ((l, "w_out0"), half(o, 0), (l, "wo0", 1)),
              ((l, "w_out1"), half(o, 1), (l, "wo1", 1))]
    m, o = a["w_in_2"][0], a["w_out_2"][0]
    w += [(("xbc0",), cols(m, (XBC2, 512)), ("xbc", 1)),
          (("xbc1",), cols(m, (XBC2 + 512, 512)), ("xbc", 3)),
          (("q",), cols(m, (Q2, 512)), ("q", 1)),
          (("k",), cols(m, (K2, 512)), ("k", 1)),
          (("z",), cols(m, (Z2, 512)), ("z", 1)),
          (("v",), cols(m, (V2, 512)), ("v", 1)),
          (("out0",), half(o, 0), ("wo", 1, 0)),
          (("out1",), half(o, 1), ("wo", 1, 1))]
    return w


def build(nc, a, out):
    plan, order, fills_used, reads_used, by_units = psum_plan()
    ctx = ExitStack()
    with ctx:
        def sb(name, *shape):
            return ctx.enter_context(nc.sbuf_tensor(name, [P, *shape], F32))

        def sem(name):
            return ctx.enter_context(nc.semaphore(name))

        def shaped(flat, *shape):
            names = "abcd"[:len(shape)]
            n = int(np.prod(shape))
            if len(shape) == 1:
                return flat[:, 0:n]
            return flat[:, 0:n].rearrange("p (" + " ".join(names) + ") -> p " + " ".join(names),
                                          **dict(zip(names[1:], shape[1:])))

        class Region:

            def __init__(self, flat, width):
                self.flat, self.width, self.at = flat, width, 0

            def take(self, *shape):
                n = int(np.prod(shape))
                assert self.at + n <= self.width, (self.at, n, self.width)
                v = shaped(self.flat[:, self.at:self.at + n], *shape)
                self.at += n
                return v

        psum = [ctx.enter_context(nc.psum_tensor(f"bank{b}", [P, 512], F32)) for b in range(8)]
        ring = sb("weight_ring", SLOTS, SLOT)
        cst = sb("shape_constants_sb", CONST_W)
        F32R = mybir.dt.float32r
        unit_hi, unit_lo = (ctx.enter_context(nc.sbuf_tensor(n, [P, UNITS, UNIT], F32R)) for n in ("unit_high", "unit_low"))
        xg_hi, xg_lo = (ctx.enter_context(nc.sbuf_tensor(n, [P, KT, T], F32R)) for n in ("tokens_high", "tokens_low"))
        act_hi, act_lo = (ctx.enter_context(nc.sbuf_tensor(n, [P, TT, FT, P], F32R)) for n in ("act_high", "act_low"))
        x = sb("residual_stream", TT, D)
        hn_f, hT_f, mixT_f, ex_f, exT_f = (sb(n, TT * D) for n in ("normed", "normed_T", "mixed_T", "probs", "probs_T"))
        hn = shaped(hn_f, TT, D)
        hT = shaped(hT_f, KT, T)
        mixT = shaped(mixT_f, KT, T)
        sm = shaped(hT_f, 2, NH, T)
        ex = shaped(ex_f, 2, NH, T)
        exT = shaped(exT_f, 2, TT, NH * P)
        arena = sb("arena", ARENA)

        small = Region(sb("small_vectors", 754), 754)
        stat = small.take(4, TT)
        normw = small.take(LAYERS, KT)
        rt = sb("rope_scratch", 2, 192)
        top8 = small.take(8)
        mx, sums, coef = (small.take(2, NH) for _ in range(3))
        cmx, csum = small.take(NH), small.take(NH)
        gate = small.take(TT, 12)
        cw = small.take(LAYERS, 3, 2)
        psc = small.take(LAYERS, 2)
        wdtf = small.take(KT, 16)
        b16 = small.take(4)
        dA = small.take(4, 16)
        bx, bqk = small.take(8), small.take(8)
        cw2 = small.take(4, 8)
        cb2 = small.take(8)
        g8 = small.take(KT)
        dsk = small.take(SH)
        wr = small.take(KT, 20)
        rb = small.take(20)
        rl = small.take(TT, 20)
        rs = small.take(12, TT, 4)
        rv = small.take(12, TT)
        grp = small.take(8, 4)
        slot_of = small.take(TT)
        coef2 = small.take(4, TT)
        pw = sb("pool_w_blocks", LAYERS, 2, P)

        A = Region(arena, ARENA)
        ni, na, nb = A.take(TT, 392), A.take(TT, 448), A.take(TT, 652)
        kiT = A.take(4, T)
        kaT, ksT, kwT = (A.take(2, T) for _ in range(3))
        qaT, qbT = A.take(2, T), A.take(2, T)
        amask = A.take(TT, T)
        kvT = A.take(T)
        blk = A.take(32, CP)
        pe2, peT = A.take(2, HD), A.take(32)
        kcN = A.take(2 * HD)
        kcT = A.take(2, CP)
        vcB = A.take(NH, HD)
        gsil = A.take(TT, 512)
        mixN = A.take(TT, 512)
        cgS = A.take(2, T)
        du = A.take(2, T + 16)
        dg = A.take(2, T)
        wcmp = shaped(ex_f, 32, HD)
        over = Region(exT_f, TT * D)
        qiT, score = over.take(2, T), over.take(2, T)
        ccS, cbS = kiT[:, 0:2, :], kiT[:, 2:4, :]
        over = Region(exT_f[:, 512:1024], 512)
        smc, ec, pcT = over.take(NH, CP), over.take(NH, CP), over.take(P)
        relu = shaped(hn_f, 8, T)
        over = Region(hn_f, TT * D)
        d2, d4, cu = over.take(2, T + 16), over.take(2, T + 16), over.take(2, T)
        ob = shaped(mixT_f, TT, 2, 256)
        cy = mixT[:, 4:6, :]

        B = Region(arena, ARENA)
        xc = B.take(8, T)
        kT2 = B.take(4, 2, T)
        qT2 = B.take(4, T)
        v2, z2 = B.take(TT, 512), B.take(TT, 512)
        cbm, seg, mTh = B.take(2, 384), B.take(2, 384), B.take(2, 384)
        dtf = B.take(8, T)
        brow = B.take(1024)
        xbc = shaped(exT_f, 8, T)
        xsN, xdt = shaped(mixT_f, TT, 512), shaped(mixT_f[:, 1024:2048], TT, 512)
        vec = shaped(ex_f, 2, D)
        merged = hn
        M = Region(arena, ARENA)
        sel = [M.take(TT, P) for _ in range(2)]
        selT = [M.take(T) for _ in range(2)]
        combine = [M.take(GE) for _ in range(2)]
        yS = [M.take(D) for _ in range(2)]
        silu_g, act_n = ([M.take(FF) for _ in range(2)] for _ in range(2))
        acc = shaped(exT_f, TT, D)
        order_i = ctx.enter_context(nc.sbuf_tensor("group_order", [P, GROUPS], mybir.dt.int32))

        def C(name, rows=P, a_=None):
            o, w = CONST[name]
            v = cst[0:rows, o:o + w]
            return v.rearrange("p (a b) -> p a b", a=a_) if a_ else v

        ident = C("ident")
        ncausal, cos64, sin64, cos32, sin32, cinv, cval, icnt = (
            C(n, a_=2) for n in ("ncausal", "cos64", "sin64", "cos32", "sin32", "cinv", "cval", "icnt"))

        def spread(ap, n):
            return ap.unsqueeze(2).broadcast_to([ap.shape[0], ap.shape[1], n])

        def repeat(ap, n):
            return ap.unsqueeze(1).broadcast_to([ap.shape[0], n, ap.shape[1]])

        filled = [sem(f"bank{b}_filled") for b in range(8)]
        drained = [sem(f"bank{b}_drained") for b in range(8)]
        slot_here = [sem(f"slot{s}_loaded") for s in range(SLOTS)]

        class Signal:

            def __init__(self, name, per=0):
                self.sem, self.n, self.per = sem(name), 0, per

            def fire(self, ins):
                self.n += 1
                return ins.then_inc(self.sem, 1)

            def at(self, l, k):
                return l * self.per + k

        x_loaded, const_loaded, small_loaded, small2_loaded = (sem(n) for n in (
            "x_loaded", "constants_loaded", "layer_vectors_loaded", "second_vectors_loaded"))
        cmp_loaded, vec_loaded, brow_loaded, stored = (sem(n) for n in (
            "cmp_weights_loaded", "row_vectors_loaded", "z_v_bias_rows_loaded", "output_stored"))
        zeroed = sem("pads_zeroed")
        vstep, astep, gstep = Signal("vector_step"), Signal("scalar_step"), Signal("pool_step")
        sumsq, invms, rstd_s = Signal("squares_summed", TT), Signal("mean_squares_inverted", 1), Signal("rstd_ready", 1)
        normed = Signal("normed_ready", TT)
        scored = Signal("index_scores_ready", TT)
        roped_i, roped_a, roped_b = Signal("idx_roped", TT), Signal("a_roped", TT), Signal("b_roped", TT)
        roped_c, blocks = Signal("kcmp_roped", 1), Signal("cmp_blocks_ready", 1)
        cmax, cexp, cprob = Signal("cmp_max_taken", TT), Signal("cmp_exp_done", TT), Signal("cmp_probs_ready", TT)
        gexp = Signal("branch_gates_exp", TT)
        rmax, expd = Signal("group_max_ready", 6), Signal("group_exp_done", 6 * NH)
        pooled, conv_y, conv_done = Signal("pooled_ready", 1), Signal("conv_taps_summed", 1), Signal("conv_into_mixed", 1)
        b_done = Signal("b_into_mixed", TT)
        mixr = Signal("mixed_natural_ready", TT)
        h0_ready = Signal("h0_ready")
        coef_in, cum_ready = Signal("dt_f_steps"), Signal("cumsums_ready")
        dt_exp, dt_w, dt_ln = Signal("dt_f_exp"), Signal("dt_f_one_plus"), Signal("dt_f_ln")
        conv2, act2 = Signal("xbc_taps_summed"), Signal("xbc_silu_ready")
        z_ready, xdt_ready = Signal("z_silu_ready"), Signal("xdt_ready")
        dec_e, decay, y_used = Signal("decay_exp"), Signal("decay_products"), Signal("y_head_done")
        ysq, yinv, yrstd = Signal("y_squares"), Signal("y_inverted"), Signal("y_rstd")
        merged_ready, ln_mu, ln_sq, ln_inv, ln_rstd = (Signal(n) for n in (
            "merged_ready", "ln_centred", "ln_squares", "ln_inverted", "ln_rstd"))
        h1_ready, final_ready = Signal("h1_ready"), Signal("output_rows_ready")
        r_in, r_exp, one_hot = Signal("router_shifted"), Signal("router_exp"), Signal("group_one_hot_ready")
        next_tile, combine_here = Signal("slots_moved_on"), Signal("slot_weights_here")
        order_ready, sel_ready = Signal("group_order_ready"), Signal("slot_selection_ready")
        yz, k2_zeroed, g8_ones = Signal("y_gated"), Signal("k2_blocks_zeroed"), Signal("merge_ones")

        def row(name):
            return a[name].rearrange("(o n) -> o n", o=1)

        def load_layer_vectors(eng):
            pairs, blocks_ = [], []
            for l in range(LAYERS):
                pairs += [(normw[:, l, :], a["norm_w"][l].rearrange("(p k) -> p k", k=KT)),
                          (psc[:, l, :], a["pool_scale"][l].rearrange("(c p) -> p c", p=P))]
                pairs += [(cw[:, l, j, :], a["conv_w"][l, j].rearrange("(c p) -> p c", p=P)) for j in range(3)]
                for h in range(2):
                    r = slice(HD * h, HD * h + HD)
                    blocks_.append((pw[r, l, :, r], a["pool_w"][l].rearrange("(j h) c d -> h c j d", h=2)[h]))
            for dst, src in pairs:
                eng.dma_start(dst, src, allow_slow_non_contiguous=True).then_inc(small_loaded, 16)
            eng.wait_ge(zeroed, ZEROED)
            for dst, src in blocks_:
                eng.dma_start(dst, src, allow_slow_non_contiguous=True).then_inc(small_loaded, 16)
            assert SMALL == 16 * len(pairs + blocks_)

        def load_second_vectors(eng):
            wi = a["w_in_2"][0].rearrange("(p k) n -> p k n", k=KT)
            bi = a["b_in_2"][0]
            col = lambda v: v.rearrange("(c p) -> p c", p=P)
            one = lambda v: v.rearrange("(n o) -> n o", o=1)
            pairs = [(wdtf[:, :, 0:8], wi[:, :, DT2:DT2 + 8]), (wdtf[:, :, 8:16], wi[:, :, F2:F2 + 8]),
                     (b16[0:8, 0:1], one(bi[DT2:DT2 + 8])), (b16[8:16, 0:1], one(bi[F2:F2 + 8])),
                     (b16[0:8, 1:2], one(a["a_log_2"][0])),
                     (bx, col(bi[XBC2:XBC2 + 1024])), (bqk, col(bi[Q2:Q2 + 1024])),
                     (cb2, col(a["conv_b_2"][0])), (g8[:, 0:4], col(a["ssd_norm_g_2"][0])),
                     (dsk, a["d_skip_2"].broadcast_to([P, SH])),
                     (rb[:, 0:4], a["router_group_b_2"].broadcast_to([P, 4])),
                     (rb[:, 4:20], a["router_expert_b_2"].rearrange("o g e -> o (g e)").broadcast_to([P, 16])),
                     (wr[:, :, 0:4], a["router_group_w_2"][0].rearrange("(p k) n -> p k n", k=KT))]
            pairs += [(cw2[:, j, :], col(a["conv_w_2"][0, j])) for j in range(4)]
            pairs += [(wr[:, :, 4 + 4 * g:8 + 4 * g], a["router_expert_w_2"][0, g].rearrange("(p k) n -> p k n", k=KT))
                      for g in range(4)]
            for dst, src in pairs:
                eng.dma_start(dst, src, allow_slow_non_contiguous=True).then_inc(small2_loaded, 16)
            assert SMALL2 == 16 * len(pairs), len(pairs)

        unit_high_made, unit_split, act_high = Signal("unit_high_made"), Signal("unit_split"), Signal("act_high_made")
        units_free, act_turned, tokens_high = (sem(n) for n in ("units_free", "act_turned", "tokens_high_made"))
        hT_high, hT_split, kiT_zeroed = Signal("hT_high_made", 1), Signal("hT_split", 1), Signal("index_keys_zeroed", 1)
        mix_high, mix_split = Signal("mix_high_made", 3), Signal("mix_split", 1)
        weighted = Signal("combine_weights_made")
        block = ctx.enter_context(nc.Block())

        def bank(key):
            return psum[plan[key][0]]

        def wait_filled(eng, key):
            b, n, _ = plan[key]
            if key in by_units:
                eng.wait_ge(units_free, UNITS + by_units[key])
            else:
                eng.wait_ge(filled[b], n + 1)
            return psum[b]

        def wait_drained(eng, key):
            b, _, n = plan[key]
            eng.wait_ge(drained[b], n + 1)

        def drains(ins, key):
            return ins.then_inc(drained[plan[key][0]], 1)

        SPLIT_BEFORE = max(by_units.values())

        unit_of = {}

        def plan_units():
            for key, end in by_units.items():
                if key in SPLIT_COLUMNS or key[-1] in SPLIT_COLUMNS:
                    chunk, c0 = SPLIT_COLUMNS[key if key in SPLIT_COLUMNS else key[-1]]
                    chunk = key[:-1] + (chunk,) if key[-1] in SPLIT_COLUMNS else (chunk,)
                    for j in range(JOB_UNITS):
                        unit_of[end - JOB_UNITS + j] = chunk, chunks[chunk][2][:, :, c0 + j * P:c0 + (j + 1) * P]
                elif key[-1] == 0:
                    chunk = {"z": ("z",), "v": ("v",)}.get(key[-2]) or (key[0], "w_out" + key[-2][-1])
                    for q in range(ROW_UNITS):
                        k = 2 * ROW_ORDER[q]
                        unit_of[end - ROW_UNITS + q] = chunk, chunks[chunk][2][:, k:k + 2, :]

        ROW_ORDER = (2, 3, 0, 1)

        def by_k(unit, k=KT):
            return unit.rearrange("p (a b) -> p a b", a=k)

        chunks, loads, value, last = {}, [], [0] * SLOTS, [None] * SLOTS
        for n, (key, pieces, job) in enumerate(weight_plan(a)):
            s = n % SLOTS
            value[s] += 16 * len(pieces)
            width = sum(p[1].shape[2] for p in pieces)
            view = ring[:, s, 0:KT * width].rearrange("p (k n) -> p k n", k=KT)
            loads.append((s, last[s], [(view[:, :, at:at + p.shape[2]], p) for at, p in pieces]))
            chunks[key] = (s, value[s], view)
            last[s] = job
        plan_units()
        STREAM = [(0, 0), (1, 0), (0, 1), (2, 0), (1, 1), (0, 2), (2, 1), (1, 2), (0, 3), (1, 3), (2, 2), (2, 3)]
        FIRST_UNIT = {c: PER_SLOT * i for i, c in enumerate(STREAM)}
        GROUP_UNITS = PER_SLOT * len(STREAM)
        LAST = GROUPS - 1
        FILLS = {0: 1, 1: 1, 4: 1, 5: 1, 6: 1, 7: 2}
        DRAINS = {0: 1, 1: 1, 2: 1, 3: 1, 4: GE + 1, 5: 2 * GE + 1, 6: 1, 7: 2}

        def fills_of(b, n, k):
            return fills_used[b] + n * FILLS[b] + k

        def reads_of(b, n, k):
            return reads_used[b] + n * DRAINS[b] + k

        def stream_slot(i):
            return (len(loads) + i) % SLOTS

        def unit_done(n, k, e, q=PER_SLOT - 1):
            return UNITS + SPLIT_BEFORE + GROUP_UNITS * n + FIRST_UNIT[k, e] + q + 1

        def put_back_after(b, tiles):
            return {4: GE, 5: 2 * GE, 6: GE * (tiles - 1), 7: 1 if tiles == 1 else 2 + 2 * GE}[b]

        silu_after = {FIRST_UNIT[0, e] + PER_SLOT - 1 + UNITS: e for e in range(GE)}
        activate_after = {FIRST_UNIT[1, e] + PER_SLOT - 1 + UNITS: e for e in range(GE)}
        turned_after = {FIRST_UNIT[0, e + 1] + PER_SLOT: e for e in range(GE - 1)} | {FIRST_UNIT[2, GE - 1] + 1: GE - 1}

        @block.sync
        def _(sp):
            for tt in range(TT):
                sp.dma_start(x[:, tt, :], a["x"][0, tt * P:(tt + 1) * P, :]).then_inc(x_loaded, 16)
            for n, (s, job, pieces) in enumerate(loads):
                if n == 1:
                    load_layer_vectors(sp)
                if job is not None:
                    wait_filled(sp, job)
                for dst, src in pieces:
                    sp.dma_start(dst, src).then_inc(slot_here[s], 16)
                if n == 2 * SLOTS:
                    load_second_vectors(sp)

            def expert_weights(i, group):
                k, e = STREAM[i]
                s = stream_slot(i)
                n = KT if k < 2 else FT
                src = a[("w_gate_2", "w_up_2", "w_down_2")[k]][0][bass.ds(group * GE + e, 1)].rearrange("o a b -> (o a) b")
                src = src.rearrange("(p k) n -> p k n", k=n) if k < 2 else src.rearrange("(k p) n -> p k n", p=P)
                sp.dma_start(ring[:, s, :].rearrange("p (k n) -> p k n", k=n), src).then_inc(slot_here[s], 16)

            def rest_of_group(n, group):
                for i in range(SLOTS, len(STREAM)):
                    sp.wait_ge(unit_split.sem, SPLIT_BEFORE + GROUP_UNITS * n + PER_SLOT * (i - SLOTS + 1))
                    expert_weights(i, group)

            sp.wait_ge(order_ready.sem, 1)
            group = sp.value_load(order_i[0:1, 0:1], min_val=0, max_val=GROUPS - 1)
            for i in range(SLOTS):
                expert_weights(i, group)
            with sp.Fori(0, LAST) as n:
                group = sp.value_load(order_i[0:1, bass.ds(n, 1)], min_val=0, max_val=GROUPS - 1)
                rest_of_group(n, group)
                group = sp.value_load(order_i[0:1, bass.ds(n + 1, 1)], min_val=0, max_val=GROUPS - 1)
                for i in range(SLOTS):
                    sp.wait_ge(unit_split.sem, SPLIT_BEFORE + GROUP_UNITS * n + GROUP_UNITS - PER_SLOT * (SLOTS - i - 1))
                    expert_weights(i, group)
            group = sp.value_load(order_i[0:1, LAST:GROUPS], min_val=0, max_val=GROUPS - 1)
            rest_of_group(LAST, group)
            for tt in range(TT):
                sp.wait_ge(final_ready.sem, tt + 1)
                sp.dma_start(out[0, tt * P:(tt + 1) * P, :], acc[:, tt, :]).then_inc(stored, 16)
            sp.wait_ge(stored, 16 * TT)

        @block.tensor
        def _(pe):
            todo = list(order)

            def claim(key):
                assert todo.pop(0) == key, key
                b, _, n = plan[key]
                if n:
                    pe.wait_ge(drained[b], n)
                return psum[b]

            def fill(ins, key):
                ins.then_inc(filled[plan[key][0]], 1)

            def weights(key):
                s, v, view = chunks[key]
                pe.wait_ge(slot_here[s], v)
                return view

            def product(dst, lhs, rhs, n=KT, **kw):
                for k in range(n):
                    ins = pe.matmul(dst, lhs(k), rhs(k), start=(k == 0), stop=(k == n - 1), **kw)
                return ins

            def token_rows(key, w, tt, c0, n):
                ps = claim(key)
                fill(product(ps[:, 0:n], lambda k: hT[:, k, tt * P:(tt + 1) * P], lambda k: w[:, k, c0:c0 + n]), key)

            def channel_rows(key, w, c0, tiles):
                ps = claim(key)
                for j in range(tiles):
                    ins = product(ps[:, j * T:(j + 1) * T], lambda k: w[:, k, c0 + j * P:c0 + (j + 1) * P],
                                  lambda k: hT[:, k, :])
                fill(ins, key)

            def split_channel_rows(key):
                ps = claim(key)
                for j in range(JOB_UNITS):
                    u = by_units[key] - JOB_UNITS + j
                    pe.wait_ge(unit_split.sem, u + 1)
                    w_hi, w_lo = (by_k(w[:, u % UNITS, :]) for w in (unit_hi, unit_lo))
                    dst = ps[:, j * T:(j + 1) * T]
                    for k in range(KT):
                        pe.matmul(dst, w_hi[:, k, :], xg_hi[:, k, :], start=(k == 0), stop=False)
                        pe.matmul(dst, w_hi[:, k, :], xg_lo[:, k, :], start=False, stop=False)
                        ins = pe.matmul(dst, w_lo[:, k, :], xg_hi[:, k, :], start=False, stop=(k == KT - 1))
                    ins.then_inc(units_free, 1)

            def split_rows(keys):
                ps = [claim(key) for key in keys]
                for q in range(ROW_UNITS):
                    u = by_units[keys[0]] - ROW_UNITS + q
                    pe.wait_ge(unit_split.sem, u + 1)
                    w_hi, w_lo = (by_k(w[:, u % UNITS, :], 2) for w in (unit_hi, unit_lo))
                    for tt in range(TT):
                        for i in range(2):
                            k = 2 * ROW_ORDER[q] + i
                            t_hi, t_lo = (t[:, k, tt * P:(tt + 1) * P] for t in (xg_hi, xg_lo))
                            pe.matmul(ps[tt][:, :], t_hi, w_hi[:, i, :], start=(q == i == 0), stop=False)
                            pe.matmul(ps[tt][:, :], t_hi, w_lo[:, i, :], start=False, stop=False)
                            ins = pe.matmul(ps[tt][:, :], t_lo, w_hi[:, i, :], start=False,
                                            stop=(q == ROW_UNITS - 1 and i == 1))
                    ins.then_inc(units_free, 1)

            def pool_product(l):
                pe.wait_ge(pooled.sem, pooled.at(l, 1))
                ps = claim((l, "pool"))
                for j in range(2):
                    ins = pe.matmul(ps[:, j * T:(j + 1) * T], pw[:, l, j, :], mixT[:, 6 + j, :], start=True, stop=True)
                fill(ins, (l, "pool"))

            def transposes(key, srcs, width=P, rows=P):
                ps = claim(key)
                for n, src in enumerate(srcs):
                    ins = pe.transpose(ps[0:src.shape[1], n * width:n * width + rows], src, ident[0:rows, 0:rows])
                fill(ins, key)

            def natural_to_T(key, src, tt, hf, strided):
                transposes(key, [src[:, tt, (4 * hf + k):D:KT] if strided else
                                 src[:, tt, (4 * hf + k) * P:(4 * hf + k + 1) * P] for k in range(4)])

            group = [0]

            def scores(tag, qT, kT, extra=None):
                tt = tag[2]
                nk = (tt + 1) * P
                for p in range(2):
                    ps = claim(tag + ("s", p))
                    dst = ps[:, 0:2 * nk].rearrange("p (a b) -> p a b", a=2)
                    ins = pe.matmul(dst, qT(p)[:, tt * P:(tt + 1) * P], kT(p)[:, :, 0:nk], start=True, stop=True)
                    if extra is not None:
                        for j in range(2):
                            ins = pe.matmul(dst[:, j, :], extra(2 * p + j), dtf[0:16, 6, 0:nk], start=False, stop=True,
                                            skip_group_check=True)
                    fill(ins, tag + ("s", p))

            def outputs(tag, v):
                tt = tag[2]
                g = group[0]
                group[0] += 1
                for h in range(NH):
                    pe.wait_ge(expd.sem, NH * g + h + 1)
                    if h == 0:
                        for kt in range(tt + 1):
                            claim(tag + ("pT", kt))
                    for kt in range(tt + 1):
                        ins = pe.transpose(bank(tag + ("pT", kt))[:, h * P:(h + 1) * P],
                                           ex[:, g % 2, h, kt * P:(kt + 1) * P], ident)
                        if h == NH - 1:
                            fill(ins, tag + ("pT", kt))
                ps = claim(tag + ("o",))
                for kt in range(tt + 1):
                    wait_drained(pe, tag + ("pT", kt))
                for h in range(NH):
                    ins = product(ps[:, h * HD:(h + 1) * HD], lambda kt: exT[:, g % 2, kt, h * P:(h + 1) * P],
                                  lambda kt: v(kt, h), n=tt + 1)
                fill(ins, tag + ("o",))

            pe.wait_ge(const_loaded, 16)
            pe.wait_ge(zeroed, ZEROED)
            for l in range(LAYERS):
                for tt in range(TT):
                    pe.wait_ge(normed.sem, normed.at(l, tt + 1))
                    for hf in range(2):
                        natural_to_T((l, "hT", tt, hf), hn, tt, hf, True)
                pe.wait_ge(cmp_loaded, 64 * (l + 1))
                transposes((l, "peT"), [pe2[0:32, :, :].rearrange("p a b -> p (a b)")], rows=32)
                for tt in range(TT):
                    for hf in range(2):
                        wait_drained(pe, (l, "hT", tt, hf))
                w = weights((l, "w_idx"))
                for tt in range(TT):
                    token_rows((l, "idx", tt), w, tt, 0, 296)
                w = weights((l, "w_qkv"))
                for tt in range(TT):
                    token_rows((l, "qkv", tt), w, tt, 0, 384)
                for tt in range(TT):
                    pe.wait_ge(roped_i.sem, roped_i.at(l, tt + 1))
                    transposes((l, "idxT", tt), [ni[:, tt, n * P:(n + 1) * P] for n in range(3)])
                for tt in range(TT):
                    wait_drained(pe, (l, "idxT", tt))
                for tt in range(TT):
                    for n in range(4):
                        ps = claim((l, "logit", tt, n))
                        nk = (tt + 1) * P
                        fill(pe.matmul(ps[:, 0:2 * nk].rearrange("p (a b) -> p a b", a=2),
                                       qiT[:, n // 2, tt * P:(tt + 1) * P],
                                       kiT[:, 2 * (n % 2):2 * (n % 2) + 2, 0:nk], start=True, stop=True),
                             (l, "logit", tt, n))
                w = weights((l, "w_bq"))
                for tt in range(TT):
                    token_rows((l, "bq", tt), w, tt, 0, 256)
                channel_rows((l, "kcvc"), w, 256, 1)
                w = weights((l, "w_bkv"))
                for tt in range(TT):
                    token_rows((l, "bkv", tt), w, tt, 0, 268)
                for tt in range(TT):
                    pe.wait_ge(roped_a.sem, roped_a.at(l, tt + 1))
                    transposes((l, "qkT_a", tt), [na[:, tt, n * P:(n + 1) * P] for n in range(3)])
                w_gates = weights((l, "w_gates"))
                token_rows((l, "gates", 0), w_gates, 0, 0, 512)
                for tt in range(TT):
                    pe.wait_ge(roped_b.sem, roped_b.at(l, tt + 1))
                    transposes((l, "qkT_b", tt), [nb[:, tt, n * P:(n + 1) * P] for n in range(4)])
                pe.wait_ge(blocks.sem, blocks.at(l, 1))
                for n, name in enumerate(("kcmp", "vcmp")):
                    r = slice(n * HD, (n + 1) * HD)
                    ps = claim((l, name))
                    fill(product(ps[0:CP, 0:HD], lambda k: blk[r, k, :], lambda k: wcmp[r, k, :], n=32), (l, name))
                pe.wait_ge(hT_split.sem, hT_split.at(l, 1))
                split_channel_rows((l, "d_u"))
                token_rows((l, "gates", 1), w_gates, 1, 0, 512)
                pe.wait_ge(roped_c.sem, roped_c.at(l, 1))
                transposes((l, "kcT"), [kcN[0:CP, :]], rows=CP)
                wait_drained(pe, (l, "kcT"))
                wait_drained(pe, (l, "vcmp"))
                for tt in range(TT):
                    wait_drained(pe, (l, "qkT_b", tt))
                for tt in range(TT):
                    ps = claim((l, "cmp_s", tt))
                    for p in range(2):
                        ins = pe.matmul(ps[:, p * 64:p * 64 + 64].rearrange("p (a b) -> p a b", a=2),
                                        qbT[:, p, tt * P:(tt + 1) * P], kcT[:, :, :], start=True, stop=True)
                    fill(ins, (l, "cmp_s", tt))
                split_channel_rows((l, "d_g"))
                for tt in range(TT):
                    pe.wait_ge(cprob.sem, cprob.at(l, tt + 1))
                    transposes((l, "cmp_pT", tt), [ec[:].rearrange("p a b -> p (a b)")])
                    wait_drained(pe, (l, "cmp_pT", tt))
                    ps = claim((l, "cmp_o", tt))
                    fill(pe.matmul(ps[:, 0:256], pcT[:, :], vcB[:].rearrange("p a b -> p (a b)"), start=True, stop=True),
                         (l, "cmp_o", tt))
                operands = {"slc": (qbT, ksT, nb, 512), "win": (qbT, kwT, nb, 576), "dsa": (qaT, kaT, na, 384)}

                def layer_scores(tag):
                    q, k, _, _ = operands[tag[1]]
                    scores(tag, lambda p: q[:, p, :], lambda p: k[:])

                groups = layer_groups(l)
                layer_scores(groups[0])
                for n, tag in enumerate(groups):
                    if n + 1 < len(groups):
                        layer_scores(groups[n + 1])
                    if n < len(BETWEEN_GROUPS):
                        name = BETWEEN_GROUPS[n]
                        if name in SPLIT_COLUMNS:
                            split_channel_rows((l, name))
                        else:
                            pool_product(l)
                    _, _, vals, column = operands[tag[1]]
                    outputs(tag, lambda kt, h: vals[:, kt, column:column + HD])
                for tt in range(TT):
                    pe.wait_ge(mixr.sem, mixr.at(l, tt + 1))
                    transposes((l, "mixT", tt), [mixN[:, tt, n * P:(n + 1) * P] for n in range(4)])
                pe.wait_ge(mix_split.sem, mix_split.at(l, 1))
                for tt in range(TT):
                    wait_drained(pe, (l, "mixT", tt))
                for hf in range(2):
                    split_rows([(l, f"wo{hf}", tt) for tt in range(TT)])
            for tt in range(TT):
                pe.wait_ge(h0_ready.sem, tt + 1)
                for hf in range(2):
                    natural_to_T(("hT", tt, hf), x, tt, hf, True)
            for tt in range(TT):
                for hf in range(2):
                    wait_drained(pe, ("hT", tt, hf))
            pe.wait_ge(small2_loaded, SMALL2)
            ps = claim(("dtf",))
            fill(product(ps[0:16, 0:T], lambda k: wdtf[:, k, :], lambda k: hT[:, k, :]), ("dtf",))
            pe.wait_ge(hT_split.sem, hT_split.at(LAYERS, 1))
            for name, jobs in (("xbc", 4), ("q", 2), ("k", 2)):
                for n in range(jobs):
                    split_channel_rows((name, n))
            for name in ("z", "v"):
                split_rows([(name, tt) for tt in range(TT)])
            pe.wait_ge(cum_ready.sem, 1)
            transposes(("tA",), [dtf[0:16, r, tt * P:(tt + 1) * P] for tt in range(TT) for r in (4, 5)], width=16, rows=16)
            pe.wait_ge(act2.sem, 8)
            for tt in range(TT):
                transposes(("xs", tt), [xc[:, n, tt * P:(tt + 1) * P] for n in range(4)])
            for g in range(2):
                ps = claim(("cb", g))
                pe.matmul(ps[:, 0:T], xc[:, 4 + g, 0:P], xc[:, 6 + g, :], start=True, stop=True)
                fill(pe.matmul(ps[:, T:T + P], xc[:, 4 + g, P:T], xc[:, 6 + g, P:T], start=True, stop=True), ("cb", g))
            for n in range(TT):
                claim(("y", n))

            def y_head(h):
                pe.wait_ge(decay.sem, h + 1)
                if h == 0:
                    pe.wait_ge(xdt_ready.sem, 1)
                r = xdt[:, :, h * HD:(h + 1) * HD]
                a0 = pe.matmul(psum[0][:, h * HD:(h + 1) * HD], mTh[:, h % 2, 0:P], r[:, 0, :], start=True, stop=True)
                pe.matmul(psum[1][:, h * HD:(h + 1) * HD], mTh[:, h % 2, P:T], r[:, 0, :], start=True, stop=False)
                a1 = pe.matmul(psum[1][:, h * HD:(h + 1) * HD], mTh[:, h % 2, T:T + P], r[:, 1, :], start=False, stop=True)
                if h < SH - 1:
                    y_used.fire(a1)
                else:
                    fill(a0, ("y", 0))
                    fill(a1, ("y", 1))

            def scores2(tag):
                h0 = NH * tag[1]
                scores(tag, lambda p: qT2[:, h0 // 2 + p, :], lambda p: kT2[:, h0 // 2 + p, :, :],
                       extra=lambda h: ident[0:16, SH + h0 + h:SH + h0 + h + 1].broadcast_to([16, P]))

            def outputs2(tag):
                h0 = NH * tag[1]
                outputs(tag, lambda kt, h: v2[:, kt, (h0 + h) * HD:(h0 + h + 1) * HD])

            for name in ("q", "k", "v"):
                wait_drained(pe, (name, 1))
            pe.wait_ge(cum_ready.sem, 2)
            scores2(GROUPS2[0])
            for h in range(SH):
                ps = claim(("Ab", h))
                fill(pe.matmul(ps[:, 0:T], ident[0:16, h:h + 1].broadcast_to([16, P]), dtf[0:16, 5, :],
                               start=True, stop=True), ("Ab", h))
                if h:
                    y_head(h - 1)
                if h % 2:
                    n = h // 2
                    if n + 1 < len(GROUPS2):
                        scores2(GROUPS2[n + 1])
                    outputs2(GROUPS2[n])
            y_head(SH - 1)

            def out_product(part):
                for tt in range(TT):
                    wait_drained(pe, ("mT", tt, part))
                    for hf in range(2):
                        w = weights((f"out{hf}",))
                        key = ("wo", tt, hf)
                        ps = claim(key) if part else bank(key)
                        for k in range(4 * part, 4 * part + 4):
                            ins = pe.matmul(ps[:, :], mixT[:, k, tt * P:(tt + 1) * P], w[:, k, :],
                                            start=(k == 4), stop=(k == 3))
                        if not part:
                            fill(ins, key)

            for tag in GROUPS2:
                wait_drained(pe, tag + ("o",))
            for tt in range(TT):
                natural_to_T(("mT", tt, 1), merged, tt, 1, False)
            out_product(1)
            for tt in range(TT):
                pe.wait_ge(merged_ready.sem, tt + 1)
                natural_to_T(("mT", tt, 0), merged, tt, 0, False)
            out_product(0)
            for tt in range(TT):
                pe.wait_ge(h1_ready.sem, tt + 1)
                for hf in range(2):
                    natural_to_T(("h1T", tt, hf), x, tt, hf, True)
            for tt in range(TT):
                for hf in range(2):
                    wait_drained(pe, ("h1T", tt, hf))
                ps = claim(("route", tt))
                fill(product(ps[:, 0:20], lambda k: hT[:, k, tt * P:(tt + 1) * P], lambda k: wr[:, k, :]), ("route", tt))
            pe.wait_ge(one_hot.sem, 1)
            oh = rs[:, 2, :, :]
            tri = C("ltri")
            ps = claim(("rank",))
            pe.matmul(ps[:, 0:4], tri[:, 0:P], oh[:, 0, :], start=True, stop=True)
            pe.matmul(ps[:, 4:8], tri[:, P:T], oh[:, 0, :], start=True, stop=False)
            pe.matmul(ps[:, 4:8], tri[:, T:T + P], oh[:, 1, :], start=False, stop=True)
            pe.matmul(ps[:, 8:12], tri[:, P:T], oh[:, 0, :], start=True, stop=False)
            fill(pe.matmul(ps[:, 8:12], tri[:, P:T], oh[:, 1, :], start=False, stop=True), ("rank",))

            def gather(n, tile, selected, k=0):
                pe.wait_ge(sel_ready.sem, selected)
                for b in range(2):
                    pe.wait_ge(drained[b], reads_of(b, n, k))
                    for j in range(4):
                        ins = product(psum[b][:, j * P:(j + 1) * P], lambda tt: x[:, tt, 4 * b + j:D:KT],
                                      lambda tt: sel[tile][:, tt, :], n=TT)
                    ins.then_inc(filled[b], 1)

            def turn_selection(n, tile, k):
                pe.wait_ge(drained[7], reads_of(7, n, k))
                for tt in range(TT):
                    pe.transpose(psum[7][:, tt * P:(tt + 1) * P], sel[tile][:, tt, :], ident)
                product(psum[7][:, T:T + GE], lambda tt: sel[tile][:, tt, :], lambda tt: rs[:, 9, tt, :], n=TT)\
                    .then_inc(filled[7], 1)

            def unit_products(n, k, e, q, tiles):
                j = FIRST_UNIT[k, e] + q
                pe.wait_ge(unit_split.sem, SPLIT_BEFORE + GROUP_UNITS * n + j + 1)
                for tile in range(tiles):
                    for half in range(2):
                        w_hi, w_lo = (u[:, (SPLIT_BEFORE + j) % UNITS, half * 512:(half + 1) * 512]
                                      for u in (unit_hi, unit_lo))
                        if k < 2:
                            i = 2 * q + half
                            t_hi, t_lo = (u[:, i, tile * P:(tile + 1) * P] for u in (xg_hi, xg_lo))
                            dst, first, last_ = psum[4 + 2 * tile + k], i == 0, i == KT - 1
                        else:
                            t_hi, t_lo = (u[:, tile, q, :] for u in (act_hi, act_lo))
                            dst = psum[(2 + half) if tile == 0 else half]
                            first, last_ = e == 0 and q == 0, e == GE - 1 and q == FT - 1
                        pe.matmul(dst[:, :], t_hi, w_hi, start=first, stop=False)
                        pe.matmul(dst[:, :], t_hi, w_lo, start=False, stop=False)
                        ins = pe.matmul(dst[:, :], t_lo, w_hi, start=False, stop=last_)
                ins.then_inc(units_free, 1)

            def turn_act(n, e, tiles):
                for tile in range(tiles):
                    b = 5 + 2 * tile
                    k = 2 * e + 1 + 2 * tile
                    pe.wait_ge(drained[b], reads_of(b, n, k))
                    for f in range(FT):
                        ins = pe.transpose(psum[b][:, f * P:(f + 1) * P], act_n[tile][:, f * P:(f + 1) * P], ident)
                    ins.then_inc(act_turned, 1)

            def group_experts(n, tiles, before_last):
                for k, e in STREAM:
                    for q in range(PER_SLOT):
                        if q == PER_SLOT - 1:
                            if k == 0 and e:
                                turn_act(n, e - 1, tiles)
                            if (k, e) == (2, GE - 2):
                                turn_act(n, GE - 1, tiles)
                        if q == 0:
                            for tile in range(tiles):
                                b = 4 + 2 * tile
                                if k == 0:
                                    pe.wait_ge(drained[b], reads_of(b, n, e))
                                elif k == 1:
                                    pe.wait_ge(drained[b + 1], reads_of(b + 1, n, 2 * e + 2 * tile))
                                else:
                                    pe.wait_ge(drained[b + 1], reads_of(b + 1, n, 2 * e + 2 + 2 * tile))
                            if (k, e) == (2, 0):
                                for b in (2, 3):
                                    pe.wait_ge(drained[b], reads_of(b, n, 0))
                        unit_products(n, k, e, q, tiles)
                    if (k, e) == (2, GE - 2):
                        before_last()

            def put_back(n, tiles):
                for b in (2, 3):
                    pe.wait_ge(drained[b], reads_of(b, n, 1))
                if tiles == 2:
                    for b in (0, 1):
                        pe.wait_ge(drained[b], reads_of(b, n, 3))
                for i in range(4):
                    b, tt, hf = 4 + i, i // 2, i % 2
                    pe.wait_ge(drained[b], reads_of(b, n, put_back_after(b, tiles)))
                    product(psum[b][:, :], lambda i: selT[i][:, tt * P:(tt + 1) * P],
                            lambda i: yS[i][:, hf * 512:(hf + 1) * 512], n=tiles).then_inc(filled[b], 1)

            gather(0, 0, 1)
            pe.wait_ge(weighted.sem, 1)
            turn_selection(0, 0, 0)
            with pe.Fori(0, LAST) as n:
                for b in range(2):
                    pe.wait_ge(drained[b], reads_of(b, n, 1))
                group_experts(n, 1, lambda: gather(n + 1, 0, n + 2))
                put_back(n, 1)
                turn_selection(n + 1, 0, 0)
            gather(LAST, 1, LAST + 2, 1)
            turn_selection(LAST, 1, 1)
            for b in range(2):
                pe.wait_ge(drained[b], reads_of(b, LAST, 2))
            group_experts(LAST, 2, lambda: None)
            put_back(LAST, 2)
            assert not todo

        @block.vector
        def _(dve):
            def step(ins):
                vstep.fire(ins)
                dve.wait_ge(vstep.sem, vstep.n)

            def step_on(signal, ins):
                signal.fire(ins)
                dve.wait_ge(signal.sem, signal.n)

            def drain_step(ins, key):
                drains(ins, key)
                wait_drained(dve, key)

            V = nc.vector

            def inverse(dst, src, guard=None):
                if guard is not None:
                    step(V.tensor_scalar(src, src, guard, None, ALU.max))
                step(V.reciprocal(dst, src))

            def invert_mean_squares(n, eps, src, dst, signal):
                step(V.tensor_scalar(src, src, 1.0 / n, eps, ALU.mult, ALU.add))
                signal.fire(V.reciprocal(dst, src))

            def copy_T(key, tt, hf, scale=None, dst=hT):
                ps = wait_filled(dve, key)[:, :].rearrange("p (a b) -> p a b", a=4)
                d = dst[:, 4 * hf:4 * hf + 4, tt * P:(tt + 1) * P]
                if scale is None:
                    drains(V.tensor_copy(d, ps), key)
                else:
                    drains(V.tensor_tensor(d, ps, spread(scale[:, 4 * hf:4 * hf + 4], P), ALU.mult), key)

            def low_of(out_, whole, high):
                return V.tensor_tensor(out_, whole, high.bitcast(F32), ALU.subtract)

            def split_weights(n):
                for u in range(split[0], split[0] + n):
                    dve.wait_ge(unit_high_made.sem, u + 1)
                    w = unit_of[u][1]
                    k = w.shape[1]
                    low_of(by_k(unit_lo[:, u % UNITS, :], k), w, by_k(unit_hi[:, u % UNITS, :], k))\
                        .then_inc(unit_split.sem, 1)
                split[0] += n

            split = [0]
            group = [0, 0]

            def mask_and_max(tag, mask):
                g, tt = group[0], tag[2]
                group[0] += 1
                nk = (tt + 1) * P
                if g >= 2:
                    dve.wait_ge(expd.sem, NH * (g - 1))
                s = sm[:, g % 2, :, 0:nk]
                for p in range(2):
                    ps = wait_filled(dve, tag + ("s", p))[:, 0:2 * nk].rearrange("p (a b) -> p a b", a=2)
                    drains(V.scalar_tensor_tensor(s[:, 2 * p:2 * p + 2, :], repeat(mask, 2), BIG, ps, ALU.mult, ALU.add),
                           tag + ("s", p))
                wait_drained(dve, tag + ("s", 1))
                wait_drained(dve, tag + ("s", 0))
                step(V.tensor_reduce(mx[:, g % 2, :], s, AX_X, ALU.max))
                rmax.fire(V.tensor_scalar(mx[:, g % 2, :], mx[:, g % 2, :], -(HD ** -0.5), None, ALU.mult))

            def row_coef():
                g = group[1]
                group[1] += 1
                dve.wait_ge(expd.sem, NH * (g + 1))
                inverse(coef[:, g % 2, :], sums[:, g % 2, :], 1e-30)
                return coef[:, g % 2, :]

            def heads(ap):
                return ap.rearrange("p (a b) -> p a b", a=NH)

            dve.wait_ge(const_loaded, 16)
            dve.wait_ge(small_loaded, SMALL)
            dve.wait_ge(zeroed, ZEROED)
            for l in range(LAYERS):
                dve.wait_ge(sumsq.sem, sumsq.at(l, TT))
                invert_mean_squares(D, EPS, stat[:, 0, :], stat[:, 1, :], invms)
                dve.wait_ge(rstd_s.sem, rstd_s.at(l, 1))
                for tt in range(TT):
                    normed.fire(V.tensor_scalar(hn[:, tt, :], x[:, tt, :], stat[:, 2, tt:tt + 1], None, ALU.mult))
                for tt in range(TT):
                    for hf in range(2):
                        copy_T((l, "hT", tt, hf), tt, hf, normw[:, l, :])
                drains(V.tensor_copy(peT[:, :], wait_filled(dve, (l, "peT"))[:, 0:32]), (l, "peT"))
                dve.wait_ge(hT_high.sem, hT_high.at(l, 1))
                hT_split.fire(low_of(xg_lo[:, :, :], hT[:, :, :], xg_hi[:, :, :]))
                for tt in range(TT):
                    nk = (tt + 1) * P
                    for n in range(4):
                        wait_drained(dve, (l, "logit", tt, n))
                    step(V.tensor_scalar(score[:, 0, 0:nk], ncausal[:, tt, 0:nk], BIG, None, ALU.mult))
                    for h in range(8):
                        ins = V.scalar_tensor_tensor(score[:, 0, 0:nk], relu[:, h, 0:nk], ni[:, tt, 384 + h:385 + h],
                                                     score[:, 0, 0:nk], ALU.mult, ALU.add)
                        step(ins) if h < 7 else step_on(scored, ins)
                    for r in range(TOPK // 8):
                        src, dst = score[:, r % 2, 0:nk], score[:, 1 - r % 2, 0:nk]
                        step(V.max(top8[:, :], src))
                        step(V.match_replace(dst, top8[:, :], src, TAKEN))
                    step(V.scalar_tensor_tensor(amask[:, tt, 0:nk], score[:, 0, 0:nk], TAKEN, ncausal[:, tt, 0:nk],
                                                ALU.not_equal, ALU.max))
                wait_drained(dve, (l, "kcvc"))
                wait_drained(dve, (l, "peT"))
                kv = kvT[:, :].rearrange("p (n b) -> p b n", b=16)
                V.tensor_tensor(blk[:, 0:16, 0:NCMP], kv[:, :, 0:NCMP], spread(peT[:, 0:16], NCMP), ALU.add)
                blocks.fire(V.tensor_tensor(blk[:, 16:32, 0:NCMP], kv[:, :, 1:NCMP + 1], spread(peT[:, 16:32], NCMP), ALU.add))
                split_weights(UNITS)
                dve.wait_ge(gexp.sem, gexp.at(l, TT))
                step(V.tensor_scalar(gate[:, :, :], gate[:, :, :], 1.0, None, ALU.add))
                step(V.reciprocal(gate[:, :, :], gate[:, :, :]))
                def convolution():
                    wait_drained(dve, (l, "c_c"))
                    ps = wait_filled(dve, (l, "c_x"))
                    drain_step(V.tensor_tensor(cu[:, :, :], ccS[:, :, :], ps[:, :].rearrange("p (a b) -> p a b", a=2), ALU.mult),
                               (l, "c_x"))
                    for j in range(2):
                        step(V.tensor_scalar(cy[:, j, :], cu[:, j, :], cw[:, l, 2, j:j + 1], None, ALU.mult))
                        for k in (1, 2):
                            ins = V.scalar_tensor_tensor(cy[:, j, k:T], cu[:, j, 0:T - k], cw[:, l, 2 - k, j:j + 1],
                                                         cy[:, j, k:T], ALU.mult, ALU.add)
                            conv_y.fire(ins) if (j, k) == (1, 2) else step(ins)

                for tt in range(TT):
                    ps = wait_filled(dve, (l, "cmp_s", tt))[:, 0:128].rearrange("p (a b) -> p a b", a=NH)
                    drain_step(V.scalar_tensor_tensor(smc[:, :, :], repeat(cinv[:, tt, :], NH), BIG, ps, ALU.mult, ALU.add),
                               (l, "cmp_s", tt))
                    step(V.tensor_reduce(cmx[:, :], smc[:, :, :], AX_X, ALU.max))
                    cmax.fire(V.tensor_tensor(smc[:, :, :], smc[:, :, :], spread(cmx[:, :], CP), ALU.subtract))
                    if tt == 0:
                        split_weights(JOB_UNITS)
                    dve.wait_ge(cexp.sem, cexp.at(l, tt + 1))
                    step_on(cprob, V.tensor_tensor(ec[:, :, :], ec[:, :, :], repeat(cval[:, tt, :], NH), ALU.mult))
                    step(V.tensor_reduce(csum[:, :], ec[:, :, :], AX_X, ALU.add))
                    inverse(csum[:, :], csum[:, :], 1e-30)
                    step(V.tensor_tensor(csum[:, :], csum[:, :], gate[:, tt, 0:12:3], ALU.mult))
                    ps = wait_filled(dve, (l, "cmp_o", tt))
                    drains(V.tensor_tensor(shaped(ob[:, tt, 0, :], NH, HD), heads(ps[:, 0:256]), spread(csum[:, :], HD), ALU.mult),
                           (l, "cmp_o", tt))
                    if tt == 0:
                        split_weights(JOB_UNITS)
                def pooled_channels():
                    ps = wait_filled(dve, (l, "pool"))
                    wait_drained(dve, (l, "d_g"))
                    for j in range(2):
                        ins = V.scalar_tensor_tensor(mixT[:, 6 + j, :], ps[:, j * T:(j + 1) * T], psc[:, l, j:j + 1], dg[:, j, :],
                                                     ALU.mult, ALU.mult)
                    drains(ins, (l, "pool"))

                groups = layer_groups(l)

                def mask_of(tag):
                    nk = (tag[2] + 1) * P
                    return (amask if tag[1] == "dsa" else ncausal)[:, tag[2], 0:nk]

                mask_and_max(groups[0], mask_of(groups[0]))
                for n, tag in enumerate(groups):
                    if n + 1 < len(groups):
                        mask_and_max(groups[n + 1], mask_of(groups[n + 1]))
                    if n < SPLIT_BETWEEN:
                        split_weights(1)
                    _, branch, tt = tag
                    c = row_coef()
                    key = tag + ("o",)
                    if branch != "dsa":
                        step(V.tensor_tensor(c, c, gate[:, tt, (1 if branch == "slc" else 2):12:3], ALU.mult))
                    ps = wait_filled(dve, key)
                    to = {"slc": ob[:, tt, 1, :], "win": mixN[:, tt, 256:512], "dsa": mixN[:, tt, 0:256]}[branch]
                    drains(V.tensor_tensor(heads(to), heads(ps[:, 0:256]), spread(c, HD), ALU.mult), key)
                    if branch == "dsa":
                        wait_drained(dve, key)
                        wait_drained(dve, (l, "gates", tt))
                        dve.wait_ge(b_done.sem, b_done.at(l, tt + 1))
                        mixr.fire(V.tensor_tensor(mixN[:, tt, 0:256], mixN[:, tt, 0:256], gsil[:, tt, 0:256], ALU.mult))
                    if BETWEEN_GROUPS[n:n + 1] == ("c_x",):
                        convolution()
                    if BETWEEN_GROUPS[n:n + 1] == ("pool",):
                        pooled_channels()
                    if n < SPLIT_BETWEEN:
                        split_weights(1)
                dve.wait_ge(mix_high.sem, mix_high.at(l, 1))
                mix_split.fire(low_of(xg_lo[:, 4:8, :], mixT[:, 4:8, :], xg_hi[:, 4:8, :]))
                for tt in range(TT):
                    dve.wait_ge(mix_high.sem, mix_high.at(l, tt + 2))
                    r = (slice(None), slice(0, 4), slice(tt * P, (tt + 1) * P))
                    ps = bank((l, "mixT", tt))[:, :].rearrange("p (a b) -> p a b", a=4)
                    drains(low_of(xg_lo[r], ps, xg_hi[r]), (l, "mixT", tt))
                split_weights(2 * ROW_UNITS - UNITS)
                for hf in range(2):
                    for tt in range(TT):
                        ps = wait_filled(dve, (l, f"wo{hf}", tt))
                        r = x[:, tt, hf * 512:(hf + 1) * 512]
                        drains(V.tensor_tensor(r, r, ps[:, :], ALU.add), (l, f"wo{hf}", tt))
            dve.wait_ge(sumsq.sem, sumsq.at(LAYERS, TT))
            invert_mean_squares(D, EPS, stat[:, 0, :], stat[:, 1, :], invms)
            dve.wait_ge(rstd_s.sem, rstd_s.at(LAYERS, 1))
            dve.wait_ge(vec_loaded, 16)
            for tt in range(TT):
                h0_ready.fire(V.scalar_tensor_tensor(x[:, tt, :], x[:, tt, :], stat[:, 2, tt:tt + 1], vec[:, 0, :],
                                                     ALU.mult, ALU.mult))
            for tt in range(TT):
                for hf in range(2):
                    copy_T(("hT", tt, hf), tt, hf)
            dve.wait_ge(hT_high.sem, hT_high.at(LAYERS, 1))
            hT_split.fire(low_of(xg_lo[:, :, :], hT[:, :, :], xg_hi[:, :, :]))
            split_weights(UNITS)
            dve.wait_ge(small2_loaded, SMALL2)
            coef_in.fire(V.tensor_tensor(b16[0:16, 2:3], b16[0:16, 0:1], C("sgn", rows=16), ALU.mult))
            dve.wait_ge(dt_exp.sem, 2)
            R = [dtf[0:16, r, :] for r in range(8)]
            step_on(dt_w, V.tensor_scalar(R[2], R[1], 1.0, None, ALU.add))
            step(V.tensor_scalar(R[3], R[2], 1.0, None, ALU.subtract))
            step(V.tensor_scalar(R[7], R[3], 0.0, None, ALU.is_equal))
            inverse(R[3], R[3], TINY)
            dve.wait_ge(dt_ln.sem, 1)
            step(V.tensor_tensor(R[4], R[4], R[3], ALU.mult))
            step(V.tensor_tensor(R[4], R[4], R[7], ALU.add))
            step(V.tensor_tensor(R[4], R[4], R[1], ALU.mult))
            step(V.scalar_tensor_tensor(R[4], R[0], 0.0, R[4], ALU.max, ALU.add))
            step(V.memset(R[2], 1.0))
            step(V.tensor_scalar(R[3], R[4], b16[0:16, 3:4], -1.0, ALU.mult, ALU.mult))
            step_on(cum_ready, V.tensor_tensor_scan(R[5], R[2], R[3], 0.0, ALU.mult, ALU.add))
            cum_ready.fire(V.tensor_scalar(R[6], R[5], -8.0, None, ALU.mult))
            for n in range(8):
                split_weights(1)
                if n % 2 == 0:
                    wait_drained(dve, ("xbc", n // 2))
                step(V.tensor_scalar(xc[:, n, :], xbc[:, n, :], cw2[:, 3, n:n + 1], cb2[:, n:n + 1], ALU.mult, ALU.add))
                for k in (1, 2, 3):
                    ins = V.scalar_tensor_tensor(xc[:, n, k:T], xbc[:, n, 0:T - k], cw2[:, 3 - k, n:n + 1],
                                                 xc[:, n, k:T], ALU.mult, ALU.add)
                    conv2.fire(ins) if k == 3 else step(ins)
                split_weights(1)
            split_weights(ROW_UNITS)
            dve.wait_ge(brow_loaded, 32)
            for tt in range(TT):
                ps = wait_filled(dve, ("z", tt))
                drains(V.tensor_tensor(z2[:, tt, :], ps[:, :], brow[:, 0:512], ALU.add), ("z", tt))
            split_weights(1)
            for tt in range(TT):
                ps = wait_filled(dve, ("v", tt))
                drains(V.tensor_tensor(v2[:, tt, :], ps[:, :], brow[:, 512:1024], ALU.add), ("v", tt))
            drain_step(V.tensor_copy(dA[:, :, :], wait_filled(dve, ("tA",))[:, 0:64].rearrange("p (a b) -> p a b", a=4)), ("tA",))
            for g in range(2):
                ps = wait_filled(dve, ("cb", g))
                drains(V.tensor_tensor(cbm[:, g, :], ps[:, 0:384], C("ltri"), ALU.mult), ("cb", g))

            def finish2(tag):
                _, half, tt = tag
                c = row_coef()
                ps = wait_filled(dve, tag + ("o",))
                drains(V.tensor_tensor(heads(merged[:, tt, 512 + 256 * half:768 + 256 * half]), heads(ps[:, 0:256]),
                                       spread(c, HD), ALU.mult), tag + ("o",))

            def mask2(tag):
                mask_and_max(tag, ncausal[:, tag[2], 0:(tag[2] + 1) * P])

            mask2(GROUPS2[0])
            for h in range(SH):
                ps = wait_filled(dve, ("Ab", h))
                if h >= 2:
                    dve.wait_ge(decay.sem, h - 1)
                V.tensor_scalar(seg[:, h % 2, 0:T], ps[:, 0:T], dA[:, 1, h:h + 1], 0.0, ALU.subtract, ALU.min)
                drains(V.tensor_scalar(seg[:, h % 2, T:T + P], ps[:, P:T], dA[:, 3, h:h + 1], 0.0, ALU.subtract, ALU.min),
                       ("Ab", h))
                if h % 2:
                    if h // 2 + 1 < len(GROUPS2):
                        mask2(GROUPS2[h // 2 + 1])
                    finish2(GROUPS2[h // 2])
            dve.wait_ge(xdt_ready.sem, 2)
            for tt in range(TT):
                ps = wait_filled(dve, ("y", tt))
                drain_step(V.tensor_tensor(merged[:, tt, 0:512], ps[:, :], xsN[:, tt, :], ALU.add), ("y", tt))
                dve.wait_ge(z_ready.sem, tt + 1)
                yz.fire(V.tensor_tensor(merged[:, tt, 0:512], merged[:, tt, 0:512], z2[:, tt, :], ALU.mult))
            dve.wait_ge(g8_ones.sem, 1)
            for tt in range(TT):
                copy_T(("mT", tt, 1), tt, 1, g8, mixT)
            dve.wait_ge(ysq.sem, 4)
            invert_mean_squares(256, 1e-5, rv[:, 0:4, 0], rv[:, 4:8, 0], yinv)
            dve.wait_ge(yrstd.sem, 1)
            for tt in range(TT):
                for g in range(2):
                    m = merged[:, tt, g * 256:(g + 1) * 256]
                    ins = V.tensor_scalar(m, m, rv[:, 8 + 2 * tt + g, 0:1], None, ALU.mult)
                merged_ready.fire(ins)
            for tt in range(TT):
                copy_T(("mT", tt, 0), tt, 0, g8, mixT)

            def layer_norm(tt, residual, loaded, done, x):
                for hf in range(2):
                    residual(hf)
                s = coef2[:, :, tt:tt + 1]
                step(V.tensor_reduce(s[:, 0, :], x[:, tt, :], AX_X, ALU.add))
                step_on(ln_mu, V.tensor_scalar(s[:, 0, :], s[:, 0, :], -1.0 / D, None, ALU.mult))
                dve.wait_ge(ln_sq.sem, ln_mu.n)
                invert_mean_squares(D, 1e-5, s[:, 1, :], s[:, 2, :], ln_inv)
                dve.wait_ge(ln_rstd.sem, ln_mu.n)
                step(V.tensor_scalar(x[:, tt, :], x[:, tt, :], s[:, 0, :], s[:, 3, :], ALU.add, ALU.mult))
                dve.wait_ge(vec_loaded, loaded)
                step(V.tensor_tensor(x[:, tt, :], x[:, tt, :], vec[:, 0, :], ALU.mult))
                done.fire(V.tensor_tensor(x[:, tt, :], x[:, tt, :], vec[:, 1, :], ALU.add))

            def residual1(tt):
                def one(hf):
                    r = x[:, tt, hf * 512:(hf + 1) * 512]
                    ps = wait_filled(dve, ("wo", tt, hf))
                    drain_step(V.scalar_tensor_tensor(r, r, ALPHA, ps[:, :], ALU.mult, ALU.add), ("wo", tt, hf))
                return one

            for tt in range(TT):
                layer_norm(tt, residual1(tt), 16 * 3, h1_ready, x)
            for tt in range(TT):
                for hf in range(2):
                    copy_T(("h1T", tt, hf), tt, hf)
            for tt in range(TT):
                ps = wait_filled(dve, ("route", tt))
                drain_step(V.tensor_tensor(rl[:, tt, :], ps[:, 0:20], rb[:, :], ALU.add), ("route", tt))
            S = [rs[:, r, :, :] for r in range(12)]
            U = [rv[:, r, :] for r in range(12)]
            rank = C("rank")

            def first_of(dst, hit, m):
                step(V.tensor_tensor(dst, hit, repeat(rank, TT), ALU.mult))
                step(V.tensor_reduce(m, dst, AX_X, ALU.max))
                ins = V.tensor_tensor(dst, dst, spread(m, 4), ALU.is_equal)
                if dst is S[2]:
                    step_on(one_hot, ins)
                else:
                    step(ins)

            step(V.tensor_reduce(U[0], rl[:, :, 0:4], AX_X, ALU.max))
            step_on(r_in, V.tensor_tensor(S[0], rl[:, :, 0:4], spread(U[0], 4), ALU.subtract))
            step(V.tensor_scalar(S[2], S[0], 0.0, None, ALU.is_equal))
            first_of(S[2], S[2], U[1])
            ps = wait_filled(dve, ("rank",))
            ranks, counts = ps[:, 0:8].rearrange("p (a b) -> p a b", a=TT), ps[:, 8:12]
            Q = [grp[:, r_, :] for r_ in range(8)]
            step(V.tensor_copy(Q[0], counts))
            step(V.tensor_reduce(U[8][:, 0:1], Q[0], AX_X, ALU.max))
            step(V.tensor_scalar(Q[1], Q[0], U[8][:, 0:1], None, ALU.is_equal))
            step(V.tensor_tensor(Q[1], Q[1], rank, ALU.mult))
            step(V.tensor_reduce(U[8][:, 0:1], Q[1], AX_X, ALU.max))
            step(V.tensor_scalar(Q[1], Q[1], U[8][:, 0:1], None, ALU.is_equal))
            step(V.memset(Q[2], 1.0))
            step(V.tensor_tensor_scan(Q[3], Q[2], Q[1], 0.0, ALU.mult, ALU.add))
            step(V.tensor_scalar(Q[4], rank, -1.0, 4.0, ALU.mult, ALU.add))
            step(V.tensor_tensor(Q[5], Q[4], Q[3], ALU.add))
            step(V.tensor_tensor(Q[6], Q[4], Q[1], ALU.mult))
            step(V.tensor_reduce(U[8][:, 0:1], Q[6], AX_X, ALU.add))
            V.tensor_copy(order_i[:, 0:LAST], Q[5][:, 0:LAST])
            order_ready.fire(V.tensor_copy(order_i[:, LAST:GROUPS], U[8][:, 0:1]))
            step(V.tensor_tensor(Q[4], Q[4], Q[3], ALU.subtract))
            step(V.tensor_tensor(Q[4], Q[4], Q[1], ALU.add))
            step(V.scalar_tensor_tensor(Q[6], rank, -1.0, Q[1], ALU.add, ALU.mult))
            step(V.tensor_tensor(Q[4], Q[4], Q[6], ALU.add))
            step(V.tensor_scalar(Q[4], Q[4], float(P), None, ALU.mult))
            drain_step(V.tensor_tensor(S[10], ranks, repeat(Q[4], TT), ALU.add), ("rank",))
            step(V.tensor_tensor(S[10], S[10], S[2], ALU.mult))
            step(V.tensor_reduce(slot_of, S[10], AX_X, ALU.add))
            step(V.tensor_scalar(slot_of, slot_of, -1.0, None, ALU.add))

            def select(tile, before):
                for tt in range(TT):
                    ins = V.tensor_scalar(sel[tile][:, tt, :], C("iota"), slot_of[:, tt:tt + 1], None, ALU.is_equal)
                sel_ready.fire(ins)
                dve.wait_ge(sel_ready.sem, before + 1)
                V.tensor_scalar(slot_of, slot_of, -float(P), None, ALU.add).then_inc(next_tile.sem, 1)

            def split_unit(n, j):
                dve.wait_ge(unit_high_made.sem, SPLIT_BEFORE + GROUP_UNITS * n + j + 1)
                s, q = stream_slot(j // PER_SLOT), j % PER_SLOT
                low_of(unit_lo[:, (SPLIT_BEFORE + j) % UNITS, :], ring[:, s, q * UNIT:(q + 1) * UNIT], unit_hi[:, (SPLIT_BEFORE + j) % UNITS, :])\
                    .then_inc(unit_split.sem, 1)

            def split_gathered(n, k, tile, count):
                dve.wait_ge(tokens_high, count)
                for b in range(2):
                    r = (slice(None), slice(4 * b, 4 * b + 4), slice(tile * P, (tile + 1) * P))
                    low_of(xg_lo[r], psum[b][:, :].rearrange("p (a b) -> p a b", a=4), xg_hi[r]).then_inc(drained[b], 1)

            def take_selection(n, k, tile, count):
                dve.wait_ge(filled[7], fills_of(7, n, k + 1))
                V.tensor_copy(combine[tile], psum[7][:, T:T + GE]).then_inc(combine_here.sem, 1)
                V.tensor_copy(selT[tile], psum[7][:, 0:T]).then_inc(drained[7], 1)
                dve.wait_ge(combine_here.sem, count)

            def activate(n, e, tile):
                b = 4 + 2 * tile
                dve.wait_ge(drained[b], reads_of(b, n, e + 1))
                dve.wait_ge(units_free, unit_done(n, 1, e))
                V.scalar_tensor_tensor(act_n[tile], silu_g[tile], combine[tile][:, e:e + 1], psum[b + 1][:, :],
                                       ALU.mult, ALU.mult).then_inc(drained[b + 1], 1)

            def split_act(n, e, tile, tiles):
                dve.wait_ge(act_high.sem, GE * n + tiles * e + tile + 1)
                b = 5 + 2 * tile
                low_of(act_lo[:, tile], psum[b][:, :].rearrange("p (a b) -> p a b", a=FT), act_hi[:, tile])\
                    .then_inc(drained[b], 1)

            def group_units(n, tiles, before_last):
                for j in range(UNITS, GROUP_UNITS + UNITS * (tiles == 1)):
                    split_unit(n, j)
                    for tile in range(tiles):
                        if j in activate_after:
                            activate(n, activate_after[j], tile)
                    for tile in range(tiles):
                        if j in turned_after:
                            split_act(n, turned_after[j], tile, tiles)
                    if turned_after.get(j) == GE - 1:
                        before_last()

            def add_outputs(n, tiles):
                for i in range(4):
                    b, tt, hf = 4 + i, i // 2, i % 2
                    dve.wait_ge(filled[b], fills_of(b, n, 1 if b < 7 else tiles + 1))
                    y = acc[:, tt, hf * 512:(hf + 1) * 512]
                    V.tensor_tensor(y, y, psum[b][:, :], ALU.add).then_inc(drained[b], 1)

            select(0, 0)
            dve.wait_ge(r_exp.sem, 1)
            step(V.tensor_reduce(U[2], S[1], AX_X, ALU.add))
            step(V.reciprocal(U[2], U[2]))
            for g in range(4):
                dst = S[3] if g == 0 else S[10]
                step(V.tensor_tensor(dst, rl[:, :, 4 + 4 * g:8 + 4 * g], spread(S[2][:, :, g], 4), ALU.mult))
                if g:
                    step(V.tensor_tensor(S[3], S[3], S[10], ALU.add))
            step(V.tensor_reduce(U[3], S[3], AX_X, ALU.max))
            step_on(r_in, V.tensor_tensor(S[4], S[3], spread(U[3], 4), ALU.subtract))
            step(V.tensor_scalar(S[6], S[4], 0.0, None, ALU.is_equal))
            first_of(S[6], S[6], U[4])
            step(V.tensor_scalar(S[7], S[6], BIG, None, ALU.mult))
            step(V.tensor_tensor(S[7], S[7], S[4], ALU.add))
            step(V.tensor_reduce(U[5], S[7], AX_X, ALU.max))
            step(V.tensor_tensor(S[8], S[7], spread(U[5], 4), ALU.is_equal))
            first_of(S[8], S[8], U[6])
            step(V.tensor_tensor(S[8], S[8], S[6], ALU.add))
            dve.wait_ge(r_exp.sem, 2)
            step(V.tensor_tensor(S[9], S[5], S[8], ALU.mult))
            step(V.tensor_reduce(U[7], S[9], AX_X, ALU.add))
            step(V.reciprocal(U[7], U[7]))
            step(V.tensor_tensor(U[7], U[7], U[2], ALU.mult))
            weighted.fire(V.tensor_tensor(S[9], S[9], spread(U[7], 4), ALU.mult))
            step(V.tensor_scalar(acc[:, :, :], x[:, :, :], ALPHA, None, ALU.mult))
            split_gathered(0, 0, 0, 2)
            for j in range(UNITS):
                split_unit(0, j)
            with dve.Fori(0, LAST) as n:
                take_selection(n, 0, 0, n + 1)
                dve.wait_ge(next_tile.sem, n + 1)
                select(0, n + 1)
                group_units(n, 1, lambda: split_gathered(n + 1, 0, 0, 2 * n + 4))
                add_outputs(n, 1)
            take_selection(LAST, 0, 0, GROUPS)
            dve.wait_ge(next_tile.sem, LAST + 1)
            select(1, LAST + 1)
            split_gathered(LAST, 1, 1, 2 * GROUPS + 2)
            take_selection(LAST, 1, 1, GROUPS + 1)
            group_units(LAST, 2, lambda: None)
            add_outputs(LAST, 2)
            for b in range(4, 8):
                dve.wait_ge(drained[b], reads_of(b, LAST, put_back_after(b, 2) + 1))
            for tt in range(TT):
                layer_norm(tt, lambda hf: None, 16 * 5, final_ready, acc)

        @block.scalar
        def _(act):
            def step(ins):
                astep.fire(ins)
                act.wait_ge(astep.sem, astep.n)

            def run(out_, in_, func=ACT.Copy, **kw):
                return nc.scalar.activation(out_, in_, func, **kw)

            act.dma_start(cst[:, :], a["shape_constants"][:, :]).then_inc(const_loaded, 16)

            def load_cmp(l):
                for n, name in enumerate(("w_cmp_k", "w_cmp_v")):
                    act.dma_start(pe2[0:32, n, :], a["pe_cmp"][l]).then_inc(cmp_loaded, 16)
                    act.dma_start(wcmp[n * HD:(n + 1) * HD, :, :], a[name][l].rearrange("(k d) e -> d k e", d=HD))\
                       .then_inc(cmp_loaded, 16)

            group = [0]

            def exps(tag):
                g, tt = group[0], tag[2]
                group[0] += 1
                nk = (tt + 1) * P
                act.wait_ge(rmax.sem, g + 1)
                if g >= 2:
                    wait_filled(act, prev_groups[g - 2] + ("pT", prev_groups[g - 2][2]))
                for h in range(NH):
                    expd.fire(run(ex[:, g % 2, h, 0:nk], sm[:, g % 2, h, 0:nk], ACT.Exp, bias=mx[:, g % 2, h:h + 1],
                                  scale=HD ** -0.5, accum_out=sums[:, g % 2, h:h + 1]))

            prev_groups = [t for l in range(LAYERS) for t in layer_groups(l)] + GROUPS2
            gdone = [0]

            def evacuate_probs(tag):
                g = gdone[0]
                gdone[0] += 1
                if g >= 2:
                    wait_filled(act, prev_groups[g - 2] + ("o",))
                for kt in range(tag[2] + 1):
                    key = tag + ("pT", kt)
                    drains(run(exT[:, g % 2, kt, :], wait_filled(act, key)[:, :]), key)

            split = [0]

            def split_weights(n):
                for u in range(split[0], split[0] + n):
                    chunk, w = unit_of[u]
                    s, v, _ = chunks[chunk]
                    act.wait_ge(slot_here[s], v)
                    act.wait_ge(units_free, u + 1)
                    unit_high_made.fire(run(by_k(unit_hi[:, u % UNITS, :], w.shape[1]), w))
                split[0] += n

            for l in range(LAYERS + 1):
                if l == 0:
                    act.wait_ge(x_loaded, 16 * TT)
                else:
                    for hf in range(2):
                        for tt in range(TT):
                            wait_drained(act, (l - 1, f"wo{hf}", tt))
                for tt in range(TT):
                    sumsq.fire(run(hn[:, tt, :], x[:, tt, :], ACT.Square, accum_out=stat[:, 0, tt:tt + 1]))
                if l == 0:
                    act.wait_ge(zeroed, ZEROED)
                    load_cmp(0)
                act.wait_ge(invms.sem, l + 1)
                rstd_s.fire(run(stat[:, 2, :], stat[:, 1, :], ACT.Sqrt))
                if l == LAYERS:
                    break
                for tt in range(TT):
                    for hf in range(2):
                        wait_drained(act, (l, "hT", tt, hf))
                hT_high.fire(run(xg_hi[:, :, :], hT[:, :, :]))

                def drain_channels(name):
                    if name in channels:
                        dst, func = channels[name]
                        ps = wait_filled(act, (l, name))
                        drains(run(dst[:, :, :], ps[:, :].rearrange("p (a b) -> p a b", a=2), func), (l, name))

                channels = {"c_b": (cbS, ACT.Copy), "c_c": (ccS, ACT.Copy), "c_g": (cgS, ACT.Silu),
                            "d_u": (du[:, :, 16:], ACT.Copy), "d_g": (dg, ACT.Silu)}
                if l:
                    act.wait_ge(kiT_zeroed.sem, kiT_zeroed.at(l - 1, 1))
                for tt in range(TT):
                    key = (l, "idx", tt)
                    ps = wait_filled(act, key)
                    run(ni[:, tt, 0:256], ps[:, 0:256])
                    run(shaped(ni[:, tt, 256:384], 4, 32), repeat(ps[:, 256:288], 4))
                    drains(run(ni[:, tt, 384:392], ps[:, 288:296], scale=1.0 / 16.0), key)
                for tt in range(TT):
                    key = (l, "qkv", tt)
                    ps = wait_filled(act, key)
                    run(na[:, tt, 0:256], ps[:, 0:256])
                    run(shaped(na[:, tt, 256:384], 2, HD), repeat(ps[:, 256:320], 2))
                    drains(run(na[:, tt, 384:448], ps[:, 320:384]), key)
                for tt in range(TT):
                    key = (l, "idxT", tt)
                    ps = wait_filled(act, key)
                    tok = slice(tt * P, (tt + 1) * P)
                    run(qiT[:, :, tok], ps[:, 0:256].rearrange("p (a b) -> p a b", a=2))
                    for j in range(4):
                        r = slice(32 * j, 32 * j + 32)
                        ins = run(kiT[r, j, tok], ps[r, 256:384])
                    drains(ins, key)
                for tt in range(TT):
                    nk = (tt + 1) * P
                    if tt:
                        act.wait_ge(scored.sem, scored.at(l, tt))
                    for n in range(4):
                        key = (l, "logit", tt, n)
                        ps = wait_filled(act, key)
                        drains(run(relu[:, 2 * n:2 * n + 2, 0:nk], ps[:, 0:2 * nk].rearrange("p (a b) -> p a b", a=2), ACT.Relu),
                               key)
                for tt in range(TT):
                    key = (l, "bq", tt)
                    drains(run(nb[:, tt, 0:256], wait_filled(act, key)[:, 0:256]), key)
                drains(run(kvT[:, :], wait_filled(act, (l, "kcvc"))[:, 0:T]), (l, "kcvc"))
                for tt in range(TT):
                    key = (l, "bkv", tt)
                    ps = wait_filled(act, key)
                    run(shaped(nb[:, tt, 256:384], 2, HD), repeat(ps[:, 0:64], 2))
                    run(nb[:, tt, 512:576], ps[:, 64:128])
                    run(shaped(nb[:, tt, 384:512], 2, HD), repeat(ps[:, 128:192], 2))
                    drains(run(nb[:, tt, 576:652], ps[:, 192:268]), key)

                def drain_gates(tt):
                    key = (l, "gates", tt)
                    drains(run(gsil[:, tt, :], wait_filled(act, key)[:, :], ACT.Silu), key)

                for tt in range(TT):
                    key = (l, "qkT_a", tt)
                    ps = wait_filled(act, key)
                    tok = slice(tt * P, (tt + 1) * P)
                    run(qaT[:, :, tok], ps[:, 0:256].rearrange("p (a b) -> p a b", a=2))
                    for j in range(2):
                        r = slice(HD * j, HD * j + HD)
                        ins = run(kaT[r, j, tok], ps[r, 256:384])
                    drains(ins, key)
                drain_gates(0)
                for tt in range(TT):
                    key = (l, "qkT_b", tt)
                    ps = wait_filled(act, key)
                    tok = slice(tt * P, (tt + 1) * P)
                    run(qbT[:, :, tok], ps[:, 0:256].rearrange("p (a b) -> p a b", a=2))
                    for m, dst in enumerate((ksT, kwT)):
                        for j in range(2):
                            r = slice(HD * j, HD * j + HD)
                            ins = run(dst[r, j, tok], ps[r, (2 + m) * P:(3 + m) * P])
                    drains(ins, key)
                split_weights(UNITS)
                ps = wait_filled(act, (l, "kcmp"))
                drains(run(shaped(kcN[0:CP, :], 2, HD), repeat(ps[0:CP, 0:HD], 2)), (l, "kcmp"))
                ps = wait_filled(act, (l, "vcmp"))
                for h in range(NH):
                    ins = run(vcB[CP * h:CP * h + CP, h, :], ps[0:CP, 0:HD])
                drains(ins, (l, "vcmp"))
                drain_channels("d_u")
                split_weights(JOB_UNITS)
                for tt in range(TT):
                    wait_drained(act, (l, "bkv", tt))
                    gexp.fire(run(gate[:, tt, :], nb[:, tt, 640:652], ACT.Exp, scale=-1.0))
                drain_gates(1)
                ps = wait_filled(act, (l, "kcT"))
                for j in range(2):
                    r = slice(HD * j, HD * j + HD)
                    ins = run(kcT[r, j, :], ps[r, 0:CP])
                drains(ins, (l, "kcT"))
                for tt in range(TT):
                    act.wait_ge(cmax.sem, cmax.at(l, tt + 1))
                    if tt:
                        wait_filled(act, (l, "cmp_pT", tt - 1))
                    cexp.fire(run(ec[:, :, :], smc[:, :, :], ACT.Exp, scale=HD ** -0.5))
                    if tt == 0:
                        drain_channels("d_g")
                    drains(run(pcT[:, :], wait_filled(act, (l, "cmp_pT", tt))[:, 0:P]), (l, "cmp_pT", tt))
                    if tt == 0:
                        split_weights(JOB_UNITS)
                for n, tag in enumerate(layer_groups(l)):
                    exps(tag)
                    if n < SPLIT_BETWEEN:
                        split_weights(1)
                    if n < len(BETWEEN_GROUPS):
                        drain_channels(BETWEEN_GROUPS[n])
                    evacuate_probs(tag)
                    if n < SPLIT_BETWEEN:
                        split_weights(1)
                if l + 1 < LAYERS:
                    load_cmp(l + 1)
                else:
                    act.dma_start(vec[:, 0, :], row("final_norm_w").broadcast_to([P, D])).then_inc(vec_loaded, 16)
                act.wait_ge(conv_done.sem, conv_done.at(l, 1))
                wait_drained(act, (l, "pool"))
                mix_high.fire(run(xg_hi[:, 4:8, :], mixT[:, 4:8, :]))
                for tt in range(TT):
                    ps = wait_filled(act, (l, "mixT", tt))
                    mix_high.fire(run(xg_hi[:, 0:4, tt * P:(tt + 1) * P], ps[:, :].rearrange("p (a b) -> p a b", a=4)))
                split_weights(2 * ROW_UNITS - UNITS)
            for tt in range(TT):
                for hf in range(2):
                    wait_drained(act, ("hT", tt, hf))
            hT_high.fire(run(xg_hi[:, :, :], hT[:, :, :]))
            split_weights(UNITS)
            act.wait_ge(small2_loaded, SMALL2)
            act.wait_ge(coef_in.sem, 1)
            ps = wait_filled(act, ("dtf",))
            drains(run(dtf[0:16, 0, :], ps[0:16, 0:T], ACT.Identity, scale=C("sgn", rows=16), bias=b16[0:16, 2:3]), ("dtf",))
            wait_drained(act, ("dtf",))
            step(run(dtf[0:16, 1, :], dtf[0:16, 0, :], ACT.Abs))
            dt_exp.fire(run(dtf[0:16, 1, :], dtf[0:16, 1, :], ACT.Exp, scale=-1.0))
            dt_exp.fire(run(b16[0:16, 3:4], b16[0:16, 1:2], ACT.Exp))
            act.wait_ge(dt_w.sem, 1)
            dt_ln.fire(run(dtf[0:16, 4, :], dtf[0:16, 2, :], ACT.Ln))
            for n in range(4):
                split_weights(1)
                ps = wait_filled(act, ("xbc", n))
                for j in range(2):
                    ins = run(xbc[:, 2 * n + j, :], ps[:, j * T:(j + 1) * T], ACT.Identity, bias=bx[:, 2 * n + j:2 * n + j + 1])
                drains(ins, ("xbc", n))
                split_weights(1)
            for n in range(2):
                split_weights(1)
                ps = wait_filled(act, ("q", n))
                for j in range(2):
                    ins = run(qT2[:, 2 * n + j, :], ps[:, j * T:(j + 1) * T], ACT.Identity, bias=bqk[:, 2 * n + j:2 * n + j + 1])
                drains(ins, ("q", n))
                split_weights(1)
            act.wait_ge(k2_zeroed.sem, 1)
            for n in range(2):
                split_weights(1)
                ps = wait_filled(act, ("k", n))
                for j in range(2):
                    for i in range(2):
                        r = slice(HD * i, HD * i + HD)
                        c = 4 + 2 * n + j
                        ins = run(kT2[r, 2 * n + j, i, :], ps[r, j * T:(j + 1) * T], ACT.Identity, bias=bqk[r, c:c + 1])
                drains(ins, ("k", n))
                split_weights(1)
            split_weights(1)
            for n in range(8):
                act.wait_ge(conv2.sem, n + 1)
                act2.fire(run(xc[:, n, :], xc[:, n, :], ACT.Silu))
            split_weights(ROW_UNITS)
            for tt in range(TT):
                wait_drained(act, ("z", tt))
                z_ready.fire(run(z2[:, tt, :], z2[:, tt, :], ACT.Silu))
            for tt in range(TT):
                drains(run(xsN[:, tt, :], wait_filled(act, ("xs", tt))[:, :]), ("xs", tt))
            exps(GROUPS2[0])
            for h in range(SH):
                wait_drained(act, ("Ab", h))
                dec_e.fire(run(seg[:, h % 2, :], seg[:, h % 2, :], ACT.Exp))
                if h % 2:
                    evacuate_probs(GROUPS2[h // 2])
                    if h // 2 + 1 < len(GROUPS2):
                        exps(GROUPS2[h // 2 + 1])
            for n, name in enumerate(("ln1_g_2", "ln1_b_2")):
                act.dma_start(vec[:, n, :], a[name].broadcast_to([P, D])).then_inc(vec_loaded, 16)
            for tt in range(TT):
                act.wait_ge(yz.sem, tt + 1)
                for g in range(2):
                    ysq.fire(run(xc[:, 2 * tt + g, :], merged[:, tt, g * 256:(g + 1) * 256],
                                 ACT.Square, accum_out=rv[:, 2 * tt + g, 0:1]))
            act.wait_ge(yinv.sem, 1)
            yrstd.fire(run(rv[:, 8:12, 0], rv[:, 4:8, 0], ACT.Sqrt))

            def layer_norm(tt, n, x):
                act.wait_ge(ln_mu.sem, n)
                ln_sq.fire(run(hn[:, tt, :], x[:, tt, :], ACT.Square, bias=coef2[:, 0, tt:tt + 1],
                               accum_out=coef2[:, 1, tt:tt + 1]))
                act.wait_ge(ln_inv.sem, n)
                ln_rstd.fire(run(coef2[:, 3, tt:tt + 1], coef2[:, 2, tt:tt + 1], ACT.Sqrt))

            for tt in range(TT):
                layer_norm(tt, tt + 1, x)
            act.wait_ge(h1_ready.sem, TT)
            for n, name in enumerate(("ln2_g_2", "ln2_b_2")):
                act.dma_start(vec[:, n, :], a[name].broadcast_to([P, D])).then_inc(vec_loaded, 16)
            for n in range(2):
                act.wait_ge(r_in.sem, n + 1)
                r_exp.fire(run(rs[:, 1 + 4 * n, :, :], rs[:, 4 * n, :, :], ACT.Exp))

            def split_unit(n, j):
                i, q = j // PER_SLOT, j % PER_SLOT
                s = stream_slot(i)
                if q == 0:
                    uses = len(STREAM) // SLOTS
                    act.wait_ge(slot_here[s], value[s] + 16 * (n * uses + i // SLOTS + 1))
                act.wait_ge(units_free, SPLIT_BEFORE + GROUP_UNITS * n + j + 1)
                unit_high_made.fire(run(unit_hi[:, (SPLIT_BEFORE + j) % UNITS, :], ring[:, s, q * UNIT:(q + 1) * UNIT]))

            def split_gathered(n, k, tile):
                for b in range(2):
                    act.wait_ge(filled[b], fills_of(b, n, k + 1))
                    run(xg_hi[:, 4 * b:4 * b + 4, tile * P:(tile + 1) * P],
                        psum[b][:, :].rearrange("p (a b) -> p a b", a=4)).then_inc(tokens_high, 1)

            def silu_gate(n, e, tile):
                act.wait_ge(units_free, unit_done(n, 0, e))
                b = 5 + 2 * tile
                before = 2 * e - 1 if e else 0
                act.wait_ge(drained[b], reads_of(b, n, before + 2 * tile))
                run(silu_g[tile], psum[b - 1][:, :], ACT.Silu).then_inc(drained[b - 1], 1)

            def split_act(n, e, tile, tiles):
                act.wait_ge(act_turned, GE * n + tiles * e + tile + 1)
                if e:
                    act.wait_ge(units_free, unit_done(n, 2, e - 1))
                act_high.fire(run(act_hi[:, tile], psum[5 + 2 * tile][:, :].rearrange("p (a b) -> p a b", a=FT)))

            def group_units(n, tiles, before_last):
                for j in range(UNITS, GROUP_UNITS + UNITS * (tiles == 1)):
                    if j == GROUP_UNITS + UNITS - 1:
                        take_outputs(n, (2, 3), 0)
                    split_unit(n, j)
                    for tile in range(tiles):
                        if j in silu_after:
                            silu_gate(n, silu_after[j], tile)
                        if j in turned_after:
                            split_act(n, turned_after[j], tile, tiles)
                    if turned_after.get(j) == GE - 1:
                        before_last()

            def take_outputs(n, banks, tile):
                act.wait_ge(units_free, unit_done(n, 2, GE - 1))
                for hf, b in enumerate(banks):
                    run(yS[tile][:, hf * 512:(hf + 1) * 512], psum[b][:, :]).then_inc(drained[b], 1)

            split_gathered(0, 0, 0)
            for j in range(UNITS):
                split_unit(0, j)
            with act.Fori(0, LAST) as n:
                group_units(n, 1, lambda: split_gathered(n + 1, 0, 0))
            split_gathered(LAST, 1, 1)
            group_units(LAST, 2, lambda: None)
            take_outputs(LAST, (2, 3), 0)
            take_outputs(LAST, (0, 1), 1)
            for tt in range(TT):
                layer_norm(tt, TT + tt + 1, acc)

        @block.gpsimd
        def _(pool):
            G = nc.gpsimd

            def step(ins):
                gstep.fire(ins)
                pool.wait_ge(gstep.sem, gstep.n)

            def rope(buf, n, half, cos, sin, signal):
                rows = buf.shape[0]
                t1, t2 = (shaped(rt[0:rows, k, :], n, 2 * half) for k in range(2))
                w = buf[:, :, 0:2 * half]
                G.tensor_tensor(t1, w, repeat(cos, n), ALU.mult)
                step(G.tensor_tensor(t2, w, repeat(sin, n), ALU.mult))
                G.tensor_tensor(w[:, :, 0:half], t1[:, :, 0:half], t2[:, :, half:2 * half], ALU.add)
                signal.fire(G.tensor_tensor(w[:, :, half:2 * half], t1[:, :, half:2 * half], t2[:, :, 0:half], ALU.add))
                pool.wait_ge(signal.sem, signal.n)

            zero_list = (kiT, kaT, ksT, kwT, blk, vcB, kcT, du, b16, pw[:, :, :, :], pe2, kcN, dtf[:, 7:8, 0:1])
            assert len(zero_list) == ZEROED
            for v in zero_list:
                pool.memset(v, 0.0).then_inc(zeroed, 1)
            pool.wait_ge(zeroed, ZEROED)
            pool.memset(b16[:, 3:4], 0.0).then_inc(units_free, UNITS)
            pool.memset(g8[:, 4:8], 1.0).then_inc(g8_ones.sem, 1)
            pool.wait_ge(const_loaded, 16)
            for l in range(LAYERS):
                for tt in range(TT):
                    wait_drained(pool, (l, "idx", tt))
                    rope(shaped(ni[:, tt, 0:384], 12, 32), 12, 4, cos32[:, tt, :], sin32[:, tt, :], roped_i)
                for tt in range(TT):
                    wait_drained(pool, (l, "qkv", tt))
                    rope(shaped(na[:, tt, 0:384], 6, HD), 6, 8, cos64[:, tt, :], sin64[:, tt, :], roped_a)
                for tt in range(TT):
                    wait_drained(pool, (l, "bq", tt))
                    wait_drained(pool, (l, "bkv", tt))
                    rope(shaped(nb[:, tt, 0:512], 8, HD), 8, 8, cos64[:, tt, :], sin64[:, tt, :], roped_b)
                wait_drained(pool, (l, "kcmp"))
                rope(shaped(kcN[0:CP, :], 2, HD), 2, 8, C("cosc", rows=CP), C("sinc", rows=CP), roped_c)
                wait_drained(pool, (l, "d_u"))
                pool.wait_ge(scored.sem, scored.at(l, TT))
                E = T + 16
                step(G.tensor_tensor(d2[:, :, 1:E], du[:, :, 1:E], du[:, :, 0:E - 1], ALU.add))
                step(G.tensor_tensor(d4[:, :, 4:E], d2[:, :, 4:E], d2[:, :, 2:E - 2], ALU.add))
                step(G.tensor_tensor(d2[:, 1, 8:E], d4[:, 1, 8:E], d4[:, 1, 4:E - 4], ALU.add))
                step(G.tensor_tensor(d4[HD:P, 1, 16:E], d2[HD:P, 1, 16:E], d2[HD:P, 1, 8:E - 8], ALU.add))
                dp = mixT[:, 6:8, :]
                G.tensor_tensor(dp[0:HD], d2[0:HD, :, 16:E], icnt[0:HD], ALU.mult)
                step(G.tensor_tensor(dp[HD:P], d4[HD:P, :, 16:E], icnt[HD:P], ALU.mult))
                pooled.fire(G.tensor_tensor(dp, dp, du[:, :, 16:E], ALU.subtract))
                pool.wait_ge(conv_y.sem, conv_y.at(l, 1))
                wait_drained(pool, (l, "c_b"))
                wait_drained(pool, (l, "c_g"))
                step(G.tensor_tensor(cy, cy, cbS, ALU.mult))
                conv_done.fire(G.tensor_tensor(cy, cy, cgS, ALU.mult))
                if l + 1 < LAYERS:
                    kiT_zeroed.fire(G.memset(kiT, 0.0))
                for tt in range(TT):
                    wait_drained(pool, (l, "win", tt, "o"))
                    m = mixN[:, tt, 256:512]
                    step(G.tensor_tensor(m, m, ob[:, tt, 0, :], ALU.add))
                    step(G.tensor_tensor(m, m, ob[:, tt, 1, :], ALU.add))
                    b_done.fire(G.tensor_tensor(m, m, gsil[:, tt, 256:512], ALU.mult))
            pool.wait_ge(h0_ready.sem, TT)
            for n, c in enumerate((Z2, V2)):
                pool.dma_start(brow[:, n * 512:(n + 1) * 512], a["b_in_2"][:, c:c + 512].broadcast_to([P, 512]))\
                    .then_inc(brow_loaded, 16)
            k2_zeroed.fire(G.memset(kT2, 0.0))
            wait_drained(pool, ("tA",))
            for tt in range(TT):
                wait_drained(pool, ("xs", tt))
                ins = G.tensor_tensor(shaped(xdt[:, tt, :], SH, HD), shaped(xsN[:, tt, :], SH, HD),
                                      spread(dA[:, 2 * tt, 0:SH], HD), ALU.mult)
            xdt_ready.fire(ins)
            pool.wait_ge(xdt_ready.sem, 1)
            for tt in range(TT):
                v = shaped(xsN[:, tt, :], SH, HD)
                ins = G.tensor_tensor(v, v, spread(dsk, HD), ALU.mult)
            xdt_ready.fire(ins)
            for g in range(2):
                wait_drained(pool, ("cb", g))
            for h in range(SH):
                pool.wait_ge(dec_e.sem, h + 1)
                if h >= 2:
                    pool.wait_ge(y_used.sem, h - 1)
                decay.fire(G.tensor_tensor(mTh[:, h % 2, :], seg[:, h % 2, :], cbm[:, h // 4, :], ALU.mult))


_INPUTS = ["x", "norm_w", "w_in", "w_out", "conv_w", "pe_cmp", "w_cmp_k", "w_cmp_v", "pool_w", "pool_scale", "final_norm_w",
           "w_in_2", "b_in_2", "conv_w_2", "conv_b_2", "a_log_2", "d_skip_2", "ssd_norm_g_2", "w_out_2", "ln1_g_2",
           "ln1_b_2", "router_group_w_2", "router_group_b_2", "router_expert_w_2", "router_expert_b_2", "w_gate_2",
           "w_up_2", "w_down_2", "ln2_g_2", "ln2_b_2"]


def kernel(**inputs):
    import concourse.bacc as bacc
    from concourse.bass_utils import run_bass_kernel_spmd

    nc = bacc.Bacc("TRN2", target_bir_lowering=False, num_devices=1)
    arrays = {n: np.ascontiguousarray(inputs[n]) for n in _INPUTS}
    arrays["shape_constants"] = shape_constants()
    feeds, aps = {}, {}
    for n, v in arrays.items():
        feeds[f"in_{n}"] = v
        aps[n] = nc.dram_tensor(f"in_{n}", v.shape, mybir.dt.from_np(v.dtype), kind="ExternalInput").ap()
    out = nc.dram_tensor("out", (1, T, D), F32, kind="ExternalOutput").ap()
    build(nc, aps, out)
    r = run_bass_kernel_spmd(nc, [feeds], core_ids=[0])
    return r.results[0]["out"]
```
